# Optimizing a Trainium2 kernel written in Bass

```python
import jax, jax.numpy as jnp
from jax import lax
import numpy as np

D_MODEL = 1024
BATCH = 1
SEQ = 256
DEPTH = 2
DEC_BATCH = 8
DEC_SEQ = 4
PAST_LEN = 2048
PAGE_SIZE = 128

N_META = 16
CONV_WIDTH = 31
D_CONV = D_MODEL
N_HEADS = D_MODEL // 64
QK_NOPE = 64
QK_ROPE = 32
V_HEAD = 64
KV_LORA = 4 * QK_NOPE
Q_LORA = D_MODEL // 2
ROPE_BASE = 10000.0
Q_BLOCK = 128
D_FF = 2816
N_EXPERTS = 8
TOP_K = 2
D_EXPERT = 7 * D_MODEL // 2
N_CONV_LAYERS = (DEPTH + 1) // 2
N_ATTN_LAYERS = DEPTH // 2
N_DENSE_LAYERS = (DEPTH + 1) // 2
N_MOE_LAYERS = DEPTH // 2
ALPHA = (2.0 * DEPTH) ** 0.25
BETA = (8.0 * DEPTH) ** -0.25
SM_SCALE = (QK_NOPE + QK_ROPE) ** -0.5
LN_EPS = 1e-5
RMS_EPS = 1e-6

kernel_name = 'conformer_mla_hybrid_decode_step'

def layer_norm(x, g, b):
    xf = x.astype(jnp.float32)
    mu = jnp.mean(xf, -1, keepdims=True)
    var = jnp.mean(jnp.square(xf - mu), -1, keepdims=True)
    return ((xf - mu) * lax.rsqrt(var + LN_EPS) * g + b).astype(x.dtype)

def rms_norm(x, g):
    xf = x.astype(jnp.float32)
    return (xf * lax.rsqrt(jnp.mean(jnp.square(xf), -1, keepdims=True) + RMS_EPS) * g).astype(x.dtype)

def rope(x, pos):
    half = QK_ROPE // 2
    freqs = ROPE_BASE ** (-jnp.arange(half, dtype=jnp.float32) / half)
    ang = pos[:, None] * freqs[None, :]
    ang = ang.reshape(ang.shape[:1] + (1,) * (x.ndim - 3) + (half,))
    cos, sin = jnp.cos(ang), jnp.sin(ang)
    xf = x.astype(jnp.float32)
    x1, x2 = xf[..., :half], xf[..., half:]
    return jnp.concatenate([x1 * cos - x2 * sin, x2 * cos + x1 * sin], -1).astype(x.dtype)

def swiglu(x, w_gu, w_down, width):
    h = x @ w_gu
    return (jax.nn.silu(h[..., :width]) * h[..., width:]) @ w_down

def moe_swiglu(x, w_router, w_gu, w_down):
    logits = jnp.einsum('btd,de->bte', x, w_router).astype(jnp.float32)
    top_val, top_idx = lax.top_k(logits, TOP_K)
    top_w = jax.nn.softmax(top_val, axis=-1)
    gate = jnp.sum(jax.nn.one_hot(top_idx, N_EXPERTS, dtype=jnp.float32) * top_w[..., None], axis=-2).astype(x.dtype)
    out = jnp.zeros_like(x)
    for e in range(N_EXPERTS):
        out = out + gate[..., e:e + 1] * swiglu(x, w_gu[e], w_down[e], D_EXPERT)
    return out

def conv_mixer(x, past, w_in, b_in, w_dw, b_dw, g_ln, b_ln, w_out):
    h = x @ w_in + b_in
    u = h[..., :D_CONV] * jax.nn.sigmoid(h[..., D_CONV:])
    if past is None:
        buf = jnp.pad(u, ((0, 0), (CONV_WIDTH - 1, 0), (0, 0)))
    else:
        buf = jnp.concatenate([past.astype(u.dtype), u], axis=1)
    conv = lax.conv_general_dilated(buf, w_dw[:, None, :].astype(u.dtype), window_strides=(1,), padding='VALID',
                                    dimension_numbers=('NWC', 'WIO', 'NWC'), feature_group_count=D_CONV) + b_dw
    y = jax.nn.silu(layer_norm(conv, g_ln, b_ln)) @ w_out
    return y, buf[:, -(CONV_WIDTH - 1):, :]

def mla_project(x, pos, w_in, g_q, g_kv, w_uq, w_uk):
    h = x @ w_in
    c_q = rms_norm(h[..., :Q_LORA], g_q)
    c_kv = rms_norm(h[..., Q_LORA:Q_LORA + KV_LORA], g_kv)
    k_rope = rope(h[..., Q_LORA + KV_LORA:], pos)
    q = jnp.einsum('btc,chd->bthd', c_q, w_uq)
    q_rope = rope(q[..., QK_NOPE:], pos)
    q_lat = jnp.einsum('bthd,rhd->bthr', q[..., :QK_NOPE], w_uk)
    return q_lat, q_rope, c_kv, k_rope

def mla_output(o_lat, w_uv, w_out):
    v = jnp.einsum('bthr,rhv->bthv', o_lat, w_uv)
    return jnp.einsum('bthv,hvd->btd', v, w_out)

def prompt_latent_attention(q_lat, q_rope, c_kv, k_rope):
    b, t = q_lat.shape[0], q_lat.shape[1]
    pad = (-t) % Q_BLOCK
    n_blk = (t + pad) // Q_BLOCK
    qb = jnp.pad(q_lat, ((0, 0), (0, pad), (0, 0), (0, 0))).reshape(b, n_blk, Q_BLOCK, N_HEADS, KV_LORA).transpose(1, 0, 2, 3, 4)
    rb = jnp.pad(q_rope, ((0, 0), (0, pad), (0, 0), (0, 0))).reshape(b, n_blk, Q_BLOCK, N_HEADS, QK_ROPE).transpose(1, 0, 2, 3, 4)
    q_pos = jnp.arange(n_blk * Q_BLOCK).reshape(n_blk, Q_BLOCK)
    k_pos = jnp.arange(t)

    def block(args):
        q_b, r_b, p_b = args
        s = (jnp.einsum('bqhr,bkr->bhqk', q_b, c_kv) + jnp.einsum('bqhd,bkd->bhqk', r_b, k_rope)).astype(jnp.float32) * SM_SCALE
        s = jnp.where(k_pos[None, :] <= p_b[:, None], s, -jnp.inf)
        p = jax.nn.softmax(s, axis=-1).astype(c_kv.dtype)
        return jnp.einsum('bhqk,bkr->bqhr', p, c_kv)

    o = lax.map(block, (qb, rb, q_pos))
    return o.transpose(1, 0, 2, 3, 4).reshape(b, n_blk * Q_BLOCK, N_HEADS, KV_LORA)[:, :t]

def sample_latent_attention(q_lat, q_rope, ckv_past, kr_past, ckv_new, kr_new):
    n_new = ckv_new.shape[1]
    s_past = (jnp.einsum('bqhr,bkr->bhqk', q_lat, ckv_past) + jnp.einsum('bqhd,bkd->bhqk', q_rope, kr_past)).astype(jnp.float32) * SM_SCALE
    s_new = (jnp.einsum('bqhr,bkr->bhqk', q_lat, ckv_new) + jnp.einsum('bqhd,bkd->bhqk', q_rope, kr_new)).astype(jnp.float32) * SM_SCALE
    causal = jnp.arange(n_new)[None, :] <= jnp.arange(n_new)[:, None]
    s_new = jnp.where(causal, s_new, -jnp.inf)
    m = jnp.maximum(s_past.max(-1, keepdims=True), s_new.max(-1, keepdims=True))
    p_past = jnp.exp(s_past - m)
    p_new = jnp.exp(s_new - m)
    inv = 1.0 / (p_past.sum(-1, keepdims=True) + p_new.sum(-1, keepdims=True))
    dt = ckv_new.dtype
    return (jnp.einsum('bhqk,bkr->bqhr', (p_past * inv).astype(dt), ckv_past)
            + jnp.einsum('bhqk,bkr->bqhr', (p_new * inv).astype(dt), ckv_new))

def setup_inputs(seed: int = 0) -> dict:
    key = jax.random.key(seed)
    ks = iter(jax.random.split(key, 32))

    def nrm(shape, scale):
        return jax.random.normal(next(ks), shape, jnp.float32) * scale

    n_pages = PAST_LEN // PAGE_SIZE
    n_used = DEC_BATCH * n_pages
    n_pool = n_used + n_used // 4
    d = D_MODEL
    inputs = {}
    inputs['x_prompt'] = nrm((BATCH, SEQ, d), 1.0)
    inputs['x_sample'] = nrm((DEC_BATCH, DEC_SEQ, d), 1.0)
    inputs['state_conv'] = nrm((N_CONV_LAYERS, DEC_BATCH, CONV_WIDTH - 1, D_CONV), 0.5)
    inputs['cache_ckv'] = nrm((N_ATTN_LAYERS, n_pool, PAGE_SIZE, KV_LORA), 1.0)
    inputs['cache_krope'] = nrm((N_ATTN_LAYERS, n_pool, PAGE_SIZE, QK_ROPE), 1.0)
    inputs['page_table'] = jax.random.permutation(next(ks), n_pool)[:n_used].reshape(DEC_BATCH, n_pages).astype(jnp.int32)
    inputs['meta_tokens'] = nrm((N_META, d), 1.0)
    inputs['conv_w_in'] = nrm((N_CONV_LAYERS, d, 2 * D_CONV), d ** -0.5)
    inputs['conv_b_in'] = nrm((N_CONV_LAYERS, 2 * D_CONV), 0.02)
    inputs['conv_w_dw'] = nrm((N_CONV_LAYERS, CONV_WIDTH, D_CONV), CONV_WIDTH ** -0.5)
    inputs['conv_b_dw'] = nrm((N_CONV_LAYERS, D_CONV), 0.02)
    inputs['conv_ln_g'] = 1.0 + nrm((N_CONV_LAYERS, D_CONV), 0.02)
    inputs['conv_ln_b'] = nrm((N_CONV_LAYERS, D_CONV), 0.02)
    inputs['conv_w_out'] = nrm((N_CONV_LAYERS, D_CONV, d), D_CONV ** -0.5 * BETA)
    inputs['mla_w_in'] = nrm((N_ATTN_LAYERS, d, Q_LORA + KV_LORA + QK_ROPE), d ** -0.5)
    inputs['mla_g_q'] = 1.0 + nrm((N_ATTN_LAYERS, Q_LORA), 0.02)
    inputs['mla_g_kv'] = 1.0 + nrm((N_ATTN_LAYERS, KV_LORA), 0.02)
    inputs['mla_w_uq'] = nrm((N_ATTN_LAYERS, Q_LORA, N_HEADS, QK_NOPE + QK_ROPE), Q_LORA ** -0.5)
    inputs['mla_w_uk'] = nrm((N_ATTN_LAYERS, KV_LORA, N_HEADS, QK_NOPE), KV_LORA ** -0.5)
    inputs['mla_w_uv'] = nrm((N_ATTN_LAYERS, KV_LORA, N_HEADS, V_HEAD), KV_LORA ** -0.5)
    inputs['mla_w_out'] = nrm((N_ATTN_LAYERS, N_HEADS, V_HEAD, d), (N_HEADS * V_HEAD) ** -0.5 * BETA)
    inputs['ffn_w_gu'] = nrm((N_DENSE_LAYERS, d, 2 * D_FF), d ** -0.5)
    inputs['ffn_w_down'] = nrm((N_DENSE_LAYERS, D_FF, d), D_FF ** -0.5 * BETA)
    inputs['moe_w_router'] = nrm((N_MOE_LAYERS, d, N_EXPERTS), d ** -0.5)
    inputs['moe_w_gu'] = nrm((N_MOE_LAYERS, N_EXPERTS, d, 2 * D_EXPERT), d ** -0.5)
    inputs['moe_w_down'] = nrm((N_MOE_LAYERS, N_EXPERTS, D_EXPERT, d), D_EXPERT ** -0.5 * BETA)
    inputs['ln_g'] = 1.0 + nrm((DEPTH, 2, d), 0.02)
    inputs['ln_b'] = nrm((DEPTH, 2, d), 0.02)
    return inputs

def reference(x_prompt, x_sample, state_conv, cache_ckv, cache_krope, page_table, meta_tokens,
              conv_w_in, conv_b_in, conv_w_dw, conv_b_dw, conv_ln_g, conv_ln_b, conv_w_out,
              mla_w_in, mla_g_q, mla_g_kv, mla_w_uq, mla_w_uk, mla_w_uv, mla_w_out,
              ffn_w_gu, ffn_w_down, moe_w_router, moe_w_gu, moe_w_down, ln_g, ln_b):
    meta = jnp.broadcast_to(meta_tokens[None].astype(x_prompt.dtype), (x_prompt.shape[0], N_META, D_MODEL))
    xp = jnp.concatenate([meta, x_prompt], axis=1)
    xs = x_sample
    n_dec = xs.shape[0]
    pos_p = jnp.arange(xp.shape[1], dtype=jnp.float32)
    pos_s = PAST_LEN + jnp.arange(xs.shape[1], dtype=jnp.float32)
    conv_p, conv_s, ckv_p, kr_p, ckv_s, kr_s = [], [], [], [], [], []
    for i in range(DEPTH):
        j = i // 2
        if i % 2 == 0:
            cw = (conv_w_in[j], conv_b_in[j], conv_w_dw[j], conv_b_dw[j], conv_ln_g[j], conv_ln_b[j], conv_w_out[j])
            mp, st_p = conv_mixer(xp, None, *cw)
            ms, st_s = conv_mixer(xs, state_conv[j], *cw)
            conv_p.append(st_p)
            conv_s.append(st_s)
        else:
            pw = (mla_w_in[j], mla_g_q[j], mla_g_kv[j], mla_w_uq[j], mla_w_uk[j])
            q_lat, q_rope, c_kv, k_rope = mla_project(xp, pos_p, *pw)
            mp = mla_output(prompt_latent_attention(q_lat, q_rope, c_kv, k_rope), mla_w_uv[j], mla_w_out[j])
            ckv_p.append(c_kv)
            kr_p.append(k_rope)
            q_lat, q_rope, c_kv, k_rope = mla_project(xs, pos_s, *pw)
            ckv_past = cache_ckv[j, page_table].reshape(n_dec, -1, KV_LORA)
            kr_past = cache_krope[j, page_table].reshape(n_dec, -1, QK_ROPE)
            ms = mla_output(sample_latent_attention(q_lat, q_rope, ckv_past, kr_past, c_kv, k_rope), mla_w_uv[j], mla_w_out[j])
            ckv_s.append(c_kv)
            kr_s.append(k_rope)
        xp = layer_norm(ALPHA * xp + mp, ln_g[i, 0], ln_b[i, 0])
        xs = layer_norm(ALPHA * xs + ms, ln_g[i, 0], ln_b[i, 0])
        if i % 2 == 0:
            fp = swiglu(xp, ffn_w_gu[j], ffn_w_down[j], D_FF)
            fs = swiglu(xs, ffn_w_gu[j], ffn_w_down[j], D_FF)
        else:
            fp = moe_swiglu(xp, moe_w_router[j], moe_w_gu[j], moe_w_down[j])
            fs = moe_swiglu(xs, moe_w_router[j], moe_w_gu[j], moe_w_down[j])
        xp = layer_norm(ALPHA * xp + fp, ln_g[i, 1], ln_b[i, 1])
        xs = layer_norm(ALPHA * xs + fs, ln_g[i, 1], ln_b[i, 1])
    return (xp[:, N_META:], xs, jnp.stack(conv_p), jnp.stack(conv_s), jnp.stack(ckv_p), jnp.stack(kr_p), jnp.stack(ckv_s), jnp.stack(kr_s))


_drawn_inputs = setup_inputs


def setup_inputs(seed=0):
    import zlib

    import numpy as np

    out = dict(_drawn_inputs(seed))
    spreads = {}
    factors = {'cache_krope': 2.913,
     'conv_b_in': 2.705,
     'conv_b_dw': 3.724,
     'conv_ln_g': 4.813,
     'conv_ln_b': 5.449,
     'mla_g_q': 8.0,
     'mla_g_kv': 2.726}
    for name, (base, spread) in spreads.items():
        noise = np.random.default_rng([zlib.crc32(name.encode()), seed]).standard_normal(out[name].shape)
        drawn = base * np.exp(spread * noise) if base else spread * noise
        out[name] = __import__('jax').numpy.asarray(drawn.astype(out[name].dtype))
    for name, factor in factors.items():
        out[name] = (out[name] * factor).astype(out[name].dtype)
    return out
```

```python
from contextlib import ExitStack

import numpy as np
import concourse.bass as bass
from concourse import mybir

F32 = mybir.dt.float32
F32R = mybir.dt.float32r
I32 = mybir.dt.int32
ALU = mybir.AluOpType
ACT = mybir.ActivationFunctionType
AX = mybir.AxisListType.X

P = 128
D = 1024
DC = D // P
SEQ, N_META, DEC_B, DEC_T = 256, 16, 8, 4
T_P = SEQ + N_META
T_S = DEC_B * DEC_T
T = T_P + T_S
PAST, PAGE = 2048, 128
PAGES = PAST // PAGE
TAPS = 31
HIST = TAPS - 1
HEADS, NOPE, ROPE, VH = 16, 64, 32, 64
LORA, QLORA = 256, 512
RC = LORA // P
FF = 2816
FC = FF // P
NEXP, DEXP = 8, 3584
DEPTH = 2
ALPHA = (2.0 * DEPTH) ** 0.25
SM_SCALE = (NOPE + ROPE) ** -0.5
LN_EPS, RMS_EPS = 1e-5, 1e-6
NEG = -1e30
TB = [(0, P), (P, P), (2 * P, T - 2 * P)]
TAIL0 = 2 * P
TAIL = T - TAIL0
QT = T_P - TAIL0
PE_TAPS = 15
DIAGS = 20
SLOTS = P
MAX_JOBS = 12
STEPS = DEXP // 512
JOB_UNITS = 6 * STEPS

RAW, SPLIT = 6, 3
UNIT = 2048
AHEAD = 2

U_CIN, U_COUT = 0, 8
U_GU = U_COUT + 4
U_DOWN = U_GU + FC
U_MIN = U_DOWN + 12
U_UQ = U_MIN + 4
U_MOUT = U_UQ + 4
U_MOE = U_MOUT + 4
G_CIN, G_COUT, G_GU = 0, 8, 12
G_DOWN = G_GU + FC
G_MIN = G_DOWN + 4
G_MOUT = G_MIN + 4
assert U_MOE % 6 == 4 and MAX_JOBS * SLOTS > 2 * T


def rope_tables():
    half = ROPE // 2
    freqs = (np.float32(10000.0) ** (-np.arange(half, dtype=np.float32) / np.float32(half))).astype(np.float32)
    pos = np.concatenate([np.arange(T_P), np.tile(PAST + np.arange(DEC_T), DEC_B)]).astype(np.float32)
    ang = (pos[None, :] * freqs[:, None]).astype(np.float32)
    cos, sin = np.cos(ang), np.sin(ang)
    return (np.tile(np.concatenate([cos, cos], 0), (4, 1)).astype(np.float32),
            np.tile(np.concatenate([-sin, sin], 0), (4, 1)).astype(np.float32))


def build(nc, x_prompt, x_sample, state_conv, cache_ckv, cache_krope, page_table, meta_tokens,
          conv_w_in, conv_b_in, conv_w_dw, conv_b_dw, conv_ln_g, conv_ln_b, conv_w_out,
          mla_w_in, mla_g_q, mla_g_kv, mla_w_uq, mla_w_uk, mla_w_uv, mla_w_out,
          ffn_w_gu, ffn_w_down, moe_w_router, moe_w_gu, moe_w_down, ln_g, ln_b, cos_t, sin_t,
          y_prompt, y_sample, new_conv_p, new_conv_s, new_ckv_p, new_kr_p, new_ckv_s, new_kr_s):
    ctx = ExitStack()
    ctx.enter_context(ctx_ok := nc.allow_non_contiguous_dma(reason="small vectors are laid out feature-major"))
    base = -(-nc.sbuf_base // 64) * 64
    limit = nc.sbuf_usable_end

    def place(name, off, shape, dt=F32):
        size = int(np.prod(shape[1:])) * 4
        assert base + off + size <= limit, (name, off, size)
        return nc.alloc_sbuf_tensor_at(name, shape, dt, offset=base + off)

    def sem(name):
        return ctx.enter_context(nc.semaphore(name))

    class Region:
        def __init__(self, start, end):
            self.at, self.end = start, end

        def __call__(self, name, shape, dt=F32):
            t = place(name, self.at, shape, dt)
            self.at += int(np.prod(shape[1:])) * 4
            self.at = -(-self.at // 32) * 32
            assert self.at <= self.end, (name, self.at, self.end)
            return t

    KB = 1024
    ACTV = T * DC * 4
    raw = place("raw", 0, [P, RAW, UNIT])
    w_hi = place("w_hi", 48 * KB, [P, SPLIT, UNIT], F32R)
    w_lo = place("w_lo", 72 * KB, [P, SPLIT, UNIT], F32R)
    A0 = 96 * KB
    xres = place("xres", A0, [P, DC, T])
    x_hi = place("x_hi", A0 + ACTV, [P, DC, T], F32R)
    x_lo = place("x_lo", A0 + 2 * ACTV, [P, DC, T], F32R)
    work = place("work", A0 + 3 * ACTV, [P, DC, T])
    sq = place("sq", A0 + 4 * ACTV, [P, DC, T])
    Z0 = A0 + 5 * ACTV
    LIM = limit - base
    cst = Region(Z0, LIM)
    ident = cst("ident", [P, P])
    ones = cst("ones", [P, P])
    before = cst("before", [P, P])
    rstd = cst("rstd", [P, T])
    lng = cst("lng", [P, 4, DC])
    lnb = cst("lnb", [P, 4, DC])
    b_in = cst("b_in", [P, 2 * DC])
    w_dw = cst("w_dw", [P, TAPS, DC])
    b_dw = cst("b_dw", [P, DC])
    cg = cst("cg", [P, DC])
    cb = cst("cb", [P, DC])
    g_q = cst("g_q", [P, QLORA // P])
    g_kv = cst("g_kv", [P, RC])
    eps = cst("eps", [P, 2])
    row_i = cst("row_i", [P, 1], I32)
    pages = cst("pages", [1, DEC_B * PAGES], I32)
    Z = cst.at
    cv = Region(Z, LIM)
    gate = cv("gate", [P, 2, T])
    htmp = cv("htmp", [P, 2, T])
    gu_end = cv.at
    u_p = cv("u_p", [P, DC, HIST + T_P])
    u_s = cv("u_s", [P, DC, DEC_B, HIST + DEC_T])
    xtok = cv("xtok", [P, 3, D])
    hist = cv("hist", [P, 2, D])
    u_new = cv("u_new", [P, DC, T_S])
    edge = xtok
    diag = cv("diag", [P, DIAGS, P])
    ff = Region(gu_end, LIM)
    h_hi = ff("h_hi", [P, FC, T], F32R)
    h_lo = ff("h_lo", [P, FC, T], F32R)
    at_ = Region(Z, LIM)
    cosT = at_("cosT", [P, T])
    sinT = at_("sinT", [P, T])
    causal = at_("causal", [P, 3 * P])
    causal_t = at_("causal_t", [P, QT])
    causal_s = at_("causal_s", [P, HEADS, DEC_T])
    ckvT = at_("ckvT", [P, RC, T])
    ckvN = at_("ckvN", [P, 3, LORA])
    krT = at_("krT", [P, T])
    krN = at_("krN", [P, 3, ROPE])
    qnT = at_("qnT", [P, HEADS // 2, T])
    qrT = at_("qrT", [P, HEADS // 4, T])
    wukT_at = at_.at
    wukT = at_("wukT", [P, HEADS // 2, LORA])
    cq_at = at_.at
    wuv = at_("wuv", [P, RC, HEADS * VH])
    qlt = at_("qlt", [P, RC, HEADS, TAIL])
    qrt = at_("qrt", [P, HEADS, TAIL])
    kt = at_("kt", [P, 2, 4, LORA])
    tailq = [kt[:, 1, 2 * i:2 * i + 2].rearrange("p a (b n) -> p (a b) n", b=2)[:, 0:RC + 1] for i in range(2)]
    cq = Region(cq_at, LIM)
    cq_f = cq("cq_f", [P, 4, T])
    cq_hi = cq("cq_hi", [P, 4, T], F32R)
    cq_lo = cq("cq_lo", [P, 4, T], F32R)
    rms_kv = place("rms_kv", A0 + 3 * ACTV + 8 * KB, [P, T])[:]
    wuk = place("wuk", A0 + 4 * ACTV, [P, RC, HEADS * NOPE])
    pa = Region(A0 + 3 * ACTV, Z0)
    ql = pa("ql", [P, 2, RC, T])
    sc = pa("sc", [P, 2, 3 * P])
    pT = pa("pT", [P, 2, 3 * P])
    oT = pa("oT", [P, 2, RC, 2 * P])
    pst = pa("pst", [P, 2, 8])
    kvn = [place("kvn0", A0 + ACTV, [P, PAGES, LORA]), place("kvn1", A0 + 3 * ACTV, [P, PAGES, LORA])]
    krn = [place("krn0", A0 + ACTV + PAGES * LORA * 4, [P, PAGES, ROPE]),
           place("krn1", A0 + 3 * ACTV + PAGES * LORA * 4, [P, PAGES, ROPE])]
    sa = Region(wukT_at, cq_at)
    ss = sa("ss", [P, PAGES, HEADS * DEC_T])
    kr4 = sa("kr4", [P, 2, P])
    qs = sa("qs", [P, RC, HEADS * DEC_T])
    qsr = sa("qsr", [P, 4, HEADS * DEC_T])
    kn = sa("kn", [P, RC + 1, DEC_T])
    knN = rstd[:, 0:LORA]
    sn = sa("sn", [P, HEADS * DEC_T])
    mx = sa("mx", [P, 2 * HEADS * DEC_T])
    dg = sa("dg", [P, HEADS * DEC_T])
    m1 = sa("m1", [P, 1])
    mo = Region(Z, LIM)
    xt = mo("xt", [P, 3, D])
    g_next = mo("g_next", [P, DC, SLOTS])
    acc = mo("acc", [P, 3, D])
    pick = mo("pick", [P, 3, P])
    pickT = mo("pickT", [P, 3, P], F32R)
    iota = mo("iota", [P, P])
    w_rt = mo("w_rt", [P, DC, NEXP])
    lt8 = mo("lt8", [P, NEXP, NEXP])
    cmp_ = mo("cmp_", [P, MAX_JOBS, NEXP])
    cmp2 = mo("cmp2", [P, NEXP, NEXP])
    lg = mo("lg", [P, 3, NEXP])
    rank = mo("rank", [P, 3, NEXP])
    oneA = mo("oneA", [P, 3, NEXP])
    oneB = mo("oneB", [P, 3, NEXP])
    valid = mo("valid", [P, 3, NEXP])
    selt = mo("selt", [P, 3, NEXP])
    keyt = mo("keyt", [P, 3, NEXP])
    jobs = mo("jobs", [P, 2, NEXP])
    starts = mo("starts", [P, NEXP])
    tk = mo("tk", [P, 12, 3])
    jobf = mo("jobf", [P, MAX_JOBS + 1])
    jobi = mo("jobi", [P, MAX_JOBS + 1], I32)
    me = Region(A0 + ACTV, Z0)
    g_hi = me("g_hi", [P, DC, SLOTS], F32R)
    g_lo = me("g_lo", [P, DC, SLOTS], F32R)
    sg = me("sg", [P, 2, 512])
    hh = me("hh", [P, 2, 512])
    hT_hi = me("hT_hi", [P, 4, SLOTS], F32R)
    hT_lo = me("hT_lo", [P, 4, SLOTS], F32R)
    y_hi = me("y_hi", [P, D], F32R)
    y_lo = me("y_lo", [P, D], F32R)
    gbc = me("gbc", [P, D])
    bbc = me("bbc", [P, D])
    sqt = place("sqt", A0, [P, D])
    stat = place("stat", A0 + 4 * KB, [P, 3, 4])

    ps = ctx.enter_context(nc.psum_tensor("ps", [P, 8, 512], F32))

    const_ld = sem("const_ld")
    x_ld = sem("x_ld")
    hist_ld = sem("hist_ld")
    consts_made = sem("consts_made")
    raw_ready = [sem(f"raw_ready{i}") for i in range(RAW)]
    hi_done = sem("hi_done")
    lo_done = sem("lo_done")
    unit_used = sem("unit_used")
    group_free = sem("group_free")
    gate_ready = sem("gate_ready")
    xpose = sem("xpose")
    xpose_free = sem("xpose_free")
    xin_raw = sem("xin_raw")
    act_own = sem("act_own")
    dve = sem("dve")
    ln_in = sem("ln_in")
    ln_mean = sem("ln_mean")
    ln_cent = sem("ln_cent")
    ln_sq = sem("ln_sq")
    ln_var = sem("ln_var")
    ln_std = sem("ln_std")
    rms_rt = sem("rms_rt")
    ln_scaled = sem("ln_scaled")
    ln_hi = sem("ln_hi")
    x_split = sem("x_split")
    h_split = sem("h_split")
    uq_free = sem("uq_free")
    att_ld = sem("att_ld")
    att_w = sem("att_w")
    attc = sem("attc")
    mask_ready = sem("mask_ready")
    edge_ready = sem("edge_ready")
    diag_ready = sem("diag_ready")
    diag_used = sem("diag_used")
    edge_copied = sem("edge_copied")
    edge_out = sem("edge_out")
    kvN_copied = sem("kvN_copied")
    rt_w = sem("rt_w")
    tail_ready = sem("tail_ready")
    qrt_ld = sem("qrt_ld")
    stores = sem("stores")
    mla_pe = sem("mla_pe")
    mla_dve = sem("mla_dve")
    mla_act = sem("mla_act")
    p_ql, p_qc, p_sc, p_sm, p_ex, p_nm, p_tr, p_pt, p_pv, p_ot, p_v, p_vc = [
        sem("pa_" + n) for n in ("qlat", "qcopied", "scores", "shifted", "exp", "normed", "transposed", "ptcopied",
                                 "pv", "otcopied", "v", "vcopied")]
    kv_ready = [sem("kv_ready0"), sem("kv_ready1")]
    s_q, s_t, s_kt, s_sc, s_new, s_mt, s_dg, s_mb, s_sh, s_ex, s_sum, s_st, s_pv, s_free, s_kn, s_knN = [
        sem("sa_" + n) for n in ("q_copied", "k_transposed", "kt_copied", "scores", "new", "max_t", "diag", "max_bc",
                                 "shifted", "exp", "summed", "sum_bc", "pv", "seq_done", "new_t", "newN")]
    v_ready = sem("v_ready")
    rt_pe = sem("rt_pe")
    rt_dve = sem("rt_dve")
    rt_act = sem("rt_act")
    rt_const = sem("rt_const")
    table_ready = sem("table_ready")
    m_zero, m_gh, m_pick, m_pickT, m_pickTc, m_g, m_gc, m_gl, m_sg, m_h, m_hT, m_hTc, m_hTl, m_yhi, m_ylo, m_sct, m_acc, m_own = [
        sem("mo_" + n) for n in ("zeroed", "next_hi", "picked", "pick_t", "pick_copied", "gathered", "g_hi", "g_lo", "silu", "h", "h_t",
                                 "hT_hi", "hT_lo", "y_hi", "y_lo", "scattered", "added", "own")]
    fin_v = sem("fin_v")
    fin_a = sem("fin_a")
    fin_sq = sem("fin_sq")
    fin_ld = sem("fin_ld")

    def km(w, c0, n):
        return w.rearrange("(c p) n -> p c n", p=P)[:, :, c0:c0 + n]

    w_in, w_o = conv_w_in[0], conv_w_out[0]
    f_gu, f_dn = ffn_w_gu[0], ffn_w_down[0]
    m_in = mla_w_in[0]
    m_uq = mla_w_uq[0].rearrange("(c p) h d -> p c (h d)", p=P)
    m_out = mla_w_out[0].rearrange("h v n -> (h v) n")
    e_gu = moe_w_gu[0].rearrange("e (c p) n -> e p c n", p=P)
    e_dn = moe_w_down[0].rearrange("e (c p) n -> e p c n", p=P)

    def slot(u, n):
        return raw[:, u % RAW, 0:n]

    def pair_unit(u, w, m, second):
        v = slot(u, UNIT).rearrange("p (c a n) -> p c a n", c=8, a=2)
        return [(v[:, :, 0, :], km(w, m, P)), (v[:, :, 1, :], km(w, second + m, P))]

    def block_unit(u, w, kc0, nk, c0, n=256):
        v = slot(u, nk * n).rearrange("p (c n) -> p c n", c=nk)
        src = km(w, c0, n)[:, kc0:kc0 + nk, :]
        return [(v[:, 0:nk // 2], src[:, 0:nk // 2]), (v[:, nk // 2:nk], src[:, nk // 2:nk])]

    SIZE = {}
    DOWN_KC = [(0, 8), (8, 8), (16, FC - 16)]

    def unit_loads(u):
        if u < U_COUT:
            return pair_unit(u, w_in, P * u, D)
        if u < U_GU:
            return block_unit(u, w_o, 0, 8, 256 * (u - U_COUT))
        if u < U_DOWN:
            return pair_unit(u, f_gu, P * (u - U_GU), FF)
        if u < U_MIN:
            i, k = divmod(u - U_DOWN, 3)
            SIZE[u] = DOWN_KC[k][1] * 256
            return block_unit(u, f_dn, *DOWN_KC[k], 256 * i)
        if u < U_UQ:
            i = u - U_MIN
            if i == 3:
                SIZE[u] = 8 * ROPE
                return block_unit(u, m_in, 0, 8, 768, ROPE)
            return block_unit(u, m_in, 0, 8, 256 * i)
        if u < U_MOUT:
            i = u - U_UQ
            v = slot(u, 4 * 384).rearrange("p (c n) -> p c n", c=4)
            s = m_uq[:, :, 384 * i:384 * (i + 1)]
            return [(v[:, 0:2], s[:, 0:2]), (v[:, 2:4], s[:, 2:4])]
        return block_unit(u, m_out, 0, 8, 256 * (u - U_MOUT))

    for u in range(U_MOE):
        unit_loads(u)

    def raw_target(u):
        return 32 * (u // RAW + 1)

    def moe_slot_base(s):
        return 32 * len([u for u in range(U_MOE) if u % RAW == s])

    def moe_raw_target(k, j):
        u = U_MOE + k
        first = (u % RAW - U_MOE) % RAW
        return moe_slot_base(u % RAW) + 16 * ((k - first) // RAW + 1) + j * (16 * JOB_UNITS // RAW)

    TURN_STEP, GATHER_STEPS = 2, (4, 5)

    def first_unit(s):
        return 0 if s == 0 else 4 + 6 * (s - 1)

    ROPE_U = U_MIN + 3

    def split_copies(u, out, src):
        if u == ROPE_U:
            o = out[:, 0:UNIT].rearrange("p (c a r b n) -> p c a r b n", c=8, a=2, r=4, b=2)
            s = src[:, 0:8 * ROPE].rearrange("p (c b n) -> p c b n", c=8, b=2)
            return ([(o[:, :, 0, r].rearrange("p c b n -> p c (b n)"), s.rearrange("p c b n -> p c (b n)"))
                     for r in range(4)] + [(o[:, :, 1, r, b], s[:, :, 1 - b]) for r in range(4) for b in range(2)])
        if U_UQ <= u < U_MOUT:
            o = out[:, 0:UNIT].rearrange("p (c n) -> p c n", c=4)
            s = src[:, 0:4 * 384].rearrange("p (c h d) -> p c h d", c=4, h=4)
            res = []
            for c in range(4):
                res.append((o[:, c, 0:256].rearrange("p (h d) -> p h d", h=4), s[:, c, :, 0:NOPE]))
                res.append((o[:, c, 256:384].rearrange("p (h d) -> p h d", h=4), s[:, c, :, NOPE:NOPE + ROPE]))
                sw = o[:, c, 384:512].rearrange("p (h b d) -> p h b d", h=4, b=2)
                for b in range(2):
                    res.append((sw[:, :, b, :], s[:, c, :, NOPE + 16 * (1 - b):NOPE + 16 * (2 - b)]))
            return res
        n = SIZE.get(u, UNIT)
        return [(out[:, 0:n], src[:, 0:n])]

    block = ctx.enter_context(nc.Block())

    @block.sync
    def _(sp):
        xt = [(xtok[0:N_META, 0], meta_tokens), (xtok[N_META:P, 0], x_prompt[0, 0:P - N_META]),
              (xtok[:, 1], x_prompt[0, P - N_META:2 * P - N_META]),
              (xtok[0:QT, 2], x_prompt[0, 2 * P - N_META:SEQ]),
              (xtok[QT:TAIL, 2], x_sample.rearrange("b t d -> (b t) d"))]
        for o, i in xt:
            sp.dma_start(o, i).then_inc(x_ld, 16)
        half = HIST * 4
        for b in range(2):
            sp.dma_start(hist[0:half, b], state_conv[0, 4 * b:4 * b + 4].rearrange("s t d -> (s t) d")).then_inc(hist_ld, 16)

        def load(u):
            if u >= RAW:
                sp.wait_ge(lo_done, u - RAW + 1)
            for o, i in unit_loads(u):
                sp.dma_start(o, i).then_inc(raw_ready[u % RAW], 16)

        for u in range(U_GU):
            load(u)
        gu_v = f_gu.rearrange("(c p) (a j n) -> p c a j n", p=P, a=2, n=P)
        with sp.Fori(0, 3) as it:
            for r in range(6):
                u = U_GU + r
                sp.wait_ge(lo_done, it * 6 + (u - RAW + 1))
                v = slot(u, UNIT).rearrange("p (c a n) -> p c a n", c=8, a=2)
                for a in range(2):
                    sp.dma_start(v[:, :, a, :], gu_v[:, :, a, bass.ds(it * 6 + r, 1), :].rearrange("p c j n -> p c (j n)")
                                 ).then_inc(raw_ready[u % RAW], 16)
        for u in range(U_GU + 18, U_MOE):
            load(u)

        def job(e_gate, e_down, j):
            k = 0
            for s in range(STEPS + 1):
                todo = []
                if s < STEPS:
                    todo += [(e_gate, 0, s), (e_gate, 1, s), (e_gate, 2, s), (e_gate, 3, s)]
                if s >= 1:
                    todo += [(e_down, 0, s - 1), (e_down, 1, s - 1)]
                for src, part, st in todo:
                    u = U_MOE + k
                    sp.wait_ge(lo_done, j * JOB_UNITS + (u - RAW + 1))
                    sp.dma_start(slot(u, UNIT).rearrange("p (c n) -> p c n", c=4 if src is e_gate else 2),
                                 src(part, st)).then_inc(raw_ready[u % RAW], 16)
                    k += 1
            assert k == JOB_UNITS

        def gate_src(e):
            def src(part, st):
                c0 = 512 * st + (DEXP if part >= 2 else 0)
                v = e_gu[e] if isinstance(e, int) else e_gu[bass.ds(e, 1)].rearrange("e p c n -> p (e c) n")
                return v[:, 4 * (part % 2):4 * (part % 2) + 4, c0:c0 + 512]
            return src

        def down_src(e):
            def src(part, st):
                v = e_dn[e] if isinstance(e, int) else e_dn[bass.ds(e, 1)].rearrange("e p c n -> p (e c) n")
                return v[:, 4 * st + 2 * part:4 * st + 2 * part + 2, :]
            return src

        job(gate_src(0), down_src(0), 0)
        sp.wait_ge(table_ready, 1)
        n_jobs = sp.value_load(jobi[0:1, MAX_JOBS:MAX_JOBS + 1], min_val=NEXP, max_val=MAX_JOBS)
        with sp.Fori(1, n_jobs) as j:
            e = sp.value_load(jobi[0:1, bass.ds(j, 1)], min_val=0, max_val=NEXP - 1)
            job(gate_src(e), down_src(e), j)

    @block.gpsimd
    def _(pool):
        nc.gpsimd.memset(ident[:], 1.0).then_inc(consts_made, 1)
        nc.gpsimd.memset(ones[:], 1.0).then_inc(consts_made, 1)
        nc.gpsimd.memset(before[:], 1.0).then_inc(consts_made, 1)
        nc.gpsimd.memset(u_p[:, :, 0:HIST], 0.0).then_inc(consts_made, 1)
        nc.gpsimd.memset(eps[:, 0:1], LN_EPS).then_inc(consts_made, 1)
        nc.gpsimd.memset(eps[:, 1:2], RMS_EPS).then_inc(consts_made, 1)
        pool.wait_ge(consts_made, 6)
        nc.gpsimd.affine_select(out=ident[:], in_=ident[:], compare_op=ALU.is_equal, fill=0.0, base=0,
                                pattern=[[-1, P]], channel_multiplier=1).then_inc(consts_made, 1)
        nc.gpsimd.affine_select(out=before[:], in_=before[:], compare_op=ALU.is_gt, fill=0.0, base=0,
                                pattern=[[1, P]], channel_multiplier=-1).then_inc(consts_made, 1)
        pool.wait_ge(consts_made, 8)
        pool.wait_ge(const_ld, CONST_LOADS * 16)
        for q in range(DC * PE_TAPS):
            m, t = divmod(q, PE_TAPS)
            if q >= DIAGS:
                pool.wait_ge(diag_used, q - DIAGS + 1)
            nc.gpsimd.tensor_scalar(diag[:, q % DIAGS], ident[:], w_dw[:, t, m:m + 1], 1.0, ALU.mult, ALU.mult
                                    ).then_inc(diag_ready, 1)
        pool.wait_ge(unit_used, U_MIN)
        nc.gpsimd.memset(causal[:], 0.0).then_inc(attc, 1)
        nc.gpsimd.memset(causal_t[:], 0.0).then_inc(attc, 1)
        nc.gpsimd.memset(causal_s[:], 0.0).then_inc(attc, 1)
        pool.wait_ge(attc, 3)
        for b in (0, 2):
            c = causal[:, P * b:P * b + P]
            nc.gpsimd.affine_select(out=c, in_=c, compare_op=ALU.is_ge, fill=NEG, base=0,
                                    pattern=[[-1, P]], channel_multiplier=1).then_inc(attc, 1)
        nc.gpsimd.iota(row_i[:], pattern=[[0, 1]], base=0, channel_multiplier=1).then_inc(attc, 1)
        nc.gpsimd.iota(kt[:, 0, 1, 0:QT], pattern=[[1, QT]], base=0, channel_multiplier=0,
                       allow_small_or_imprecise_dtypes=True).then_inc(attc, 1)
        nc.gpsimd.affine_select(out=causal_s[:], in_=causal_s[:], compare_op=ALU.is_ge, fill=NEG, base=0,
                                pattern=[[0, HEADS], [1, DEC_T]], channel_multiplier=-1).then_inc(attc, 1)

        def fetch(s, b):
            for p in range(PAGES):
                pg = pool.value_load(pages[0:1, bass.ds(s * PAGES + p, 1)] if not isinstance(s, int)
                                     else pages[0:1, s * PAGES + p:s * PAGES + p + 1],
                                     min_val=0, max_val=cache_ckv.shape[1] - 1)
                pool.dma_start(kvn[b][:, p, :], cache_ckv[0, bass.ds(pg, 1)].rearrange("a k r -> k (a r)")
                               ).then_inc(kv_ready[b], 16)
                pool.dma_start(krn[b][:, p, :], cache_krope[0, bass.ds(pg, 1)].rearrange("a k r -> k (a r)")
                               ).then_inc(kv_ready[b], 16)

        pool.wait_ge(const_ld, CONST_LOADS * 16)
        pool.wait_ge(unit_used, U_MOUT)
        fetch(0, 0)
        pool.wait_ge(p_vc, HEADS + 2)
        fetch(1, 1)
        with pool.Fori(1, DEC_B // 2) as it:
            for b in range(2):
                pool.wait_ge(s_free, it * 2 + (b - 1))
                fetch(it * 2 + b, b)

        pool.wait_ge(ln_scaled, 4)
        nc.gpsimd.iota(iota[:], pattern=[[1, P]], base=0, channel_multiplier=0,
                       allow_small_or_imprecise_dtypes=True).then_inc(rt_const, 1)
        nc.gpsimd.memset(lt8[:], 1.0).then_inc(rt_const, 1)
        nc.gpsimd.memset(valid[:], 0.0).then_inc(rt_const, 1)
        nc.gpsimd.memset(lg[:], 0.0).then_inc(rt_const, 1)
        nc.gpsimd.iota(jobf[:], pattern=[[1, MAX_JOBS + 1]], base=0, channel_multiplier=0,
                       allow_small_or_imprecise_dtypes=True).then_inc(rt_const, 1)
        pool.wait_ge(rt_const, 5)
        nc.gpsimd.affine_select(out=lt8[:], in_=lt8[:], compare_op=ALU.is_gt, fill=0.0, base=0,
                                pattern=[[1, NEXP], [-1, NEXP]], channel_multiplier=0).then_inc(rt_const, 1)
        nc.gpsimd.memset(valid[:, 0:2], 1.0).then_inc(rt_const, 1)
        nc.gpsimd.memset(valid[0:TAIL, 2], 1.0).then_inc(rt_const, 1)
        pool.dma_start(w_rt[:], moe_w_router[0].rearrange("(c p) e -> p c e", p=P)).then_inc(rt_w, 16)

    @block.scalar
    def _(act):
        own = [0]

        def chain(ins):
            own[0] += 1
            ins.then_inc(act_own, 1)
            act.wait_ge(act_own, own[0])

        small = [(ln_g.rearrange("a b (c p) -> p (a b) c", p=P), lng), (ln_b.rearrange("a b (c p) -> p (a b) c", p=P), lnb)]
        for src, dst in small:
            for a in range(4):
                act.dma_start(dst[:, a], src[:, a]).then_inc(const_ld, 16)
        act.dma_start(b_in[:], conv_b_in[0].rearrange("(c p) -> p c", p=P)).then_inc(const_ld, 16)
        for c in range(DC):
            act.dma_start(w_dw[:, :, c], conv_w_dw[0, :, P * c:P * c + P].rearrange("k p -> p k")).then_inc(const_ld, 16)
        act.dma_start(b_dw[:], conv_b_dw[0].rearrange("(c p) -> p c", p=P)).then_inc(const_ld, 16)
        act.dma_start(cg[:], conv_ln_g[0].rearrange("(c p) -> p c", p=P)).then_inc(const_ld, 16)
        act.dma_start(cb[:], conv_ln_b[0].rearrange("(c p) -> p c", p=P)).then_inc(const_ld, 16)
        act.dma_start(g_q[:], mla_g_q[0].rearrange("(c p) -> p c", p=P)).then_inc(const_ld, 16)
        act.dma_start(g_kv[:], mla_g_kv[0].rearrange("(c p) -> p c", p=P)).then_inc(const_ld, 16)
        act.dma_start(pages[:], page_table.rearrange("(o b) n -> o (b n)", o=1)).then_inc(const_ld, 16)
        act.dma_start(new_conv_s[0, :, 0:HIST - DEC_T], state_conv[0, :, DEC_T:HIST]).then_inc(stores, 16)

        def split(u, it=None):
            if u >= U_MOE:
                return
            extra = 0 if it is None else it * 6
            act.wait_ge(raw_ready[u % RAW], raw_target(u) + (0 if it is None else it * 32))
            if u >= SPLIT:
                act.wait_ge(unit_used, extra + (u - SPLIT + 1))
            todo = split_copies(u, w_hi[:, u % SPLIT], raw[:, u % RAW])
            for o, i in todo:
                last = nc.scalar.activation(o, i, ACT.Copy)
            last.then_inc(hi_done, 1)

        for u in range(AHEAD):
            split(u)
        for c in range(DC):
            act.wait_ge(xpose, c + 1)
            nc.scalar.activation(x_hi[:, c], ps[:, 6 + c % 2, 0:T], ACT.Copy).then_inc(xin_raw, 1)
        act.wait_ge(consts_made, 8)
        act.wait_ge(const_ld, CONST_LOADS * 16)
        for m in range(8):
            split(U_CIN + m + AHEAD)
            act.wait_ge(unit_used, U_CIN + m + 1)
            if m >= 2:
                act.wait_ge(group_free, m - 1)
            nc.scalar.activation(gate[:, m % 2], ps[:, 2 * ((G_CIN + m) % 3) + 1, 0:T], ACT.Sigmoid,
                                 bias=b_in[:, DC + m:DC + m + 1]).then_inc(gate_ready, 1)

        def layer_norm(n, out, func, g, b):
            act.wait_ge(ln_cent, n + 1)
            nc.scalar.activation(sq[:], work[:], ACT.Square).then_inc(ln_sq, 1)
            act.wait_ge(ln_var, n + 1)
            nc.scalar.activation(rstd[:], ps[:, 7, 0:T], ACT.Sqrt, scale=1.0 / D, bias=eps[:, 0:1]).then_inc(ln_std, 1)
            act.wait_ge(ln_scaled, n + 1)
            for c in range(DC):
                last = nc.scalar.activation(out[:, c], work[:, c], func, scale=g(c), bias=b(c))
            chain(last)
            nc.scalar.activation(x_hi[:], out[:], ACT.Copy).then_inc(ln_hi, 1)

        layer_norm(0, sq, ACT.Silu, lambda c: cg[:, c:c + 1], lambda c: cb[:, c:c + 1])
        act.wait_ge(edge_copied, 1)
        act.dma_start(new_conv_p[0, 0], edge[0:HIST, 0]).then_inc(edge_out, 16)
        for s_ in range(DEC_B):
            act.dma_start(new_conv_s[0, s_, HIST - DEC_T:HIST], edge[DEC_T * s_:DEC_T * s_ + DEC_T, 1]).then_inc(edge_out, 16)
        for i in range(4):
            split(U_COUT + i + AHEAD)
        layer_norm(1, xres, ACT.Identity, lambda c: lng[:, 0, c:c + 1], lambda c: lnb[:, 0, c:c + 1])

        def gate_silu(r, it=0):
            if isinstance(it, int):
                split(U_GU + 6 * it + r + AHEAD)
            else:
                split(U_GU + r + AHEAD, it)
            act.wait_ge(unit_used, it * 6 + (U_GU + r + 1))
            act.wait_ge(group_free, it * 6 + (G_GU + r - 1))
            nc.scalar.activation(gate[:, r % 2], ps[:, 2 * ((G_GU + r) % 3), 0:T], ACT.Silu).then_inc(gate_ready, 1)

        with act.Fori(0, 3) as it:
            for r in range(6):
                gate_silu(r, it)
        for r in range(FC - 18):
            gate_silu(r, 3)
        for i in range(12):
            split(U_DOWN + i + AHEAD)
        layer_norm(2, xres, ACT.Identity, lambda c: lng[:, 1, c:c + 1], lambda c: lnb[:, 1, c:c + 1])

        act.dma_start(cosT[:], cos_t).then_inc(att_ld, 16)
        act.dma_start(sinT[:], sin_t).then_inc(att_ld, 16)
        for i in range(4):
            split(U_MIN + i + AHEAD)
        act.wait_ge(group_free, G_MIN + 3)
        nc.scalar.activation(sq[:, 0:4], cq_f[:], ACT.Square)
        nc.scalar.activation(sq[:, 4:6], ckvT[:], ACT.Square).then_inc(mla_act, 1)
        act.wait_ge(mla_pe, 1)
        nc.scalar.activation(rstd[:], ps[:, 6, 0:T], ACT.Sqrt, scale=1.0 / QLORA, bias=eps[:, 1:2])
        nc.scalar.activation(rms_kv, ps[:, 7, 0:T], ACT.Sqrt, scale=1.0 / LORA, bias=eps[:, 1:2]).then_inc(rms_rt, 1)
        act.wait_ge(mla_dve, 1)
        for c in range(4):
            nc.scalar.activation(cq_f[:, c], cq_f[:, c], ACT.Copy, scale=g_q[:, c:c + 1])
        for c in range(RC):
            last = nc.scalar.activation(ckvT[:, c], ckvT[:, c], ACT.Copy, scale=g_kv[:, c:c + 1])
        chain(last)
        nc.scalar.activation(cq_hi[:], cq_f[:], ACT.Copy).then_inc(mla_act, 1)
        act.wait_ge(mla_pe, 2)
        act.dma_start(wuk[:], mla_w_uk[0].rearrange("(c p) h d -> p c (h d)", p=P)).then_inc(att_ld, 16)
        for b, (t0, n) in enumerate(TB):
            nc.scalar.activation(ckvN[0:n, b], ps[0:n, 6, 0:LORA] if b == 0 else ps[0:n, 6, 256:512] if b == 1
                                 else ps[0:n, 7, 0:LORA], ACT.Copy)
            last = nc.scalar.activation(krN[0:n, b], ps[0:n, 7, 256 + 32 * b:288 + 32 * b], ACT.Copy)
        last.then_inc(kvN_copied, 1)
        act.wait_ge(kvN_copied, 1)
        for b, (t0, n) in enumerate(TB[:2]):
            act.dma_start(new_ckv_p[0, 0, t0:t0 + n], ckvN[0:n, b]).then_inc(stores, 16)
            act.dma_start(new_kr_p[0, 0, t0:t0 + n], krN[0:n, b]).then_inc(stores, 16)
        act.dma_start(new_ckv_p[0, 0, TAIL0:T_P], ckvN[0:QT, 2]).then_inc(stores, 16)
        act.dma_start(new_kr_p[0, 0, TAIL0:T_P], krN[0:QT, 2]).then_inc(stores, 16)
        act.dma_start(new_ckv_s[0].rearrange("b t r -> (b t) r"), ckvN[QT:TAIL, 2]).then_inc(stores, 16)
        act.dma_start(new_kr_s[0].rearrange("b t r -> (b t) r"), krN[QT:TAIL, 2]).then_inc(stores, 16)
        for i in range(4):
            split(U_UQ + i + AHEAD)
        act.wait_ge(uq_free, 4)
        act.wait_ge(unit_used, U_MOUT)
        act.dma_start(wuv[:], mla_w_uv[0].rearrange("(c p) h v -> p c (h v)", p=P)).then_inc(att_w, 16)
        for r in range(4):
            for hh_ in range(4):
                act.dma_start(qrt[32 * r:32 * r + 32, hh_:HEADS:4, :], qrT[32 * hh_:32 * hh_ + 32, :, TAIL0:T]
                              ).then_inc(qrt_ld, 16)
        for j in range(HEADS // 2):
            act.wait_ge(mla_pe, 3 + j)
            nc.scalar.activation(wukT[:, j], ps[:, 6 + j % 2, 0:LORA], ACT.Copy).then_inc(mla_act, 1)

        def soft(i, n_groups):
            b = i % 2
            act.wait_ge(p_sm, i + 1)
            for o, a, e in n_groups:
                last = nc.scalar.activation(sc[:, b, a:e], sc[:, b, a:e], ACT.Exp, scale=SM_SCALE,
                                            bias=pst[:, b, o:o + 1], accum_out=pst[:, b, 2 + o:3 + o])
            last.then_inc(p_ex, 1)

        def pt_copy(i, n):
            act.wait_ge(p_tr, i + 1)
            if i >= 2:
                act.wait_ge(p_pv, i - 1)
            nc.scalar.activation(pT[:, i % 2, 0:n], ps[:, 5, 0:n], ACT.Copy).then_inc(p_pt, 1)

        for h in range(HEADS + 1):
            if h < HEADS:
                act.wait_ge(p_ql, h + 1)
                if h >= 2:
                    act.wait_ge(p_sc, h - 1)
                for c in range(RC):
                    nc.scalar.activation(ql[:, h % 2, c], ps[:, c, 0:T], ACT.Copy)
                for c in range(RC):
                    last = nc.scalar.activation(qlt[:, c, h], ps[:, c, TAIL0:T], ACT.Copy)
                last.then_inc(p_qc, 1)
                soft(h, [(0, 0, P), (1, P, 3 * P)])
            if h >= 1:
                pt_copy(h - 1, 3 * P)
        for i in range(2):
            soft(HEADS + i, [(0, 0, T_P)])
            pt_copy(HEADS + i, 3 * P)

        with act.Fori(0, DEC_B // 2) as it:
            for b in range(2):
                for g in range(4):
                    act.wait_ge(s_t, it * 8 + (4 * b + g + 1))
                    if b * 4 + g >= 2:
                        act.wait_ge(s_sc, it * 8 + (4 * b + g - 1))
                    for c in range(2):
                        last = nc.scalar.activation(kt[:, g % 2, 2 * c:2 * c + 2], ps[:, c, 0:512].rearrange(
                            "p (a r) -> p a r", a=2), ACT.Copy)
                    last.then_inc(s_kt, 1)
                act.wait_ge(s_sh, it * 2 + (b + 1))
                nc.scalar.activation(ss[:], ss[:], ACT.Exp, scale=SM_SCALE)
                nc.scalar.activation(sn[0:DEC_T, :], sn[0:DEC_T, :], ACT.Exp, scale=SM_SCALE).then_inc(s_ex, 1)

        act.wait_ge(v_ready, 1)
        nc.scalar.activation(x_hi[:], qnT[:], ACT.Copy).then_inc(ln_hi, 1)
        for i in range(4):
            split(U_MOUT + i + AHEAD)
        act.wait_ge(ln_cent, 4)
        nc.scalar.activation(sq[:], work[:], ACT.Square).then_inc(ln_sq, 1)
        act.wait_ge(ln_var, 4)
        nc.scalar.activation(rstd[:], ps[:, 7, 0:T], ACT.Sqrt, scale=1.0 / D, bias=eps[:, 0:1]).then_inc(ln_std, 1)
        act.wait_ge(ln_scaled, 4)
        for c in range(DC):
            last = nc.scalar.activation(xres[:, c], work[:, c], ACT.Identity, scale=lng[:, 2, c:c + 1], bias=lnb[:, 2, c:c + 1])
        last.then_inc(ln_hi, 1)
        for i in range(6):
            b, hf = divmod(i, 2)
            n = TB[b][1]
            act.wait_ge(rt_pe, i + 1)
            nc.scalar.activation(xt[0:n, b, 512 * hf:512 * hf + 512], ps[0:n, i % 2, :], ACT.Copy).then_inc(rt_act, 1)
        act.wait_ge(rt_dve, 1)
        nc.scalar.activation(tk[:, 3], tk[:, 2], ACT.Exp).then_inc(rt_act, 1)

        act.wait_ge(table_ready, 1)
        n_jobs = act.value_load(jobi[0:1, MAX_JOBS:MAX_JOBS + 1], min_val=NEXP, max_val=MAX_JOBS)

        def y_upper(jobs_done):
            act.wait_ge(unit_used, jobs_done * JOB_UNITS + U_MOE)
            for q in range(2):
                last = nc.scalar.activation(y_hi[:, 512 * q:512 * q + 512], ps[:, 4 + q, :], ACT.Copy)
            last.then_inc(m_yhi, 1)

        def gathered(part, job):
            act.wait_ge(m_g, job * 2 + (part + 1))
            nc.scalar.activation(g_next[:, 4 * part:4 * part + 4], ps[:, 7, :].rearrange("p (c s) -> p c s", c=4), ACT.Copy
                                 ).then_inc(m_gc, 1)

        def next_upper():
            nc.scalar.activation(g_hi[:], g_next[:], ACT.Copy).then_inc(m_gh, 1)

        gathered(0, 0)
        gathered(1, 0)
        act.wait_ge(m_gc, 2)
        next_upper()
        act.wait_ge(m_zero, 1)
        with act.Fori(0, n_jobs) as j:
            def split_moe(k):
                if k >= JOB_UNITS:
                    return
                u = U_MOE + k
                act.wait_ge(raw_ready[u % RAW], moe_raw_target(k, j))
                act.wait_ge(unit_used, j * JOB_UNITS + (u - SPLIT + 1))
                nc.scalar.activation(w_hi[:, u % SPLIT], raw[:, u % RAW], ACT.Copy).then_inc(hi_done, 1)

            split_moe(0)
            split_moe(1)
            y_upper(j)
            k = 0
            for s in range(STEPS + 1):
                if s < STEPS:
                    split_moe(k + 2)
                    split_moe(k + 3)
                    k += 2
                if s >= 1:
                    act.wait_ge(m_hT, j * STEPS + s)
                    nc.scalar.activation(hT_hi[:], ps[:, 6, :].rearrange("p (c s) -> p c s", c=4), ACT.Copy).then_inc(m_hTc, 1)
                if s < STEPS:
                    act.wait_ge(unit_used, j * JOB_UNITS + (U_MOE + first_unit(s) + 2))
                    nc.scalar.activation(sg[:, s % 2], ps[:, 2 * (s % 2), :], ACT.Silu).then_inc(m_sg, 1)
                    split_moe(k + 2)
                    split_moe(k + 3)
                    k += 2
                if s == TURN_STEP:
                    act.wait_ge(m_pickT, j + 1)
                    nc.scalar.activation(pickT[:], ps[:, 7, 0:3 * P].rearrange("p (b t) -> p b t", b=3), ACT.Copy
                                         ).then_inc(m_pickTc, 1)
                if s in GATHER_STEPS:
                    gathered(GATHER_STEPS.index(s), j + 1)
                if 1 <= s < STEPS:
                    split_moe(k + 2)
                    split_moe(k + 3)
                    k += 2
            act.wait_ge(unit_used, j * JOB_UNITS + (U_MOE + JOB_UNITS - 4))
            next_upper()
        y_upper(n_jobs)

        act.dma_start(gbc[:], ln_g[1, 1:2].partition_broadcast(P) if False else ln_g[1, 1:2].broadcast_to([P, D])).then_inc(fin_ld, 16)
        act.dma_start(bbc[:], ln_b[1, 1:2].broadcast_to([P, D])).then_inc(fin_ld, 16)
        for b, (t0, n) in enumerate(TB):
            act.wait_ge(fin_v, 2 * b + 1)
            nc.scalar.activation(sqt[0:n], acc[0:n, b], ACT.Square, accum_out=stat[0:n, b, 2:3]).then_inc(fin_sq, 1)
            act.wait_ge(fin_sq, b + 1)
            nc.scalar.activation(stat[0:n, b, 3:4], stat[0:n, b, 2:3], ACT.Sqrt, scale=1.0 / D, bias=eps[0:n, 0:1]).then_inc(fin_a, 1)
            act.wait_ge(fin_v, 2 * b + 2)
            if b == 0:
                act.dma_start(y_prompt[0, 0:P - N_META], acc[N_META:P, 0]).then_inc(stores, 16)
            elif b == 1:
                act.dma_start(y_prompt[0, P - N_META:2 * P - N_META], acc[:, 1]).then_inc(stores, 16)
            else:
                act.dma_start(y_prompt[0, 2 * P - N_META:SEQ], acc[0:QT, 2]).then_inc(stores, 16)
                act.dma_start(y_sample.rearrange("b t d -> (b t) d"), acc[QT:TAIL, 2]).then_inc(stores, 16)
        act.wait_ge(stores, STORES * 16)

    @block.vector
    def _(v):
        V = nc.vector
        n_own = [0]

        def mark(ins):
            n_own[0] += 1
            ins.then_inc(dve, 1)

        def settle():
            v.wait_ge(dve, n_own[0])

        def chain(ins):
            mark(ins)
            settle()

        def split(u, it=None):
            if u >= U_MOE:
                return
            v.wait_ge(hi_done, (u + 1) if it is None else it * 6 + (u + 1))
            his = [o for o, _ in split_copies(u, w_hi[:, u % SPLIT], raw[:, u % RAW])]
            los = split_copies(u, w_lo[:, u % SPLIT], raw[:, u % RAW])
            for hi, (lo, src) in zip(his, los):
                last = V.tensor_tensor(lo, src, hi.bitcast(F32), ALU.subtract)
            last.then_inc(lo_done, 1)

        for u in range(AHEAD):
            split(u)
        for c in range(DC):
            v.wait_ge(xin_raw, c + 1)
            V.tensor_tensor(x_lo[:, c], ps[:, 6 + c % 2, 0:T], x_hi[:, c].bitcast(F32), ALU.subtract)
            V.tensor_copy(xres[:, c], ps[:, 6 + c % 2, 0:T]).then_inc(xpose_free, 1)
        for c in range(DC):
            v.wait_ge(xpose, DC + c + 1)
            last = V.tensor_copy(u_s[:, c, :, 0:HIST], ps[:, 6 + c % 2, 0:DEC_B * HIST].rearrange("p (s t) -> p s t", s=DEC_B))
            last.then_inc(xpose_free, 1)
        v.wait_ge(const_ld, CONST_LOADS * 16)
        v.wait_ge(consts_made, 8)
        def add_taps(m):
            v.wait_ge(diag_used, PE_TAPS * (m + 1))
            V.tensor_tensor(work[:, m], work[:, m], ps[:, 6 + m % 2, 0:T], ALU.add).then_inc(ln_in, 1)

        for m in range(8):
            split(U_CIN + m + AHEAD)
            v.wait_ge(gate_ready, m + 1)
            a = ps[:, 2 * ((G_CIN + m) % 3)]
            V.scalar_tensor_tensor(out=u_p[:, m, HIST:], in0=a[:, 0:T_P], scalar=b_in[:, m:m + 1],
                                   in1=gate[:, m % 2, 0:T_P], op0=ALU.add, op1=ALU.mult)
            last = V.scalar_tensor_tensor(out=u_s[:, m, :, HIST:], in0=a[:, T_P:T].rearrange("p (s t) -> p s t", s=DEC_B),
                                          scalar=b_in[:, m:m + 1],
                                          in1=gate[:, m % 2, T_P:T].rearrange("p (s t) -> p s t", s=DEC_B),
                                          op0=ALU.add, op1=ALU.mult)
            last.then_inc(group_free, 1)
            v.wait_ge(group_free, m + 1)
            wp = work[:, m, 0:T_P]
            wsm = work[:, m, T_P:T].rearrange("p (s t) -> p s t", s=DEC_B)
            for t in range(PE_TAPS, TAPS):
                if t == PE_TAPS:
                    mark(V.tensor_scalar(wp, u_p[:, m, t:t + T_P], w_dw[:, t, m:m + 1], b_dw[:, m:m + 1], ALU.mult, ALU.add))
                    mark(V.tensor_scalar(wsm, u_s[:, m, :, t:t + DEC_T], w_dw[:, t, m:m + 1], b_dw[:, m:m + 1], ALU.mult, ALU.add))
                else:
                    v.wait_ge(dve, n_own[0] - 1)
                    mark(V.scalar_tensor_tensor(out=wp, in0=u_p[:, m, t:t + T_P], scalar=w_dw[:, t, m:m + 1], in1=wp,
                                                op0=ALU.mult, op1=ALU.add))
                    v.wait_ge(dve, n_own[0] - 1)
                    mark(V.scalar_tensor_tensor(out=wsm, in0=u_s[:, m, :, t:t + DEC_T], scalar=w_dw[:, t, m:m + 1],
                                                in1=wsm, op0=ALU.mult, op1=ALU.add))
            if m >= 1:
                add_taps(m - 1)
        settle()
        add_taps(7)
        V.tensor_copy(u_new[:].rearrange("p c (s t) -> p c s t", s=DEC_B), u_s[:, :, :, HIST:]).then_inc(ln_in, 1)
        v.wait_ge(edge_ready, 1)
        V.tensor_copy(edge[0:HIST, 0].rearrange("p (b n) -> p b n", b=2), ps[0:HIST, 4:6, :])
        V.tensor_copy(edge[0:T_S, 1].rearrange("p (b n) -> p b n", b=2), ps[0:T_S, 0:2, :]).then_inc(edge_copied, 1)

        def layer_norm(n, out, split_x=True):
            v.wait_ge(ln_mean, n + 1)
            chain(V.tensor_scalar(rstd[:], ps[:, 6, 0:T], 1.0 / D, None, ALU.mult))
            V.tensor_tensor(work[:], work[:], rstd[:].unsqueeze(1).broadcast_to([P, DC, T]), ALU.subtract).then_inc(ln_cent, 1)
            v.wait_ge(ln_std, n + 1)
            chain(V.reciprocal(rstd[:], rstd[:]))
            V.tensor_tensor(work[:], work[:], rstd[:].unsqueeze(1).broadcast_to([P, DC, T]), ALU.mult).then_inc(ln_scaled, 1)
            if split_x:
                v.wait_ge(ln_hi, n + 1)
                V.tensor_tensor(x_lo[:], out[:], x_hi[:].bitcast(F32), ALU.subtract).then_inc(x_split, 1)

        def residual(u, g, c0):
            v.wait_ge(unit_used, u + 1)
            for o in range(2):
                last = V.scalar_tensor_tensor(out=work[:, c0 + o], in0=xres[:, c0 + o], scalar=ALPHA,
                                              in1=ps[:, 2 * (g % 3) + o, 0:T], op0=ALU.mult, op1=ALU.add)
            last.then_inc(group_free, 1)

        layer_norm(0, sq)
        for i in range(4):
            split(U_COUT + i + AHEAD)
            residual(U_COUT + i, G_COUT + i, 2 * i)
        layer_norm(1, xres)

        own_gu = n_own[0]
        v.wait_ge(edge_out, 16 * (1 + DEC_B))

        def ffn_h(r, it=0):
            if isinstance(it, int):
                split(U_GU + 6 * it + r + AHEAD)
            else:
                split(U_GU + r + AHEAD, it)
            v.wait_ge(gate_ready, it * 6 + (8 + r + 1))
            idx = it * 6 + r
            hs, ls = (h_hi[:, idx], h_lo[:, idx]) if isinstance(it, int) else (
                h_hi[:, bass.ds(idx, 1)].rearrange("p a t -> p (a t)"), h_lo[:, bass.ds(idx, 1)].rearrange("p a t -> p (a t)"))
            V.tensor_tensor(htmp[:, r % 2], gate[:, r % 2], ps[:, 2 * ((G_GU + r) % 3) + 1, 0:T], ALU.mult).then_inc(group_free, 1)
            v.wait_ge(group_free, it * 6 + (G_GU + r + 1))
            V.tensor_scalar(hs, htmp[:, r % 2], 1.0, None, ALU.mult).then_inc(dve, 1)
            v.wait_ge(dve, it * 6 + (own_gu + r + 1))
            V.tensor_tensor(ls, htmp[:, r % 2], hs.bitcast(F32), ALU.subtract).then_inc(h_split, 1)

        with v.Fori(0, 3) as it:
            for r in range(6):
                ffn_h(r, it)
        for r in range(FC - 18):
            ffn_h(r, 3)
        n_own[0] += FC
        for i in range(4):
            for k in range(3):
                split(U_DOWN + 3 * i + k + AHEAD)
            residual(U_DOWN + 3 * i + 2, G_DOWN + i, 2 * i)
        layer_norm(2, xres)

        for i in range(3):
            split(U_MIN + i + AHEAD)
            g = G_MIN + i
            v.wait_ge(unit_used, U_MIN + i + 1)
            for o in range(2):
                dst = cq_f[:, 2 * i + o] if i < 2 else ckvT[:, o]
                last = V.tensor_copy(dst, ps[:, 2 * (g % 3) + o, 0:T])
            last.then_inc(group_free, 1)
        split(U_MIN + 3 + AHEAD)
        v.wait_ge(att_ld, 32)
        g = G_MIN + 3

        def rotate(dst, x_ps, sw_ps):
            mark(V.tensor_tensor(htmp_a, sw_ps, sinT[:], ALU.mult))
            chain(V.tensor_tensor(dst, x_ps, cosT[:], ALU.mult))
            return V.tensor_tensor(dst, dst, htmp_a, ALU.add)

        htmp_a = work[:, 0]
        v.wait_ge(unit_used, U_MIN + 4)
        rotate(krT[:], ps[:, 2 * (g % 3), 0:T], ps[:, 2 * (g % 3) + 1, 0:T]).then_inc(group_free, 1)
        v.wait_ge(group_free, G_MIN + 4)
        v.wait_ge(rms_rt, 1)
        chain(V.reciprocal(rstd[:], rstd[:]))
        mark(V.tensor_tensor(cq_f[:], cq_f[:], rstd[:].unsqueeze(1).broadcast_to([P, 4, T]), ALU.mult))
        settle()
        chain(V.reciprocal(rms_kv, rms_kv))
        V.tensor_tensor(ckvT[:], ckvT[:], rms_kv.unsqueeze(1).broadcast_to([P, RC, T]), ALU.mult).then_inc(mla_dve, 1)
        v.wait_ge(mla_act, 2)
        V.tensor_tensor(cq_lo[:], cq_f[:], cq_hi[:].bitcast(F32), ALU.subtract).then_inc(mla_dve, 1)
        for i in range(4):
            split(U_UQ + i + AHEAD)
            v.wait_ge(unit_used, U_UQ + i + 1)
            pb = 4 * (i % 2)
            V.tensor_copy(qnT[:, 2 * i], ps[:, pb, 0:T])
            V.tensor_copy(qnT[:, 2 * i + 1], ps[:, pb + 1, 0:T])
            if i:
                v.wait_ge(uq_free, i)
            rotate(qrT[:, i], ps[:, pb + 2, 0:T], ps[:, pb + 3, 0:T]).then_inc(uq_free, 1)
        v.wait_ge(attc, 8)
        v.wait_ge(qrt_ld, 16 * 16)
        chain(V.tensor_scalar(row_i[:], row_i[:], QT - 1, None, ALU.bitwise_and))
        chain(V.tensor_copy(kt[:, 0, 0, 1:2], row_i[:]))
        V.tensor_scalar(causal_t[:], kt[:, 0, 1, 0:QT], kt[:, 0, 0, 1:2], NEG, ALU.is_gt, ALU.mult).then_inc(mask_ready, 1)
        v.wait_ge(mask_ready, 1)

        def shift(i, groups, mask_at, mask):
            b = i % 2
            v.wait_ge(p_sc, i + 1)
            bank = 2 + i % 2
            n = groups[-1][2]
            if i >= 2:
                v.wait_ge(p_tr, i - 1)
            if mask_at:
                V.tensor_copy(sc[:, b, 0:mask_at], ps[:, bank, 0:mask_at])
            chain(V.tensor_tensor(sc[:, b, mask_at:n], ps[:, bank, mask_at:n], mask, ALU.add))
            for o, a, e in groups:
                mark(V.reduce_max(pst[:, b, 4 + o:5 + o], sc[:, b, a:e], AX))
            settle()
            V.tensor_scalar(pst[:, b, 0:2], pst[:, b, 4:6], -SM_SCALE, None, ALU.mult).then_inc(p_sm, 1)

        def norm(i, groups):
            b = i % 2
            v.wait_ge(p_ex, i + 1)
            chain(V.reciprocal(pst[:, b, 6:8], pst[:, b, 2:4]))
            for o, a, e in groups:
                last = V.tensor_scalar(sc[:, b, a:e], sc[:, b, a:e], pst[:, b, 6 + o:7 + o], None, ALU.mult)
            last.then_inc(p_nm, 1)

        G2 = [(0, 0, P), (1, P, 3 * P)]
        v.wait_ge(p_ql, 1)
        chain(V.memset(pst[:], 1.0))
        for h in range(HEADS + 1):
            if h < HEADS:
                shift(h, G2, 0, causal[:])
                norm(h, G2)
            if h >= 1:
                k = h - 1
                v.wait_ge(p_pv, k + 1)
                if k >= 2:
                    v.wait_ge(p_v, k - 1)
                V.tensor_copy(oT[:, k % 2], ps[:, 6, :].rearrange("p (c q) -> p c q", c=RC)).then_inc(p_ot, 1)
                v.wait_ge(p_v, k + 1)
                r0 = VH * (k % 2)
                V.tensor_copy(qnT[r0:r0 + VH, k // 2, 0:2 * P], ps[r0:r0 + VH, 7, 0:2 * P]).then_inc(p_vc, 1)
        v.wait_ge(p_qc, HEADS)
        for i in range(2):
            for c in range(RC):
                V.tensor_copy(tailq[i][:, c].rearrange("p (h q) -> p h q", h=8), qlt[:, c, 8 * i:8 * i + 8, 0:QT])
            V.tensor_copy(tailq[i][:, RC].rearrange("p (h q) -> p h q", h=8), qrt[:, 8 * i:8 * i + 8, 0:QT]).then_inc(tail_ready, 1)
        for i in range(2):
            k = HEADS + i
            shift(k, [(0, 0, T_P)], 2 * P, causal_t[:])
            norm(k, [(0, 0, T_P)])
            v.wait_ge(p_pv, k + 1)
            V.tensor_copy(qlt[:, :, 8 * i:8 * i + 8, 0:QT], ps[:, 6, 0:RC * P].rearrange("p (c h q) -> p c h q", c=RC, h=8)).then_inc(p_vc, 1)

        NQ = HEADS * DEC_T
        mark(V.memset(qsr[:], 0.0))
        chain(V.memset(mx[:, NQ:2 * NQ], 0.0))
        with v.Fori(0, DEC_B // 2) as it:
            OWN = 6
            for b in range(2):
                s = it * 2 + b
                cnt = [0]

                def done(ins):
                    cnt[0] += 1
                    ins.then_inc(s_st, 1)
                    v.wait_ge(s_st, s * OWN + cnt[0])

                if b == 1:
                    v.wait_ge(s_free, it * 2 + 1)
                for c in range(RC):
                    V.tensor_scalar(qs[:, c].rearrange("p (h t) -> p h t", h=HEADS), qlt[:, c, :, bass.ds(s * DEC_T + QT, DEC_T)],
                                    1.0, None, ALU.mult)
                    V.tensor_copy(kn[:, c], ckvT[:, c, bass.ds(s * DEC_T + T_P, DEC_T)])
                V.tensor_copy(kn[:, RC], krT[:, bass.ds(s * DEC_T + T_P, DEC_T)])
                for p in range(4):
                    rs = slice(32 * p, 32 * p + 32)
                    last = V.tensor_copy(qsr[rs, p].rearrange("p (h t) -> p h t", h=HEADS), qrt[rs, :, bass.ds(s * DEC_T + QT, DEC_T)])
                last.then_inc(s_q, 1)
                for g in range(4):
                    v.wait_ge(s_t, s * 4 + (g + 1))
                    if b * 4 + g >= 2:
                        v.wait_ge(s_sc, s * 4 + (g - 1))
                    V.tensor_copy(kr4[:, g % 2], ps[:, 2, 0:P]).then_inc(s_kn, 1)
                v.wait_ge(s_new, s + 1)
                V.tensor_copy(knN[0:DEC_T], ps[0:DEC_T, 5, 64:64 + LORA]).then_inc(s_knN, 1)
                v.wait_ge(s_sc, s * 4 + 4)
                mark_ = V.tensor_tensor(sn[0:DEC_T], ps[0:DEC_T, 5, 0:NQ], causal_s[0:DEC_T].rearrange("p h t -> p (h t)"), ALU.add)
                done(mark_)
                done(V.reduce_max(mx[:, 0:NQ], ps[:, 3:5, :].rearrange("p b (g q) -> p q (b g)", q=NQ), AX))
                V.tensor_tensor(mx[0:DEC_T, 0:NQ], mx[0:DEC_T, 0:NQ], sn[0:DEC_T], ALU.max).then_inc(s_mt, 1)
                v.wait_ge(s_dg, s * 2 + 1)
                done(V.reduce_max(m1[0:NQ], ps[0:NQ, 5, 320:448], AX))
                V.tensor_scalar(dg[0:NQ], ident[0:NQ, 0:NQ], m1[0:NQ, 0:1], None, ALU.mult).then_inc(s_mb, 1)
                v.wait_ge(s_dg, s * 2 + 2)
                done(V.tensor_copy(dg[:], ps[:, 5, 448:448 + NQ]))
                V.tensor_tensor(ss[:].rearrange("p (b g) q -> p b g q", b=2), ps[:, 3:5, :].rearrange("p b (g q) -> p b g q", q=NQ),
                                dg[:].unsqueeze(1).unsqueeze(1).broadcast_to([P, 2, 8, NQ]), ALU.subtract)
                V.tensor_tensor(sn[0:DEC_T], sn[0:DEC_T], dg[0:DEC_T], ALU.subtract).then_inc(s_sh, 1)
                v.wait_ge(s_ex, s + 1)
                done(V.reduce_sum(mx[:, 0:NQ], ss[:].rearrange("p g q -> p q g"), AX))
                V.tensor_tensor(mx[0:DEC_T, 0:NQ], mx[0:DEC_T, 0:NQ], sn[0:DEC_T], ALU.add).then_inc(s_sum, 1)
                v.wait_ge(s_pv, s + 1)
                done(V.reciprocal(dg[:], ps[:, 5, 448:448 + NQ]))
                for c in range(RC):
                    last = V.tensor_tensor(qlt[:, c, :, bass.ds(s * DEC_T + QT, DEC_T)],
                                           ps[:, 6 + c, 0:NQ].rearrange("p (h t) -> p h t", h=HEADS),
                                           dg[:].rearrange("p (h t) -> p h t", h=HEADS), ALU.mult)
                last.then_inc(s_free, 1)
                assert cnt[0] == OWN, cnt[0]
        v.wait_ge(p_v, HEADS + 1)
        for h in range(HEADS):
            r0 = VH * (h % 2)
            last = V.tensor_copy(qnT[r0:r0 + VH, h // 2, TAIL0:T], ps[r0:r0 + VH, (h % 4) // 2 + 4 * (h % 2), TAIL * (h // 4):TAIL * (h // 4) + TAIL])
        last.then_inc(v_ready, 1)
        v.wait_ge(ln_hi, 4)
        V.tensor_tensor(x_lo[:], qnT[:], x_hi[:].bitcast(F32), ALU.subtract).then_inc(x_split, 1)
        for i in range(4):
            split(U_MOUT + i + AHEAD)
            residual(U_MOUT + i, G_MOUT + i, 2 * i)
        layer_norm(3, xres, split_x=False)
        for i in range(6):
            b, hf = divmod(i, 2)
            n = TB[b][1]
            cs = slice(512 * hf, 512 * hf + 512)
            v.wait_ge(rt_act, i + 1)
            V.tensor_scalar(acc[0:n, b, cs], ps[0:n, i % 2, :], ALPHA, None, ALU.mult).then_inc(xpose_free, 1)
        v.wait_ge(rt_const, 8)
        v.wait_ge(rt_pe, 7)
        V.tensor_copy(lg[:, 0:2], ps[:, 2, 0:2 * NEXP].rearrange("p (b e) -> p b e", b=2))
        chain(V.tensor_copy(lg[0:TAIL, 2], ps[0:TAIL, 2, 2 * NEXP:3 * NEXP]))
        for b in range(3):
            one = lg[:, b].unsqueeze(2).broadcast_to([P, NEXP, NEXP])
            other = lg[:, b].unsqueeze(1).broadcast_to([P, NEXP, NEXP])
            mark(V.tensor_tensor(cmp_[:, 0:NEXP], other, one, ALU.is_gt))
            chain(V.tensor_tensor(cmp2[:], other, one, ALU.is_equal))
            chain(V.tensor_tensor(cmp2[:], cmp2[:], lt8[:], ALU.mult))
            chain(V.tensor_tensor(cmp2[:], cmp2[:], cmp_[:, 0:NEXP], ALU.add))
            chain(V.reduce_sum(rank[:, b], cmp2[:], AX))
        mark(V.tensor_scalar(oneA[:], rank[:], 0.0, None, ALU.is_equal))
        chain(V.tensor_scalar(oneB[:], rank[:], 1.0, None, ALU.is_equal))
        mark(V.tensor_tensor(oneA[:], oneA[:], valid[:], ALU.mult))
        chain(V.tensor_tensor(oneB[:], oneB[:], valid[:], ALU.mult))
        mark(V.tensor_tensor(selt[:], oneA[:], oneB[:], ALU.add))
        chain(V.tensor_tensor(keyt[:], oneA[:], lg[:], ALU.mult))
        chain(V.reduce_sum(tk[:, 0], keyt[:], AX))
        chain(V.tensor_tensor(keyt[:], oneB[:], lg[:], ALU.mult))
        chain(V.reduce_sum(tk[:, 1], keyt[:], AX))
        V.tensor_tensor(tk[:, 2], tk[:, 1], tk[:, 0], ALU.subtract).then_inc(rt_dve, 1)
        v.wait_ge(rt_act, 7)
        chain(V.tensor_scalar(tk[:, 4], tk[:, 3], 1.0, None, ALU.add))
        chain(V.reciprocal(tk[:, 4], tk[:, 4]))
        chain(V.tensor_tensor(tk[:, 5], tk[:, 4], tk[:, 3], ALU.mult))
        v.wait_ge(rt_pe, 8)
        counts = ps[:, 4, 32:32 + NEXP]
        mark(V.tensor_scalar(jobs[:, 0], counts, float(SLOTS), None, ALU.is_gt))
        chain(V.tensor_scalar(jobs[:, 1], counts, float(2 * SLOTS), None, ALU.is_gt))
        chain(V.tensor_tensor(jobs[:, 0], jobs[:, 0], jobs[:, 1], ALU.add))
        chain(V.tensor_scalar(jobs[:, 0], jobs[:, 0], 1.0, None, ALU.add))
        chain(V.tensor_tensor(cmp2[:], jobs[:, 0].unsqueeze(1).broadcast_to([P, NEXP, NEXP]), lt8[:], ALU.mult))
        chain(V.reduce_sum(starts[:], cmp2[:], AX))
        for b in range(3):
            chain(V.scalar_tensor_tensor(out=keyt[:, b], in0=starts[:], scalar=float(SLOTS), in1=ps[:, 4, NEXP * b:NEXP * b + NEXP],
                                         op0=ALU.mult, op1=ALU.add))
        chain(V.tensor_scalar(keyt[:], keyt[:], 1.0, None, ALU.add))
        for o, one in enumerate((oneA, oneB)):
            chain(V.tensor_tensor(selt2 := rank[:], keyt[:], one[:], ALU.mult))
            chain(V.reduce_sum(tk[:, 6 + o], rank[:], AX))
            chain(V.tensor_scalar(tk[:, 6 + o], tk[:, 6 + o], -1.0, None, ALU.add))
        chain(V.tensor_tensor(cmp_[:], jobf[:, 0:MAX_JOBS].unsqueeze(2).broadcast_to([P, MAX_JOBS, NEXP]),
                              starts[:].unsqueeze(1).broadcast_to([P, MAX_JOBS, NEXP]), ALU.is_ge))
        chain(V.reduce_sum(jobf[:, 0:MAX_JOBS], cmp_[:], AX))
        chain(V.tensor_scalar(jobf[:, 0:MAX_JOBS], jobf[:, 0:MAX_JOBS], -1.0, None, ALU.add))
        chain(V.reduce_sum(jobf[:, MAX_JOBS:MAX_JOBS + 1], jobs[:, 0], AX))
        V.tensor_copy(jobi[:], jobf[:]).then_inc(table_ready, 1)
        v.wait_ge(table_ready, 1)

        n_jobs = v.value_load(jobi[0:1, MAX_JOBS:MAX_JOBS + 1], min_val=NEXP, max_val=MAX_JOBS)

        def make_pick(settled):
            for b in range(3):
                settled(V.tensor_scalar(pick[:, b], iota[:], tk[:, 6, b:b + 1], None, ALU.is_equal), b == 2)
            for b in range(3):
                last = V.scalar_tensor_tensor(out=pick[:, b], in0=iota[:], scalar=tk[:, 7, b:b + 1], in1=pick[:, b],
                                              op0=ALU.is_equal, op1=ALU.add)
            last.then_inc(m_pick, 1)

        def next_lower(job):
            v.wait_ge(m_gh, job + 1)
            V.tensor_tensor(g_lo[:], g_next[:], g_hi[:].bitcast(F32), ALU.subtract).then_inc(m_gl, 1)

        def y_lower(j):
            v.wait_ge(m_yhi, j + 1)
            V.tensor_tensor(y_lo[:].rearrange("p (q n) -> p q n", q=2), ps[:, 4:6, :],
                            y_hi[:].bitcast(F32).rearrange("p (q n) -> p q n", q=2), ALU.subtract).then_inc(m_ylo, 1)

        def add_rows(i, j):
            b, q = divmod(i, 2)
            n = TB[b][1]
            cs = slice(512 * q, 512 * q + 512)
            v.wait_ge(m_sct, j * 6 + (i + 1))
            V.scalar_tensor_tensor(out=acc[0:n, b, cs], in0=ps[0:n, 6 + i % 2, :], scalar=tk[0:n, 8, b:b + 1],
                                   in1=acc[0:n, b, cs], op0=ALU.mult, op1=ALU.add).then_inc(m_acc, 1)

        make_pick(lambda ins, end: chain(ins) if end else mark(ins))
        V.memset(ps[:, 4:6, :], 0.0)
        V.memset(pickT[:].bitcast(F32), 0.0)
        V.memset(tk[:, 8], 0.0).then_inc(m_zero, 1)
        next_lower(0)
        with v.Fori(0, n_jobs) as j:
            OWN = 11
            cnt = [0]

            def mo_mark(ins):
                cnt[0] += 1
                ins.then_inc(m_own, 1)

            def mo_settle():
                v.wait_ge(m_own, j * OWN + cnt[0])

            def split_moe(k):
                u = U_MOE + k
                v.wait_ge(hi_done, j * JOB_UNITS + (u + 1))
                V.tensor_tensor(w_lo[:, u % SPLIT], raw[:, u % RAW], w_hi[:, u % SPLIT].bitcast(F32), ALU.subtract).then_inc(lo_done, 1)

            split_moe(0)
            split_moe(1)
            y_lower(j)
            k = 0
            for s in range(STEPS + 1):
                if s < STEPS:
                    split_moe(k + 2)
                    split_moe(k + 3)
                    k += 2
                if s == 0:
                    add_rows(0, j)
                    add_rows(1, j)
                if s == 1:
                    add_rows(4, j)
                    add_rows(5, j)
                if s >= 1:
                    v.wait_ge(m_hTc, j * STEPS + s)
                    V.tensor_tensor(hT_lo[:], ps[:, 6, :].rearrange("p (c s) -> p c s", c=4), hT_hi[:].bitcast(F32),
                                    ALU.subtract).then_inc(m_hTl, 1)
                if s < STEPS:
                    split_moe(k + 2)
                    split_moe(k + 3)
                    k += 2
                    v.wait_ge(m_sg, j * STEPS + (s + 1))
                    v.wait_ge(unit_used, j * JOB_UNITS + (U_MOE + first_unit(s) + 4))
                    V.tensor_tensor(hh[:, s % 2], sg[:, s % 2], ps[:, 2 * (s % 2) + 1, :], ALU.mult).then_inc(m_h, 1)
                if s == 0:
                    add_rows(2, j)
                    add_rows(3, j)
                if s == TURN_STEP:
                    for o in range(2):
                        mo_mark(V.tensor_scalar(tk[:, 8 + o], tk[:, 6 + o], 0.0, None, ALU.is_ge))
                    for o in range(2):
                        mo_mark(V.tensor_scalar(tk[:, 10 + o], tk[:, 6 + o], float(SLOTS), None, ALU.is_lt))
                    mo_settle()
                    mo_mark(V.tensor_tensor(tk[:, 8:10], tk[:, 8:10], tk[:, 10:12], ALU.mult))
                    mo_settle()
                    mo_mark(V.tensor_tensor(tk[:, 8:10], tk[:, 8:10], tk[:, 4:6], ALU.mult))
                    mo_settle()
                    mo_mark(V.tensor_tensor(tk[:, 8], tk[:, 8], tk[:, 9], ALU.add))
                    mo_mark(V.tensor_scalar(tk[:, 6:8], tk[:, 6:8], -float(SLOTS), None, ALU.add))
                    mo_settle()
                if s == TURN_STEP + 1:
                    v.wait_ge(m_pickT, j + 1)
                    make_pick(lambda ins, end: (mo_mark(ins), mo_settle() if end else None))
                if 1 <= s < STEPS:
                    split_moe(k + 2)
                    split_moe(k + 3)
                    k += 2
            next_lower(j + 1)
            assert cnt[0] == OWN, cnt[0]
        y_lower(n_jobs)
        for i in range(6):
            add_rows(i, n_jobs)
        v.wait_ge(m_acc, n_jobs * 6 + 6)

        v.wait_ge(fin_ld, 32)
        for b, (t0, n) in enumerate(TB):
            a = acc[0:n, b]
            chain(V.reduce_sum(stat[0:n, b, 0:1], a, AX))
            chain(V.tensor_scalar(stat[0:n, b, 1:2], stat[0:n, b, 0:1], -1.0 / D, None, ALU.mult))
            V.tensor_scalar(a, a, stat[0:n, b, 1:2], None, ALU.add).then_inc(fin_v, 1)
            v.wait_ge(fin_a, b + 1)
            chain(V.reciprocal(stat[0:n, b, 3:4], stat[0:n, b, 3:4]))
            chain(V.scalar_tensor_tensor(out=a, in0=a, scalar=stat[0:n, b, 3:4], in1=gbc[0:n], op0=ALU.mult, op1=ALU.mult))
            V.tensor_tensor(a, a, bbc[0:n], ALU.add).then_inc(fin_v, 1)

    @block.tensor
    def _(pe):
        def mm3(out, hi, lo, xh, xl, start, stop):
            nc.tensor.matmul(out, hi, xh, start=start, stop=False, skip_group_check=True)
            nc.tensor.matmul(out, lo, xh, start=False, stop=False, skip_group_check=True)
            return nc.tensor.matmul(out, hi, xl, start=False, stop=stop, skip_group_check=True)

        def linear(u, g, nk, layout, xh, xl, it=None, first=True, last=True, free=True):
            off = 0 if it is None else it * 6
            pe.wait_ge(lo_done, off + (u + 1))
            if first and g >= 3 and free:
                pe.wait_ge(group_free, off + (g - 2))
            hi, lo = layout(w_hi[:, u % SPLIT]), layout(w_lo[:, u % SPLIT])
            for o in range(2):
                for k in range(nk):
                    m = mm3(ps[:, 2 * (g % 3) + o, 0:T], hi(k, o), lo(k, o), xh(k), xl(k),
                            first and k == 0, last and k == nk - 1)
            m.then_inc(unit_used, 1)

        def pairs(w):
            v = w.rearrange("p (c a n) -> p c a n", c=8, a=2)
            return lambda k, o: v[:, k, o, :]

        X = (lambda k: x_hi[:, k], lambda k: x_lo[:, k])
        pe.wait_ge(x_ld, 5 * 16)
        pe.wait_ge(consts_made, 8)
        for c in range(DC):
            if c >= 2:
                pe.wait_ge(xpose_free, c - 1)
            for t0, n in TB:
                m = nc.tensor.transpose(ps[:, 6 + c % 2, t0:t0 + n], xtok[0:n, t0 // P, P * c:P * c + P], ident[0:n, 0:n])
            m.then_inc(xpose, 1)
        pe.wait_ge(hist_ld, 32)
        hb = 4 * HIST
        for c in range(DC):
            pe.wait_ge(xpose_free, DC + c - 1)
            for b in range(2):
                m = nc.tensor.transpose(ps[:, 6 + c % 2, hb * b:hb * b + hb], hist[0:hb, b, P * c:P * c + P], ident[0:hb, 0:hb])
            m.then_inc(xpose, 1)
        pe.wait_ge(xpose_free, 2 * DC)
        def taps(m):
            pe.wait_ge(group_free, m + 1)
            if m >= 2:
                pe.wait_ge(ln_in, m - 1)
            for t in range(PE_TAPS):
                q = PE_TAPS * m + t
                pe.wait_ge(diag_ready, q + 1)
                d = diag[:, q % DIAGS]
                nc.tensor.matmul(ps[:, 6 + m % 2, 0:T_P], d, u_p[:, m, t:t + T_P], start=t == 0, stop=t == PE_TAPS - 1,
                                 skip_group_check=True)
                last = nc.tensor.matmul(ps[:, 6 + m % 2, T_P:T].rearrange("p (s t) -> p s t", s=DEC_B), d, u_s[:, m, :, t:t + DEC_T],
                                        start=False, stop=t == PE_TAPS - 1, skip_group_check=True)
                last.then_inc(diag_used, 1)

        for m_ in range(8):
            linear(U_CIN + m_, G_CIN + m_, 8, pairs, *X)
            if m_ >= 1:
                taps(m_ - 1)
        taps(7)
        pe.wait_ge(group_free, 8)
        pe.wait_ge(ln_in, DC + 1)
        for c in range(DC):
            cs = slice(P * (c % 4), P * (c % 4) + P)
            nc.tensor.transpose(ps[0:HIST, 4 + c // 4, cs], u_p[:, c, T_P:T_P + HIST], ident[:])
            m = nc.tensor.transpose(ps[0:T_S, c // 4, cs], u_new[:, c], ident[:])
        m.then_inc(edge_ready, 1)

        def stats(n, chunks, bank, src, signal):
            for c in range(chunks):
                m = nc.tensor.matmul(ps[:, bank, 0:T], ones[:], src(c), start=c == 0, stop=c == chunks - 1)
            if signal is not None:
                m.then_inc(signal, 1)

        def layer_norm(n):
            stats(n, DC, 6, lambda c: work[:, c], ln_mean)
            pe.wait_ge(ln_sq, n + 1)
            stats(n, DC, 7, lambda c: sq[:, c], ln_var)

        layer_norm(0)
        pe.wait_ge(edge_copied, 1)
        pe.wait_ge(x_split, 1)

        def blocks(w):
            v = w.rearrange("p (c a n) -> p c a n", c=8, a=2)
            return lambda k, o: v[:, k, o, :]

        for i in range(4):
            linear(U_COUT + i, G_COUT + i, 8, blocks, *X)
        pe.wait_ge(group_free, G_COUT + 4)
        layer_norm(1)
        pe.wait_ge(x_split, 2)
        with pe.Fori(0, 3) as it:
            for r in range(6):
                linear(U_GU + r, G_GU + r, 8, pairs, *X, it=it)
        for j in range(18, FC):
            linear(U_GU + j, G_GU + j, 8, pairs, *X)
        pe.wait_ge(h_split, FC)
        for i in range(4):
            for k, (k0, nk) in enumerate(DOWN_KC):
                linear(U_DOWN + 3 * i + k, G_DOWN + i, nk, blocks, lambda q: h_hi[:, k0 + q], lambda q: h_lo[:, k0 + q],
                       first=k == 0, last=k == 2)
        pe.wait_ge(group_free, G_DOWN + 4)
        layer_norm(2)
        pe.wait_ge(x_split, 3)
        for i in range(4):
            linear(U_MIN + i, G_MIN + i, 8, blocks, *X)
        pe.wait_ge(mla_act, 1)
        stats(0, 4, 6, lambda c: sq[:, c], None)
        stats(0, RC, 7, lambda c: sq[:, 4 + c], mla_pe)
        pe.wait_ge(mla_act, 2)
        for b, (t0, n) in enumerate(TB):
            for c in range(RC):
                o = 256 * b + P * c
                nc.tensor.transpose(ps[0:n, 6 + o // 512, o % 512:o % 512 + P], ckvT[:, c, t0:t0 + n], ident[:])
            m = nc.tensor.transpose(ps[0:n, 7, 256 + 32 * b:288 + 32 * b], krT[0:ROPE, t0:t0 + n], ident[0:ROPE, 0:ROPE])
        m.then_inc(mla_pe, 1)
        pe.wait_ge(mla_dve, 2)
        pe.wait_ge(kvN_copied, 1)
        pe.wait_ge(group_free, G_MIN + 4)
        for i in range(4):
            u = U_UQ + i
            pe.wait_ge(lo_done, u + 1)
            if i >= 2:
                pe.wait_ge(uq_free, i - 1)
            for o in range(4):
                for k in range(4):
                    cs = slice(512 * k + P * o, 512 * k + P * o + P)
                    m = mm3(ps[:, 4 * (i % 2) + o, 0:T], w_hi[:, u % SPLIT, cs], w_lo[:, u % SPLIT, cs],
                            cq_hi[:, k], cq_lo[:, k], k == 0, k == 3)
            m.then_inc(unit_used, 1)
        pe.wait_ge(att_ld, 48)
        pe.wait_ge(uq_free, 4)
        for j in range(HEADS // 2):
            if j >= 2:
                pe.wait_ge(mla_act, 2 + j - 1)
            for c in range(RC):
                m = nc.tensor.transpose(ps[:, 6 + j % 2, P * c:P * c + P], wuk[:, c, P * j:P * j + P], ident[:])
            m.then_inc(mla_pe, 1)
        pe.wait_ge(mla_act, 2 + 8)
        pe.wait_ge(qrt_ld, 16 * 16)
        pe.wait_ge(att_w, 16)
        pe.wait_ge(attc, 8)
        pe.wait_ge(mask_ready, 1)

        def qlat(h):
            r0 = NOPE * (h % 2)
            if h >= 1:
                pe.wait_ge(p_qc, h)
            for c in range(RC):
                m = nc.tensor.matmul(ps[:, c, 0:T], wukT[r0:r0 + NOPE, h // 2, P * c:P * c + P], qnT[r0:r0 + NOPE, h // 2],
                                     start=True, stop=True)
            m.then_inc(p_ql, 1)

        def scores(h):
            pe.wait_ge(p_qc, h + 1)
            if h >= 2:
                pe.wait_ge(p_sm, h - 1)
            bank, r0 = 2 + h % 2, 32 * (h % 4)
            for q0, n, c0 in ((0, P, 0), (P, 2 * P, P)):
                for c in range(RC):
                    nc.tensor.matmul(ps[:, bank, c0:c0 + n], ql[:, h % 2, c, q0:q0 + P], ckvT[:, c, 0:n], start=c == 0,
                                     stop=False, skip_group_check=True)
                m = nc.tensor.matmul(ps[:, bank, c0:c0 + n], qrT[r0:r0 + 32, h // 4, q0:q0 + P], krT[r0:r0 + 32, 0:n],
                                     start=False, stop=True, skip_group_check=True)
            m.then_inc(p_sc, 1)

        def turn(i, widths):
            pe.wait_ge(p_nm, i + 1)
            if i >= 1:
                pe.wait_ge(p_pt, i)
            for b, n in enumerate(widths):
                m = nc.tensor.transpose(ps[0:n, 5, P * b:P * b + P], sc[:, i % 2, P * b:P * b + n], ident[:])
            m.then_inc(p_tr, 1)

        def pv(i, parts, n_out):
            pe.wait_ge(p_pt, i + 1)
            if i >= 1:
                pe.wait_ge(p_ot, min(i, HEADS))
            if i > HEADS:
                pe.wait_ge(p_vc, i)
            for c in range(RC):
                for o0, terms in parts:
                    for t, (kb, nk, s0) in enumerate(terms):
                        m = nc.tensor.matmul(ps[:, 6, n_out * c + o0:n_out * c + o0 + P], ckvN[0:nk, kb, P * c:P * c + P],
                                             pT[0:nk, i % 2, s0:s0 + P], start=t == 0, stop=t == len(terms) - 1,
                                             skip_group_check=True)
            m.then_inc(p_pv, 1)

        def values(h):
            pe.wait_ge(p_ot, h + 1)
            if h >= 1:
                pe.wait_ge(p_vc, h)
            r0 = VH * (h % 2)
            for c in range(RC):
                m = nc.tensor.matmul(ps[r0:r0 + VH, 7, 0:2 * P], wuv[:, c, VH * h:VH * h + VH], oT[:, h % 2, c], start=c == 0, stop=c == RC - 1)
            m.then_inc(p_v, 1)

        PARTS = [(0, [(0, P, 0)]), (P, [(0, P, P), (1, P, 2 * P)])]
        qlat(0)
        for h in range(HEADS + 1):
            if h < HEADS:
                scores(h)
                if h + 1 < HEADS:
                    qlat(h + 1)
            if h >= 1:
                turn(h - 1, (P, P, P))
                pv(h - 1, PARTS, 2 * P)
                values(h - 1)
        for i in range(2):
            n = HEADS + i
            pe.wait_ge(p_sm, n - 1)
            bank = 2 + n % 2
            pe.wait_ge(tail_ready, i + 1)
            for c in range(RC):
                nc.tensor.matmul(ps[:, bank, 0:T_P], tailq[i][:, c], ckvT[:, c, 0:T_P], start=c == 0, stop=False)
            nc.tensor.matmul(ps[:, bank, 0:T_P], tailq[i][0:32, RC], krT[0:32, 0:T_P], start=False, stop=True).then_inc(p_sc, 1)
            turn(n, (P, P, QT))
            pv(n, [(0, [(0, P, 0), (1, P, P), (2, QT, 2 * P)])], P)
        pe.wait_ge(p_vc, HEADS + 2)

        NQ = HEADS * DEC_T
        with pe.Fori(0, DEC_B // 2) as it:
            for b in range(2):
                s = it * 2 + b
                pe.wait_ge(kv_ready[b], it * (32 * PAGES) + 32 * PAGES)
                pe.wait_ge(s_q, s + 1)

                def turn_keys(g):
                    if b * 4 + g >= 1:
                        pe.wait_ge(s_kt, s * 4 + g)
                        pe.wait_ge(s_kn, s * 4 + g)
                    for p in range(4):
                        for c in range(RC):
                            nc.tensor.transpose(ps[:, p // 2, 256 * (p % 2) + P * c:256 * (p % 2) + P * c + P],
                                                kvn[b][:, 4 * g + p, P * c:P * c + P], ident[:])
                    nc.tensor.transpose(ps[:, 2, 0:P], krn[b][:, 4 * g:4 * g + 4].rearrange("p a r -> p (a r)"), ident[:]
                                        ).then_inc(s_t, 1)

                def page_scores(g):
                    pe.wait_ge(s_kt, s * 4 + (g + 1))
                    pe.wait_ge(s_kn, s * 4 + (g + 1))
                    for p in range(4):
                        q0 = NQ * (4 * (g % 2) + p)
                        out = ps[:, 3 + g // 2, q0:q0 + NQ]
                        for c in range(RC):
                            nc.tensor.matmul(out, kt[:, g % 2, p, P * c:P * c + P], qs[:, c], start=c == 0, stop=False, skip_group_check=True)
                        m = nc.tensor.matmul(out, kr4[:, g % 2], qsr[:, p], start=False, stop=True, skip_group_check=True)
                    m.then_inc(s_sc, 1)

                turn_keys(0)
                out = ps[0:DEC_T, 5, 0:NQ]
                for c in range(RC):
                    nc.tensor.matmul(out, kn[:, c], qs[:, c], start=c == 0, stop=False, skip_group_check=True)
                nc.tensor.matmul(out, kn[:, RC], qsr[:, 0], start=False, stop=True, skip_group_check=True)
                for c in range(RC):
                    m = nc.tensor.transpose(ps[0:DEC_T, 5, 64 + P * c:64 + P * c + P], kn[:, c], ident[:])
                m.then_inc(s_new, 1)
                for g in range(4):
                    if g < 3:
                        turn_keys(g + 1)
                    page_scores(g)
                pe.wait_ge(s_mt, s + 1)
                nc.tensor.transpose(ps[:, 5, 320:448], mx[:], ident[:]).then_inc(s_dg, 1)
                pe.wait_ge(s_mb, s + 1)
                nc.tensor.matmul(ps[:, 5, 448:448 + NQ], ones[0:NQ], dg[0:NQ], start=True, stop=True, skip_group_check=True).then_inc(s_dg, 1)
                pe.wait_ge(s_ex, s + 1)
                pe.wait_ge(s_knN, s + 1)
                for c in range(RC):
                    for p in range(PAGES):
                        nc.tensor.matmul(ps[:, 6 + c, 0:NQ], kvn[b][:, p, P * c:P * c + P], ss[:, p], start=p == 0, stop=False)
                    nc.tensor.matmul(ps[:, 6 + c, 0:NQ], knN[0:DEC_T, P * c:P * c + P], sn[0:DEC_T], start=False, stop=True)
                pe.wait_ge(s_sum, s + 1)
                nc.tensor.matmul(ps[:, 5, 448:448 + NQ], ones[:], mx[:, 0:NQ], start=True, stop=True, skip_group_check=True).then_inc(s_pv, 1)
        pe.wait_ge(s_free, DEC_B)
        for h in range(HEADS):
            r0 = VH * (h % 2)
            bank, c0 = (h % 4) // 2 + 4 * (h % 2), TAIL * (h // 4)
            for c in range(RC):
                m = nc.tensor.matmul(ps[r0:r0 + VH, bank, c0:c0 + TAIL], wuv[:, c, VH * h:VH * h + VH], qlt[:, c, h],
                                     start=c == 0, stop=c == RC - 1, skip_group_check=True)
        m.then_inc(p_v, 1)
        pe.wait_ge(x_split, 4)
        for i in range(4):
            linear(U_MOUT + i, G_MOUT + i, 8, blocks, *X)
        pe.wait_ge(group_free, G_MOUT + 4)
        layer_norm(3)
        pe.wait_ge(ln_hi, 5)
        for i in range(6):
            b, hf = divmod(i, 2)
            t0, n = TB[b]
            if i >= 2:
                pe.wait_ge(xpose_free, 2 * DC + i - 1)
            for c in range(4):
                m = nc.tensor.transpose(ps[0:n, i % 2, P * c:P * c + P], xres[:, 4 * hf + c, t0:t0 + n], ident[:])
            m.then_inc(rt_pe, 1)
        pe.wait_ge(rt_w, 16)
        for b, (t0, n) in enumerate(TB):
            for c in range(DC):
                m = nc.tensor.matmul(ps[0:n, 2, NEXP * b:NEXP * b + NEXP], xres[:, c, t0:t0 + n], w_rt[:, c], start=c == 0, stop=c == DC - 1, skip_group_check=True)
        m.then_inc(rt_pe, 1)
        pe.wait_ge(rt_dve, 1)
        for b in range(4):
            o = ps[:, 4, NEXP * b:NEXP * b + NEXP] if b < 3 else ps[:, 4, 32:32 + NEXP]
            for a in range(min(b, 2) + 1 if b < 3 else 3):
                m = nc.tensor.matmul(o, before[:] if a == b else ones[:], selt[:, a], start=a == 0,
                                     stop=a == (b if b < 3 else 2), skip_group_check=True)
        m.then_inc(rt_pe, 1)

        pe.wait_ge(table_ready, 1)
        pe.wait_ge(xpose_free, 2 * DC + 6)
        n_jobs = pe.value_load(jobi[0:1, MAX_JOBS:MAX_JOBS + 1], min_val=NEXP, max_val=MAX_JOBS)

        def gather(part, job):
            if part == 0:
                pe.wait_ge(m_pick, job + 1)
            for c in range(4 * part, 4 * part + 4):
                for b, (t0, n) in enumerate(TB):
                    m = nc.tensor.matmul(ps[:, 7, P * (c % 4):P * (c % 4) + SLOTS], xt[0:n, b, P * c:P * c + P],
                                         pick[0:n, b], start=b == 0, stop=b == 2, skip_group_check=True)
            m.then_inc(m_g, 1)

        def scatter(i, j):
            b, q = divmod(i, 2)
            n = TB[b][1]
            if i >= 2:
                pe.wait_ge(m_acc, j * 6 + (i - 1))
            nc.tensor.matmul(ps[0:n, 6 + i % 2, :], pickT[:, b, 0:n], y_hi[:, 512 * q:512 * q + 512], start=True, stop=False)
            nc.tensor.matmul(ps[0:n, 6 + i % 2, :], pickT[:, b, 0:n], y_lo[:, 512 * q:512 * q + 512], start=False, stop=True
                             ).then_inc(m_sct, 1)

        gather(0, 0)
        pe.wait_ge(m_gc, 1)
        gather(1, 0)
        pe.wait_ge(m_gc, 2)
        pe.wait_ge(m_zero, 1)
        with pe.Fori(0, n_jobs) as j:
            pe.wait_ge(m_gl, j + 1)
            k = 0

            def unit(tok_hi, tok_lo, outs, first, last):
                nonlocal k
                u = U_MOE + k
                pe.wait_ge(lo_done, j * JOB_UNITS + (u + 1))
                for i in range(4):
                    bank, c = outs(i)
                    wh, wl = w_hi[:, u % SPLIT, 512 * i:512 * i + 512], w_lo[:, u % SPLIT, 512 * i:512 * i + 512]
                    nc.tensor.matmul(ps[:, bank, :], tok_hi[:, c], wh, start=first(i), stop=False, skip_group_check=True)
                    nc.tensor.matmul(ps[:, bank, :], tok_hi[:, c], wl, start=False, stop=False, skip_group_check=True)
                    m = nc.tensor.matmul(ps[:, bank, :], tok_lo[:, c], wh, start=False, stop=last(i), skip_group_check=True)
                m.then_inc(unit_used, 1)
                k += 1

            for s in range(STEPS + 1):
                if s < STEPS:
                    if s >= 2:
                        pe.wait_ge(m_h, j * STEPS + (s - 1))
                    for part in range(2):
                        unit(g_hi, g_lo, lambda i: (2 * (s % 2), 4 * part + i), lambda i: part == 0 and i == 0,
                             lambda i: part == 1 and i == 3)
                if s == 0:
                    pe.wait_ge(m_ylo, j + 1)
                    scatter(0, j)
                    scatter(1, j)
                if s == 1:
                    scatter(4, j)
                    scatter(5, j)
                    pe.wait_ge(m_acc, j * 6 + 6)
                if s >= 1:
                    pe.wait_ge(m_h, j * STEPS + s)
                    for c in range(4):
                        m = nc.tensor.transpose(ps[:, 6, P * c:P * c + P], hh[:, (s - 1) % 2, P * c:P * c + P], ident[:])
                    m.then_inc(m_hT, 1)
                if s < STEPS:
                    for part in range(2):
                        unit(g_hi, g_lo, lambda i: (2 * (s % 2) + 1, 4 * part + i), lambda i: part == 0 and i == 0,
                             lambda i: part == 1 and i == 3)
                if s == 0:
                    scatter(2, j)
                    scatter(3, j)
                if s == TURN_STEP:
                    for b in range(3):
                        m = nc.tensor.transpose(ps[:, 7, P * b:P * b + P], pick[:, b], ident[:])
                    m.then_inc(m_pickT, 1)
                if s == GATHER_STEPS[0]:
                    pe.wait_ge(m_pickTc, j + 1)
                    gather(0, j + 1)
                if s == GATHER_STEPS[1]:
                    pe.wait_ge(m_gc, j * 2 + 3)
                    gather(1, j + 1)
                if s >= 1:
                    pe.wait_ge(m_hTl, j * STEPS + s)
                    for part in range(2):
                        unit(hT_hi, hT_lo, lambda i: (4 + i % 2, 2 * part + i // 2), lambda i: s == 1 and part == 0 and i < 2,
                             lambda i: s == STEPS and part == 1 and i >= 2)
        pe.wait_ge(m_ylo, n_jobs + 1)
        pe.wait_ge(m_pickTc, n_jobs)
        for i in range(6):
            scatter(i, n_jobs)

    ctx.close()


CONST_LOADS = 8 + 1 + DC + 6
STORES = 1 + 8 + 4
_INS = ['x_prompt', 'x_sample', 'state_conv', 'cache_ckv', 'cache_krope', 'page_table', 'meta_tokens',
        'conv_w_in', 'conv_b_in', 'conv_w_dw', 'conv_b_dw', 'conv_ln_g', 'conv_ln_b', 'conv_w_out',
        'mla_w_in', 'mla_g_q', 'mla_g_kv', 'mla_w_uq', 'mla_w_uk', 'mla_w_uv', 'mla_w_out',
        'ffn_w_gu', 'ffn_w_down', 'moe_w_router', 'moe_w_gu', 'moe_w_down', 'ln_g', 'ln_b']
_OUTS = [(1, SEQ, D), (DEC_B, DEC_T, D), (1, 1, HIST, D), (1, DEC_B, HIST, D), (1, 1, T_P, LORA), (1, 1, T_P, ROPE),
         (1, DEC_B, DEC_T, LORA), (1, DEC_B, DEC_T, ROPE)]


def kernel(**inputs):
    import concourse.bacc as bacc
    from concourse.bass_utils import run_bass_kernel_spmd

    nc = bacc.Bacc("TRN2", target_bir_lowering=False, num_devices=1)
    arrays, args = {}, []
    cos_t, sin_t = rope_tables()
    for name, a in [(n, np.ascontiguousarray(inputs[n])) for n in _INS] + [("cos_t", cos_t), ("sin_t", sin_t)]:
        arrays["in_" + name] = a
        args.append(nc.dram_tensor("in_" + name, a.shape, mybir.dt.from_np(a.dtype), kind="ExternalInput").ap())
    for i, shape in enumerate(_OUTS):
        args.append(nc.dram_tensor(f"out_{i}", shape, F32, kind="ExternalOutput").ap())
    build(nc, *args)
    r = run_bass_kernel_spmd(nc, [arrays], core_ids=[0])
    return tuple(r.results[0][f"out_{i}"] for i in range(len(_OUTS)))
```

```python
from contextlib import ExitStack

import numpy as np
import concourse.bass as bass
from concourse import mybir

F32 = mybir.dt.float32
F32R = mybir.dt.float32r
I32 = mybir.dt.int32
ALU = mybir.AluOpType
ACT = mybir.ActivationFunctionType
AX = mybir.AxisListType.X

P = 128
D = 1024
DC = D // P
SEQ, N_META, DEC_B, DEC_T = 256, 16, 8, 4
T_P = SEQ + N_META
T_S = DEC_B * DEC_T
T = T_P + T_S
PAST, PAGE = 2048, 128
PAGES = PAST // PAGE
TAPS = 31
HIST = TAPS - 1
HEADS, NOPE, ROPE, VH = 16, 64, 32, 64
LORA, QLORA = 256, 512
RC = LORA // P
FF = 2816
FC = FF // P
NEXP, DEXP = 8, 3584
DEPTH = 2
ALPHA = (2.0 * DEPTH) ** 0.25
SM_SCALE = (NOPE + ROPE) ** -0.5
LN_EPS, RMS_EPS = 1e-5, 1e-6
NEG = -1e30
TB = [(0, P), (P, P), (2 * P, T - 2 * P)]
TAIL0 = 2 * P
TAIL = T - TAIL0
QT = T_P - TAIL0
PE_TAPS = 15
DIAGS = 20
SLOTS = P
MAX_JOBS = 12
STEPS = DEXP // 512
JOB_UNITS = 6 * STEPS

RAW, SPLIT = 6, 3
UNIT = 2048
AHEAD = 2

U_CIN, U_COUT = 0, 8
U_GU = U_COUT + 4
U_DOWN = U_GU + FC
U_MIN = U_DOWN + 12
U_UQ = U_MIN + 4
U_MOUT = U_UQ + 4
U_MOE = U_MOUT + 4
G_CIN, G_COUT, G_GU = 0, 8, 12
G_DOWN = G_GU + FC
G_MIN = G_DOWN + 4
G_MOUT = G_MIN + 4
assert U_MOE % 6 == 4 and MAX_JOBS * SLOTS > 2 * T


def rope_tables():
    half = ROPE // 2
    freqs = (np.float32(10000.0) ** (-np.arange(half, dtype=np.float32) / np.float32(half))).astype(np.float32)
    pos = np.concatenate([np.arange(T_P), np.tile(PAST + np.arange(DEC_T), DEC_B)]).astype(np.float32)
    ang = (pos[None, :] * freqs[:, None]).astype(np.float32)
    cos, sin = np.cos(ang), np.sin(ang)
    return (np.tile(np.concatenate([cos, cos], 0), (4, 1)).astype(np.float32),
            np.tile(np.concatenate([-sin, sin], 0), (4, 1)).astype(np.float32))


def build(nc, x_prompt, x_sample, state_conv, cache_ckv, cache_krope, page_table, meta_tokens,
          conv_w_in, conv_b_in, conv_w_dw, conv_b_dw, conv_ln_g, conv_ln_b, conv_w_out,
          mla_w_in, mla_g_q, mla_g_kv, mla_w_uq, mla_w_uk, mla_w_uv, mla_w_out,
          ffn_w_gu, ffn_w_down, moe_w_router, moe_w_gu, moe_w_down, ln_g, ln_b, cos_t, sin_t,
          y_prompt, y_sample, new_conv_p, new_conv_s, new_ckv_p, new_kr_p, new_ckv_s, new_kr_s):
    ctx = ExitStack()
    ctx.enter_context(ctx_ok := nc.allow_non_contiguous_dma(reason="small vectors are laid out feature-major"))
    base = -(-nc.sbuf_base // 64) * 64
    limit = nc.sbuf_usable_end

    def place(name, off, shape, dt=F32):
        size = int(np.prod(shape[1:])) * 4
        assert base + off + size <= limit, (name, off, size)
        return nc.alloc_sbuf_tensor_at(name, shape, dt, offset=base + off)

    def sem(name):
        return ctx.enter_context(nc.semaphore(name))

    class Region:
        def __init__(self, start, end):
            self.at, self.end = start, end

        def __call__(self, name, shape, dt=F32):
            t = place(name, self.at, shape, dt)
            self.at += int(np.prod(shape[1:])) * 4
            self.at = -(-self.at // 32) * 32
            assert self.at <= self.end, (name, self.at, self.end)
            return t

    KB = 1024
    ACTV = T * DC * 4
    raw = place("raw", 0, [P, RAW, UNIT])
    w_hi = place("w_hi", 48 * KB, [P, SPLIT, UNIT], F32R)
    w_lo = place("w_lo", 72 * KB, [P, SPLIT, UNIT], F32R)
    A0 = 96 * KB
    xres = place("xres", A0, [P, DC, T])
    x_hi = place("x_hi", A0 + ACTV, [P, DC, T], F32R)
    x_lo = place("x_lo", A0 + 2 * ACTV, [P, DC, T], F32R)
    work = place("work", A0 + 3 * ACTV, [P, DC, T])
    sq = place("sq", A0 + 4 * ACTV, [P, DC, T])
    Z0 = A0 + 5 * ACTV
    LIM = limit - base
    cst = Region(Z0, LIM)
    ident = cst("ident", [P, P])
    ones = cst("ones", [P, P])
    before = cst("before", [P, P])
    rstd = cst("rstd", [P, T])
    lng = cst("lng", [P, 4, DC])
    lnb = cst("lnb", [P, 4, DC])
    b_in = cst("b_in", [P, 2 * DC])
    w_dw = cst("w_dw", [P, TAPS, DC])
    b_dw = cst("b_dw", [P, DC])
    cg = cst("cg", [P, DC])
    cb = cst("cb", [P, DC])
    g_q = cst("g_q", [P, QLORA // P])
    g_kv = cst("g_kv", [P, RC])
    eps = cst("eps", [P, 2])
    row_i = cst("row_i", [P, 1], I32)
    pages = cst("pages", [1, DEC_B * PAGES], I32)
    Z = cst.at
    cv = Region(Z, LIM)
    gate = cv("gate", [P, 2, T])
    htmp = cv("htmp", [P, 2, T])
    gu_end = cv.at
    u_p = cv("u_p", [P, DC, HIST + T_P])
    u_s = cv("u_s", [P, DC, DEC_B, HIST + DEC_T])
    xtok = cv("xtok", [P, 3, D])
    hist = cv("hist", [P, 2, D])
    u_new = cv("u_new", [P, DC, T_S])
    edge = xtok
    diag = cv("diag", [P, DIAGS, P])
    tap_rows = diag[0:TAPS].rearrange("p a b -> p (a b)")[:, 0:D]
    ff = Region(gu_end, LIM)
    h_hi = ff("h_hi", [P, FC, T], F32R)
    h_lo = ff("h_lo", [P, FC, T], F32R)
    at_ = Region(Z, LIM)
    cosT = at_("cosT", [P, T])
    sinT = at_("sinT", [P, T])
    causal = at_("causal", [P, 3 * P])
    causal_t_at = at_.at
    causal_t = at_("causal_t", [P, QT])
    causal_s = at_("causal_s", [P, HEADS, DEC_T])
    ckvT = at_("ckvT", [P, RC, T])
    ckvN = at_("ckvN", [P, 3, LORA])
    krT = at_("krT", [P, T])
    krN = at_("krN", [P, 3, ROPE])
    qnT = at_("qnT", [P, HEADS // 2, T])
    qrT_at = at_.at
    qrT = at_("qrT", [P, HEADS // 4, T])
    wukT_at = at_.at
    wukT = at_("wukT", [P, HEADS // 2, LORA])
    cq_at = at_.at
    wuv = at_("wuv", [P, RC, HEADS * VH])
    qlt = at_("qlt", [P, RC, HEADS, TAIL])
    qrt = at_("qrt", [P, HEADS, TAIL])
    kt = at_("kt", [P, 2, 4, LORA])
    key_f = at_("key_f", [P, QT])
    row_f = at_("row_f", [P, 1])
    tailq = [kt[:, 1, 2 * i:2 * i + 2].rearrange("p a (b n) -> p (a b) n", b=2)[:, 0:RC + 1] for i in range(2)]
    cq = Region(cq_at, LIM)
    cq_f = cq("cq_f", [P, 4, T])
    cq_hi = cq("cq_hi", [P, 4, T], F32R)
    cq_lo = cq("cq_lo", [P, 4, T], F32R)
    rms_kv = place("rms_kv", A0 + 3 * ACTV + 8 * KB, [P, T])[:]
    wuk = kt[:].rearrange("p a b r -> p (a b r)").rearrange("p (c n) -> p c n", c=RC)
    pa = Region(A0 + 3 * ACTV, Z0)
    ql = pa("ql", [P, 2, RC, T])
    sc = pa("sc", [P, 2, 3 * P])
    pT = pa("pT", [P, 2, 3 * P])
    oT = pa("oT", [P, 2, RC, 2 * P])
    pst = pa("pst", [P, 2, 8])
    kvn = [place("kvn0", A0 + ACTV, [P, PAGES, LORA]), place("kvn1", A0 + 3 * ACTV, [P, PAGES, LORA])]
    krn = [place("krn0", A0 + ACTV + PAGES * LORA * 4, [P, PAGES, ROPE]),
           place("krn1", A0 + 3 * ACTV + PAGES * LORA * 4, [P, PAGES, ROPE])]
    NQ = HEADS * DEC_T
    sa = Region(wukT_at, cq_at)
    sb_ = Region(qrT_at, wukT_at)
    sc_ = Region(Z, causal_t_at)
    ss = [sa("ss0", [P, PAGES, NQ]), sb_("ss1", [P, PAGES, NQ])]
    kr4 = sa("kr4", [P, 2, P])
    qs = [sa("qs0", [P, RC, NQ]), sc_("qs1", [P, RC, NQ])]
    qsr = [sa("qsr0", [P, 4, NQ]), sc_("qsr1", [P, 4, NQ])]
    kn = [sa("kn0", [P, RC + 1, DEC_T]), sc_("kn1", [P, RC + 1, DEC_T])]
    knN = [rstd[:, 0:LORA], sc_("knN1", [P, LORA])]
    sn = [sa("sn0", [P, NQ]), sc_("sn1", [P, NQ])]
    mx = [sa("mx0", [P, 2 * NQ]), sc_("mx1", [P, 2 * NQ])]
    dg = [sa("dg0", [P, NQ]), sc_("dg1", [P, NQ])]
    m1 = [sa("m10", [P, 1]), sc_("m11", [P, 1])]
    mo = Region(Z, LIM)
    xt = mo("xt", [P, 3, D])
    g_next = mo("g_next", [P, DC, SLOTS])
    acc = mo("acc", [P, 3, D])
    pick = mo("pick", [P, 3, P])
    pickT = mo("pickT", [P, 3, P], F32R)
    iota = mo("iota", [P, P])
    w_rt = mo("w_rt", [P, DC, NEXP])
    lt8 = mo("lt8", [P, NEXP, NEXP])
    cmp_ = mo("cmp_", [P, MAX_JOBS, NEXP])
    cmp2 = mo("cmp2", [P, NEXP, NEXP])
    gt8 = mo("gt8", [P, 3, NEXP, NEXP])
    eq8 = mo("eq8", [P, 3, NEXP, NEXP])
    lg = mo("lg", [P, 3, NEXP])
    rank = mo("rank", [P, 3, NEXP])
    oneA = mo("oneA", [P, 3, NEXP])
    oneB = mo("oneB", [P, 3, NEXP])
    valid = mo("valid", [P, 3, NEXP])
    selt = mo("selt", [P, 3, NEXP])
    keyt = mo("keyt", [P, 3, NEXP])
    jobs = mo("jobs", [P, 2, NEXP])
    starts = mo("starts", [P, NEXP])
    tk = mo("tk", [P, 12, 3])
    jobf = mo("jobf", [P, MAX_JOBS + 1])
    jobi = mo("jobi", [P, MAX_JOBS + 1], I32)
    me = Region(A0 + ACTV, Z0)
    g_hi = me("g_hi", [P, DC, SLOTS], F32R)
    g_lo = me("g_lo", [P, DC, SLOTS], F32R)
    sg = me("sg", [P, 2, 512])
    hh = me("hh", [P, 2, 512])
    hT_hi = me("hT_hi", [P, 4, SLOTS], F32R)
    hT_lo = me("hT_lo", [P, 4, SLOTS], F32R)
    y_hi = me("y_hi", [P, D], F32R)
    y_lo = me("y_lo", [P, D], F32R)
    gbc = me("gbc", [P, D])
    bbc = me("bbc", [P, D])
    sqt = place("sqt", A0, [P, D])
    stat = place("stat", A0 + 4 * KB, [P, 3, 4])

    ps = ctx.enter_context(nc.psum_tensor("ps", [P, 8, 512], F32))

    const_ld = sem("const_ld")
    x_ld = sem("x_ld")
    hist_ld = sem("hist_ld")
    consts_made = sem("consts_made")
    raw_ready = [sem(f"raw_ready{i}") for i in range(RAW)]
    hi_done = sem("hi_done")
    lo_done = sem("lo_done")
    unit_used = sem("unit_used")
    group_free = sem("group_free")
    gate_ready = sem("gate_ready")
    xpose = sem("xpose")
    xpose_free = sem("xpose_free")
    xin_raw = sem("xin_raw")
    act_own = sem("act_own")
    dve = sem("dve")
    ln_in = sem("ln_in")
    ln_mean = sem("ln_mean")
    ln_cent = sem("ln_cent")
    ln_sq = sem("ln_sq")
    ln_var = sem("ln_var")
    ln_std = sem("ln_std")
    rms_rt = sem("rms_rt")
    ln_scaled = sem("ln_scaled")
    ln_hi = sem("ln_hi")
    x_split = sem("x_split")
    h_split = sem("h_split")
    uq_free = sem("uq_free")
    att_ld = sem("att_ld")
    att_w = sem("att_w")
    attc = sem("attc")
    wuk_ld = sem("wuk_ld")
    tap_ld = sem("tap_ld")
    taps_turned = sem("taps_turned")
    taps_ready = sem("taps_ready")
    cq_hi_done = sem("cq_hi_done")
    cq_lo_done = sem("cq_lo_done")
    edge_ready = sem("edge_ready")
    diag_ready = sem("diag_ready")
    diag_used = sem("diag_used")
    edge_copied = sem("edge_copied")
    edge_out = sem("edge_out")
    kvN_copied = sem("kvN_copied")
    rt_w = sem("rt_w")
    tail_ready = sem("tail_ready")
    qrt_ld = sem("qrt_ld")
    stores = sem("stores")
    mla_pe = sem("mla_pe")
    mla_dve = sem("mla_dve")
    mla_act = sem("mla_act")
    p_ql, p_qc, p_sc, p_sm, p_ex, p_nm, p_tr, p_pt, p_pv, p_ot, p_v, p_vc = [
        sem("pa_" + n) for n in ("qlat", "qcopied", "scores", "shifted", "exp", "normed", "transposed", "ptcopied",
                                 "pv", "otcopied", "v", "vcopied")]
    kv_ready = [[sem(f"kv_ready{b}_{g}") for g in range(4)] for b in range(2)]
    kr_ready = [[sem(f"kr_ready{b}_{g}") for g in range(4)] for b in range(2)]
    s_q, s_t, s_kt, s_sc, s_mt, s_dg, s_mb, s_sh, s_ex, s_sum, s_st, s_pv, s_free, s_kn = [
        sem("sa_" + n) for n in ("q_copied", "k_transposed", "kt_copied", "scores", "max_t", "diag", "max_bc",
                                 "shifted", "exp", "summed", "sum_bc", "pv", "seq_done", "kr_copied")]
    v_ready = sem("v_ready")
    rt_pe = sem("rt_pe")
    rt_dve = sem("rt_dve")
    rt_logits = sem("rt_logits")
    rt_act = sem("rt_act")
    rt_const = sem("rt_const")
    table_ready = sem("table_ready")
    m_zero, m_gh, m_pick, m_pickT, m_pickTc, m_g, m_gc, m_gl, m_sg, m_h, m_hT, m_hTc, m_hTl, m_yhi, m_ylo, m_sct, m_acc, m_own = [
        sem("mo_" + n) for n in ("zeroed", "next_hi", "picked", "pick_t", "pick_copied", "gathered", "g_hi", "g_lo", "silu", "h", "h_t",
                                 "hT_hi", "hT_lo", "y_hi", "y_lo", "scattered", "added", "own")]
    fin_v = sem("fin_v")
    fin_a = sem("fin_a")
    fin_sq = sem("fin_sq")
    fin_ld = sem("fin_ld")

    def km(w, c0, n):
        return w.rearrange("(c p) n -> p c n", p=P)[:, :, c0:c0 + n]

    w_in, w_o = conv_w_in[0], conv_w_out[0]
    f_gu, f_dn = ffn_w_gu[0], ffn_w_down[0]
    m_in = mla_w_in[0]
    m_uq = mla_w_uq[0].rearrange("(c p) h d -> p c (h d)", p=P)
    m_out = mla_w_out[0].rearrange("h v n -> (h v) n")
    e_gu = moe_w_gu[0].rearrange("e (c p) n -> e p c n", p=P)
    e_dn = moe_w_down[0].rearrange("e (c p) n -> e p c n", p=P)

    def slot(u, n):
        return raw[:, u % RAW, 0:n]

    def pair_unit(u, w, m, second):
        v = slot(u, UNIT).rearrange("p (c a n) -> p c a n", c=8, a=2)
        return [(v[:, :, 0, :], km(w, m, P)), (v[:, :, 1, :], km(w, second + m, P))]

    def block_unit(u, w, kc0, nk, c0, n=256):
        v = slot(u, nk * n).rearrange("p (c n) -> p c n", c=nk)
        src = km(w, c0, n)[:, kc0:kc0 + nk, :]
        return [(v[:, 0:nk // 2], src[:, 0:nk // 2]), (v[:, nk // 2:nk], src[:, nk // 2:nk])]

    SIZE = {}
    DOWN_KC = [(0, 8), (8, 8), (16, FC - 16)]

    def unit_loads(u):
        if u < U_COUT:
            return pair_unit(u, w_in, P * u, D)
        if u < U_GU:
            return block_unit(u, w_o, 0, 8, 256 * (u - U_COUT))
        if u < U_DOWN:
            return pair_unit(u, f_gu, P * (u - U_GU), FF)
        if u < U_MIN:
            i, k = divmod(u - U_DOWN, 3)
            SIZE[u] = DOWN_KC[k][1] * 256
            return block_unit(u, f_dn, *DOWN_KC[k], 256 * i)
        if u < U_UQ:
            i = u - U_MIN
            if i == 3:
                SIZE[u] = 8 * ROPE
                return block_unit(u, m_in, 0, 8, 768, ROPE)
            return block_unit(u, m_in, 0, 8, 256 * i)
        if u < U_MOUT:
            i = u - U_UQ
            v = slot(u, 4 * 384).rearrange("p (c n) -> p c n", c=4)
            s = m_uq[:, :, 384 * i:384 * (i + 1)]
            return [(v[:, 0:2], s[:, 0:2]), (v[:, 2:4], s[:, 2:4])]
        return block_unit(u, m_out, 0, 8, 256 * (u - U_MOUT))

    for u in range(U_MOE):
        unit_loads(u)

    def raw_target(u):
        return 32 * (u // RAW + 1)

    def moe_slot_base(s):
        return 32 * len([u for u in range(U_MOE) if u % RAW == s])

    def moe_raw_target(k, j):
        u = U_MOE + k
        first = (u % RAW - U_MOE) % RAW
        return moe_slot_base(u % RAW) + 16 * ((k - first) // RAW + 1) + j * (16 * JOB_UNITS // RAW)

    TURN_STEP, GATHER_STEPS = 2, (4, 5)

    def first_unit(s):
        return 0 if s == 0 else 4 + 6 * (s - 1)

    ROPE_U = U_MIN + 3

    def split_copies(u, out, src):
        if u == ROPE_U:
            o = out[:, 0:UNIT].rearrange("p (c a r b n) -> p c a r b n", c=8, a=2, r=4, b=2)
            s = src[:, 0:8 * ROPE].rearrange("p (c b n) -> p c b n", c=8, b=2)
            return ([(o[:, :, 0, r].rearrange("p c b n -> p c (b n)"), s.rearrange("p c b n -> p c (b n)"))
                     for r in range(4)] + [(o[:, :, 1, r, b], s[:, :, 1 - b]) for r in range(4) for b in range(2)])
        if U_UQ <= u < U_MOUT:
            o = out[:, 0:UNIT].rearrange("p (c n) -> p c n", c=4)
            s = src[:, 0:4 * 384].rearrange("p (c h d) -> p c h d", c=4, h=4)
            res = []
            for c in range(4):
                res.append((o[:, c, 0:256].rearrange("p (h d) -> p h d", h=4), s[:, c, :, 0:NOPE]))
                res.append((o[:, c, 256:384].rearrange("p (h d) -> p h d", h=4), s[:, c, :, NOPE:NOPE + ROPE]))
                sw = o[:, c, 384:512].rearrange("p (h b d) -> p h b d", h=4, b=2)
                for b in range(2):
                    res.append((sw[:, :, b, :], s[:, c, :, NOPE + 16 * (1 - b):NOPE + 16 * (2 - b)]))
            return res
        n = SIZE.get(u, UNIT)
        return [(out[:, 0:n], src[:, 0:n])]

    block = ctx.enter_context(nc.Block())

    WUK_BANKS = [2 * ((G_MIN + q) % 3) + o for q in (1, 2) for o in range(2)]

    ROW_BANKS = (7, 0, 1, 3, 5, 6)
    LOGIT_BANKS = (2, 4, 6)

    def page_of(engine, s, p):
        at = slice(s * PAGES + p, s * PAGES + p + 1) if isinstance(s, int) else bass.ds(s * PAGES + p, 1)
        return engine.value_load(pages[0:1, at], min_val=0, max_val=cache_ckv.shape[1] - 1)

    @block.sync
    def _(sp):
        xt = [(xtok[0:N_META, 0], meta_tokens), (xtok[N_META:P, 0], x_prompt[0, 0:P - N_META]),
              (xtok[:, 1], x_prompt[0, P - N_META:2 * P - N_META]),
              (xtok[0:QT, 2], x_prompt[0, 2 * P - N_META:SEQ]),
              (xtok[QT:TAIL, 2], x_sample.rearrange("b t d -> (b t) d"))]
        for o, i in xt:
            sp.dma_start(o, i).then_inc(x_ld, 16)
        half = HIST * 4
        for b in range(2):
            sp.dma_start(hist[0:half, b], state_conv[0, 4 * b:4 * b + 4].rearrange("s t d -> (s t) d")).then_inc(hist_ld, 16)

        def load(u):
            if u >= RAW:
                sp.wait_ge(lo_done, u - RAW + 1)
            for o, i in unit_loads(u):
                sp.dma_start(o, i).then_inc(raw_ready[u % RAW], 16)

        for u in range(U_GU):
            load(u)
        gu_v = f_gu.rearrange("(c p) (a j n) -> p c a j n", p=P, a=2, n=P)
        with sp.Fori(0, 3) as it:
            for r in range(6):
                u = U_GU + r
                sp.wait_ge(lo_done, it * 6 + (u - RAW + 1))
                v = slot(u, UNIT).rearrange("p (c a n) -> p c a n", c=8, a=2)
                for a in range(2):
                    sp.dma_start(v[:, :, a, :], gu_v[:, :, a, bass.ds(it * 6 + r, 1), :].rearrange("p c j n -> p c (j n)")
                                 ).then_inc(raw_ready[u % RAW], 16)
        for u in range(U_GU + 18, U_MOE):
            load(u)

        def page_numbers(s):
            return [page_of(sp, s, p) for p in range(PAGES)]

        def fetch(numbers, b):
            for p, pg in enumerate(numbers):
                sp.dma_start(kvn[b][:, p, :], cache_ckv[0, bass.ds(pg, 1)].rearrange("a k r -> k (a r)")
                             ).then_inc(kv_ready[b][p // 4], 16)

        sp.wait_ge(const_ld, CONST_LOADS * 16)
        numbers = page_numbers(0)
        sp.wait_ge(unit_used, U_MOUT)
        sp.dma_start(wuv[:], mla_w_uv[0].rearrange("(c p) h v -> p c (h v)", p=P)).then_inc(att_w, 16)
        sp.wait_ge(uq_free, 4)
        for r in range(4):
            for hh_ in range(4):
                sp.dma_start(qrt[32 * r:32 * r + 32, hh_:HEADS:4, :], qrT[32 * hh_:32 * hh_ + 32, :, TAIL0:T]
                             ).then_inc(qrt_ld, 16)
        fetch(numbers, 0)
        numbers = page_numbers(1)
        sp.wait_ge(p_vc, HEADS + 2)
        fetch(numbers, 1)
        with sp.Fori(1, DEC_B // 2) as it:
            for b in range(2):
                numbers = page_numbers(it * 2 + b)
                sp.wait_ge(s_pv, it * 2 + (b - 1))
                fetch(numbers, b)

        def job(e_gate, e_down, j):
            k = 0
            for s in range(STEPS + 1):
                todo = []
                if s < STEPS:
                    todo += [(e_gate, 0, s), (e_gate, 1, s), (e_gate, 2, s), (e_gate, 3, s)]
                if s >= 1:
                    todo += [(e_down, 0, s - 1), (e_down, 1, s - 1)]
                for src, part, st in todo:
                    u = U_MOE + k
                    sp.wait_ge(lo_done, j * JOB_UNITS + (u - RAW + 1))
                    sp.dma_start(slot(u, UNIT).rearrange("p (c n) -> p c n", c=4 if src is e_gate else 2),
                                 src(part, st)).then_inc(raw_ready[u % RAW], 16)
                    k += 1
            assert k == JOB_UNITS

        def gate_src(e):
            def src(part, st):
                c0 = 512 * st + (DEXP if part >= 2 else 0)
                v = e_gu[e] if isinstance(e, int) else e_gu[bass.ds(e, 1)].rearrange("e p c n -> p (e c) n")
                return v[:, 4 * (part % 2):4 * (part % 2) + 4, c0:c0 + 512]
            return src

        def down_src(e):
            def src(part, st):
                v = e_dn[e] if isinstance(e, int) else e_dn[bass.ds(e, 1)].rearrange("e p c n -> p (e c) n")
                return v[:, 4 * st + 2 * part:4 * st + 2 * part + 2, :]
            return src

        job(gate_src(0), down_src(0), 0)
        sp.wait_ge(table_ready, 1)
        n_jobs = sp.value_load(jobi[0:1, MAX_JOBS:MAX_JOBS + 1], min_val=NEXP, max_val=MAX_JOBS)
        with sp.Fori(1, n_jobs) as j:
            e = sp.value_load(jobi[0:1, bass.ds(j, 1)], min_val=0, max_val=NEXP - 1)
            job(gate_src(e), down_src(e), j)

    @block.gpsimd
    def _(pool):
        nc.gpsimd.memset(ident[:], 1.0).then_inc(consts_made, 1)
        nc.gpsimd.memset(ones[:], 1.0).then_inc(consts_made, 1)
        nc.gpsimd.memset(before[:], 1.0).then_inc(consts_made, 1)
        nc.gpsimd.memset(u_p[:, :, 0:HIST], 0.0).then_inc(consts_made, 1)
        nc.gpsimd.memset(eps[:, 0:1], LN_EPS).then_inc(consts_made, 1)
        nc.gpsimd.memset(eps[:, 1:2], RMS_EPS).then_inc(consts_made, 1)
        pool.wait_ge(consts_made, 6)
        nc.gpsimd.affine_select(out=ident[:], in_=ident[:], compare_op=ALU.is_equal, fill=0.0, base=0,
                                pattern=[[-1, P]], channel_multiplier=1).then_inc(consts_made, 1)
        nc.gpsimd.affine_select(out=before[:], in_=before[:], compare_op=ALU.is_gt, fill=0.0, base=0,
                                pattern=[[1, P]], channel_multiplier=-1).then_inc(consts_made, 1)
        pool.wait_ge(consts_made, 8)
        pool.wait_ge(taps_ready, 1)
        for q in range(DC * PE_TAPS):
            m, t = divmod(q, PE_TAPS)
            if q >= DIAGS:
                pool.wait_ge(diag_used, q - DIAGS + 1)
            nc.gpsimd.tensor_scalar(diag[:, q % DIAGS], ident[:], w_dw[:, t, m:m + 1], 1.0, ALU.mult, ALU.mult
                                    ).then_inc(diag_ready, 1)
        pool.wait_ge(unit_used, U_MIN)
        nc.gpsimd.memset(causal[:], 0.0).then_inc(attc, 1)
        nc.gpsimd.memset(causal_t[:], 0.0).then_inc(attc, 1)
        nc.gpsimd.memset(causal_s[:], 0.0).then_inc(attc, 1)
        pool.wait_ge(attc, 3)
        for b in (0, 2):
            c = causal[:, P * b:P * b + P]
            nc.gpsimd.affine_select(out=c, in_=c, compare_op=ALU.is_ge, fill=NEG, base=0,
                                    pattern=[[-1, P]], channel_multiplier=1).then_inc(attc, 1)
        nc.gpsimd.iota(row_i[:], pattern=[[0, 1]], base=0, channel_multiplier=1).then_inc(attc, 1)
        nc.gpsimd.iota(key_f[:], pattern=[[1, QT]], base=0, channel_multiplier=0,
                       allow_small_or_imprecise_dtypes=True).then_inc(attc, 1)
        nc.gpsimd.affine_select(out=causal_s[:], in_=causal_s[:], compare_op=ALU.is_ge, fill=NEG, base=0,
                                pattern=[[0, HEADS], [1, DEC_T]], channel_multiplier=-1).then_inc(attc, 1)

        def fetch(s, b):
            for p in range(PAGES):
                pg = page_of(pool, s, p)
                pool.dma_start(krn[b][:, p, :], cache_krope[0, bass.ds(pg, 1)].rearrange("a k r -> k (a r)")
                               ).then_inc(kr_ready[b][p // 4], 16)

        pool.wait_ge(const_ld, CONST_LOADS * 16)
        pool.wait_ge(unit_used, U_MOUT)
        fetch(0, 0)
        pool.wait_ge(p_vc, HEADS + 2)
        fetch(1, 1)
        with pool.Fori(1, DEC_B // 2) as it:
            for b in range(2):
                pool.wait_ge(s_t, it * 8 + (4 * b - 4))
                fetch(it * 2 + b, b)

        pool.wait_ge(x_split, DC * 4)
        pool.wait_ge(stores, 9 * 16)
        pool.dma_start(w_rt[:], moe_w_router[0].rearrange("(c p) e -> p c e", p=P)).then_inc(rt_w, 16)
        nc.gpsimd.iota(iota[:], pattern=[[1, P]], base=0, channel_multiplier=0,
                       allow_small_or_imprecise_dtypes=True).then_inc(rt_const, 1)
        nc.gpsimd.memset(lt8[:], 1.0).then_inc(rt_const, 1)
        nc.gpsimd.memset(valid[:], 0.0).then_inc(rt_const, 1)
        nc.gpsimd.memset(lg[:], 0.0).then_inc(rt_const, 1)
        nc.gpsimd.iota(jobf[:], pattern=[[1, MAX_JOBS + 1]], base=0, channel_multiplier=0,
                       allow_small_or_imprecise_dtypes=True).then_inc(rt_const, 1)
        pool.wait_ge(rt_const, 5)
        nc.gpsimd.affine_select(out=lt8[:], in_=lt8[:], compare_op=ALU.is_gt, fill=0.0, base=0,
                                pattern=[[1, NEXP], [-1, NEXP]], channel_multiplier=0).then_inc(rt_const, 1)
        nc.gpsimd.memset(valid[:, 0:2], 1.0).then_inc(rt_const, 1)
        nc.gpsimd.memset(valid[0:TAIL, 2], 1.0).then_inc(rt_const, 1)

    @block.scalar
    def _(act):
        own = [0]

        def chain(ins):
            own[0] += 1
            ins.then_inc(act_own, 1)
            act.wait_ge(act_own, own[0])

        act.dma_start(b_in[:], conv_b_in[0].rearrange("(c p) -> p c", p=P)).then_inc(const_ld, 16)
        act.dma_start(tap_rows, conv_w_dw[0]).then_inc(tap_ld, 16)
        for src, dst in ((ln_g, lng), (ln_b, lnb)):
            act.dma_start(dst[:].rearrange("p a c -> p (a c)"), src.rearrange("a b (c p) -> p (a b c)", p=P)).then_inc(const_ld, 16)
        act.dma_start(b_dw[:], conv_b_dw[0].rearrange("(c p) -> p c", p=P)).then_inc(const_ld, 16)
        act.dma_start(cg[:], conv_ln_g[0].rearrange("(c p) -> p c", p=P)).then_inc(const_ld, 16)
        act.dma_start(cb[:], conv_ln_b[0].rearrange("(c p) -> p c", p=P)).then_inc(const_ld, 16)
        act.dma_start(g_q[:], mla_g_q[0].rearrange("(c p) -> p c", p=P)).then_inc(const_ld, 16)
        act.dma_start(g_kv[:], mla_g_kv[0].rearrange("(c p) -> p c", p=P)).then_inc(const_ld, 16)
        act.dma_start(pages[:], page_table.rearrange("(o b) n -> o (b n)", o=1)).then_inc(const_ld, 16)

        def split(u, it=None):
            if u >= U_MOE:
                return
            extra = 0 if it is None else it * 6
            act.wait_ge(raw_ready[u % RAW], raw_target(u) + (0 if it is None else it * 32))
            if u >= SPLIT:
                act.wait_ge(unit_used, extra + (u - SPLIT + 1))
            todo = split_copies(u, w_hi[:, u % SPLIT], raw[:, u % RAW])
            for o, i in todo:
                last = nc.scalar.activation(o, i, ACT.Copy)
            last.then_inc(hi_done, 1)

        for c in range(DC):
            act.wait_ge(xpose, c + 1)
            nc.scalar.activation(x_hi[:, c], ps[:, 6 + c % 2, 0:T], ACT.Copy).then_inc(xin_raw, 1)
        for u in range(AHEAD):
            split(u)
        act.dma_start(new_conv_s[0, :, 0:HIST - DEC_T], state_conv[0, :, DEC_T:HIST]).then_inc(stores, 16)
        act.wait_ge(consts_made, 8)
        act.wait_ge(const_ld, CONST_LOADS * 16)
        for m in range(8):
            split(U_CIN + m + AHEAD)
            act.wait_ge(unit_used, U_CIN + m + 1)
            if m >= 2:
                act.wait_ge(group_free, m - 1)
            nc.scalar.activation(gate[:, m % 2], ps[:, 2 * ((G_CIN + m) % 3) + 1, 0:T], ACT.Sigmoid,
                                 bias=b_in[:, DC + m:DC + m + 1]).then_inc(gate_ready, 1)

        def spread(n):
            for c in range(DC):
                act.wait_ge(ln_cent, DC * n + c + 1)
                nc.scalar.activation(sq[:, c], work[:, c], ACT.Square).then_inc(ln_sq, 1)
            act.wait_ge(ln_var, n + 1)
            nc.scalar.activation(rstd[:], ps[:, 7, 0:T], ACT.Sqrt, scale=1.0 / D, bias=eps[:, 0:1]).then_inc(ln_std, 1)

        def layer_norm(n, out, func, g, b):
            spread(n)
            for c in range(DC):
                act.wait_ge(ln_scaled, DC * n + c + 1)
                nc.scalar.activation(out[:, c], work[:, c], func, scale=g(c), bias=b(c))
                nc.scalar.activation(x_hi[:, c], work[:, c], func, scale=g(c), bias=b(c)).then_inc(ln_hi, 1)

        layer_norm(0, sq, ACT.Silu, lambda c: cg[:, c:c + 1], lambda c: cb[:, c:c + 1])
        act.wait_ge(edge_copied, 1)
        act.dma_start(new_conv_p[0, 0], edge[0:HIST, 0]).then_inc(edge_out, 16)
        for s_ in range(DEC_B):
            act.dma_start(new_conv_s[0, s_, HIST - DEC_T:HIST], edge[DEC_T * s_:DEC_T * s_ + DEC_T, 1]).then_inc(edge_out, 16)
        for i in range(4):
            split(U_COUT + i + AHEAD)
        layer_norm(1, xres, ACT.Identity, lambda c: lng[:, 0, c:c + 1], lambda c: lnb[:, 0, c:c + 1])

        def gate_silu(r, it=0):
            if isinstance(it, int):
                split(U_GU + 6 * it + r + AHEAD)
            else:
                split(U_GU + r + AHEAD, it)
            act.wait_ge(unit_used, it * 6 + (U_GU + r + 1))
            act.wait_ge(group_free, it * 6 + (G_GU + r - 1))
            nc.scalar.activation(gate[:, r % 2], ps[:, 2 * ((G_GU + r) % 3), 0:T], ACT.Silu).then_inc(gate_ready, 1)

        with act.Fori(0, 3) as it:
            for r in range(6):
                gate_silu(r, it)
        for r in range(FC - 18):
            gate_silu(r, 3)
        for i in range(12):
            split(U_DOWN + i + AHEAD)
        layer_norm(2, xres, ACT.Identity, lambda c: lng[:, 1, c:c + 1], lambda c: lnb[:, 1, c:c + 1])

        act.wait_ge(unit_used, U_MIN)
        act.dma_start(wuk[:], mla_w_uk[0].rearrange("(c p) h d -> p c (h d)", p=P)).then_inc(wuk_ld, 16)
        act.dma_start(cosT[:], cos_t).then_inc(att_ld, 16)
        act.dma_start(sinT[:], sin_t).then_inc(att_ld, 16)
        for i in range(4):
            split(U_MIN + i + AHEAD)
        act.wait_ge(group_free, G_MIN + 3)
        nc.scalar.activation(sq[:, 0:4], cq_f[:], ACT.Square)
        nc.scalar.activation(sq[:, 4:6], ckvT[:], ACT.Square).then_inc(mla_act, 1)
        act.wait_ge(mla_pe, 1)
        nc.scalar.activation(rstd[:], ps[:, 6, 0:T], ACT.Sqrt, scale=1.0 / QLORA, bias=eps[:, 1:2])
        nc.scalar.activation(rms_kv, ps[:, 7, 0:T], ACT.Sqrt, scale=1.0 / LORA, bias=eps[:, 1:2]).then_inc(rms_rt, 1)
        act.wait_ge(mla_pe, 2)
        for q, bank in enumerate(WUK_BANKS):
            last = nc.scalar.activation(wukT[:, 2 * q:2 * q + 2], ps[:, bank, :].rearrange("p (j r) -> p j r", j=2), ACT.Copy)
        last.then_inc(mla_act, 1)
        for c in range(4):
            act.wait_ge(mla_dve, c + 1)
            nc.scalar.activation(cq_hi[:, c], cq_f[:, c], ACT.Copy, scale=g_q[:, c:c + 1])
            nc.scalar.activation(cq_f[:, c], cq_f[:, c], ACT.Copy, scale=g_q[:, c:c + 1]).then_inc(cq_hi_done, 1)
        act.wait_ge(mla_dve, 5)
        for c in range(RC):
            last = nc.scalar.activation(ckvT[:, c], ckvT[:, c], ACT.Copy, scale=g_kv[:, c:c + 1])
        last.then_inc(mla_act, 1)
        split(U_UQ + AHEAD)
        act.wait_ge(mla_pe, 3)
        for b, (t0, n) in enumerate(TB):
            nc.scalar.activation(ckvN[0:n, b], ps[0:n, 6, 0:LORA] if b == 0 else ps[0:n, 6, 256:512] if b == 1
                                 else ps[0:n, 7, 0:LORA], ACT.Copy)
            last = nc.scalar.activation(krN[0:n, b], ps[0:n, 7, 256 + 32 * b:288 + 32 * b], ACT.Copy)
        last.then_inc(kvN_copied, 1)
        act.wait_ge(kvN_copied, 1)
        for b, (t0, n) in enumerate(TB[:2]):
            act.dma_start(new_ckv_p[0, 0, t0:t0 + n], ckvN[0:n, b]).then_inc(stores, 16)
            act.dma_start(new_kr_p[0, 0, t0:t0 + n], krN[0:n, b]).then_inc(stores, 16)
        act.dma_start(new_ckv_p[0, 0, TAIL0:T_P], ckvN[0:QT, 2]).then_inc(stores, 16)
        act.dma_start(new_kr_p[0, 0, TAIL0:T_P], krN[0:QT, 2]).then_inc(stores, 16)
        act.dma_start(new_ckv_s[0].rearrange("b t r -> (b t) r"), ckvN[QT:TAIL, 2]).then_inc(stores, 16)
        act.dma_start(new_kr_s[0].rearrange("b t r -> (b t) r"), krN[QT:TAIL, 2]).then_inc(stores, 16)
        for i in range(1, 4):
            split(U_UQ + i + AHEAD)

        def soft(i, n_groups):
            b = i % 2
            act.wait_ge(p_sm, i + 1)
            for o, a, e in n_groups:
                last = nc.scalar.activation(sc[:, b, a:e], sc[:, b, a:e], ACT.Exp, scale=SM_SCALE,
                                            bias=pst[:, b, o:o + 1], accum_out=pst[:, b, 2 + o:3 + o])
            last.then_inc(p_ex, 1)

        def pt_copy(i, n):
            act.wait_ge(p_tr, i + 1)
            if i >= 2:
                act.wait_ge(p_pv, i - 1)
            nc.scalar.activation(pT[:, i % 2, 0:n], ps[:, 5, 0:n], ACT.Copy).then_inc(p_pt, 1)

        def ql_copy(h):
            act.wait_ge(p_ql, h + 1)
            if h >= 2:
                act.wait_ge(p_sc, h - 1)
            for c in range(RC):
                nc.scalar.activation(ql[:, h % 2, c], ps[:, c, 0:T], ACT.Copy)
            for c in range(RC):
                last = nc.scalar.activation(qlt[:, c, h], ps[:, c, TAIL0:T], ACT.Copy)
            last.then_inc(p_qc, 1)

        ql_copy(0)
        for h in range(HEADS + 1):
            if h < HEADS:
                soft(h, [(0, 0, P), (1, P, 3 * P)])
            if h + 1 < HEADS:
                ql_copy(h + 1)
            if h >= 1:
                pt_copy(h - 1, 3 * P)
        for i in range(2):
            soft(HEADS + i, [(0, 0, T_P)])
            pt_copy(HEADS + i, 3 * P)

        def k_copy(s, b, g):
            act.wait_ge(s_t, s * 4 + (g + 1))
            if not isinstance(s, int) or s * 4 + g >= 2:
                act.wait_ge(s_sc, s * 4 + (g - 1))
            for c in range(2):
                last = nc.scalar.activation(kt[:, g % 2, 2 * c:2 * c + 2], ps[:, c, 0:512].rearrange(
                    "p (a r) -> p a r", a=2), ACT.Copy)
            last.then_inc(s_kt, 1)

        def exps(s, b):
            act.wait_ge(s_sh, s + 1)
            nc.scalar.activation(ss[b][:], ss[b][:], ACT.Exp, scale=SM_SCALE)
            nc.scalar.activation(sn[b][0:DEC_T, :], sn[b][0:DEC_T, :], ACT.Exp, scale=SM_SCALE).then_inc(s_ex, 1)

        def sample(s, b):
            k_copy(s, b, 0)
            k_copy(s, b, 1)
            exps(s - 1, 1 - b)
            k_copy(s, b, 2)
            k_copy(s, b, 3)

        for g in range(4):
            k_copy(0, 0, g)
        with act.Fori(0, (DEC_B - 2) // 2) as it:
            sample(it * 2 + 1, 1)
            sample(it * 2 + 2, 0)
        sample(DEC_B - 1, 1)
        exps(DEC_B - 1, 1)

        act.wait_ge(v_ready, 1)
        for c in range(DC):
            nc.scalar.activation(x_hi[:, c], qnT[:, c], ACT.Copy).then_inc(ln_hi, 1)
        for i in range(4):
            split(U_MOUT + i + AHEAD)
        spread(3)
        for c in range(DC):
            act.wait_ge(ln_scaled, DC * 3 + c + 1)
            nc.scalar.activation(xres[:, c], work[:, c], ACT.Identity, scale=lng[:, 2, c:c + 1], bias=lnb[:, 2, c:c + 1]
                                 ).then_inc(ln_hi, 1)
        act.wait_ge(stores, 9 * 16)
        for i in range(6):
            b, hf = divmod(i, 2)
            n = TB[b][1]
            act.wait_ge(rt_pe, i + 2)
            nc.scalar.activation(xt[0:n, b, 512 * hf:512 * hf + 512], ps[0:n, ROW_BANKS[i], :], ACT.Copy).then_inc(rt_act, 1)
        act.wait_ge(rt_dve, 1)
        nc.scalar.activation(tk[:, 3], tk[:, 2], ACT.Exp).then_inc(rt_act, 1)

        act.wait_ge(table_ready, 1)
        n_jobs = act.value_load(jobi[0:1, MAX_JOBS:MAX_JOBS + 1], min_val=NEXP, max_val=MAX_JOBS)

        def y_upper(jobs_done):
            act.wait_ge(unit_used, jobs_done * JOB_UNITS + U_MOE)
            for q in range(2):
                last = nc.scalar.activation(y_hi[:, 512 * q:512 * q + 512], ps[:, 4 + q, :], ACT.Copy)
            last.then_inc(m_yhi, 1)

        def gathered(part, job):
            act.wait_ge(m_g, job * 2 + (part + 1))
            nc.scalar.activation(g_next[:, 4 * part:4 * part + 4], ps[:, 7, :].rearrange("p (c s) -> p c s", c=4), ACT.Copy
                                 ).then_inc(m_gc, 1)

        def next_upper():
            nc.scalar.activation(g_hi[:], g_next[:], ACT.Copy).then_inc(m_gh, 1)

        gathered(0, 0)
        gathered(1, 0)
        act.wait_ge(m_gc, 2)
        next_upper()
        act.wait_ge(m_zero, 1)
        with act.Fori(0, n_jobs) as j:
            def split_moe(k):
                if k >= JOB_UNITS:
                    return
                u = U_MOE + k
                act.wait_ge(raw_ready[u % RAW], moe_raw_target(k, j))
                act.wait_ge(unit_used, j * JOB_UNITS + (u - SPLIT + 1))
                nc.scalar.activation(w_hi[:, u % SPLIT], raw[:, u % RAW], ACT.Copy).then_inc(hi_done, 1)

            split_moe(0)
            split_moe(1)
            y_upper(j)
            k = 0
            for s in range(STEPS + 1):
                if s < STEPS:
                    split_moe(k + 2)
                    split_moe(k + 3)
                    k += 2
                if s >= 1:
                    act.wait_ge(m_hT, j * STEPS + s)
                    nc.scalar.activation(hT_hi[:], ps[:, 6, :].rearrange("p (c s) -> p c s", c=4), ACT.Copy).then_inc(m_hTc, 1)
                if s < STEPS:
                    act.wait_ge(unit_used, j * JOB_UNITS + (U_MOE + first_unit(s) + 2))
                    nc.scalar.activation(sg[:, s % 2], ps[:, 2 * (s % 2), :], ACT.Silu).then_inc(m_sg, 1)
                    split_moe(k + 2)
                    split_moe(k + 3)
                    k += 2
                if s == TURN_STEP:
                    act.wait_ge(m_pickT, j + 1)
                    nc.scalar.activation(pickT[:], ps[:, 7, 0:3 * P].rearrange("p (b t) -> p b t", b=3), ACT.Copy
                                         ).then_inc(m_pickTc, 1)
                if 1 <= s < STEPS:
                    split_moe(k + 2)
                    split_moe(k + 3)
                    k += 2
                if s in GATHER_STEPS:
                    gathered(GATHER_STEPS.index(s), j + 1)
            act.wait_ge(unit_used, j * JOB_UNITS + (U_MOE + JOB_UNITS - 4))
            next_upper()

        act.dma_start(gbc[:], ln_g[1, 1:2].broadcast_to([P, D])).then_inc(fin_ld, 16)
        act.dma_start(bbc[:], ln_b[1, 1:2].broadcast_to([P, D])).then_inc(fin_ld, 16)
        y_upper(n_jobs)
        for b, (t0, n) in enumerate(TB):
            act.wait_ge(fin_v, b + 1)
            nc.scalar.activation(sqt[0:n], acc[0:n, b], ACT.Square, accum_out=stat[0:n, b, 2:3]).then_inc(fin_sq, 1)
            act.wait_ge(fin_sq, b + 1)
            nc.scalar.activation(stat[0:n, b, 3:4], stat[0:n, b, 2:3], ACT.Sqrt, scale=1.0 / D, bias=eps[0:n, 0:1]).then_inc(fin_a, 1)
        act.wait_ge(fin_v, 3 + 1)
        act.dma_start(y_prompt[0, 0:P - N_META], acc[N_META:P, 0]).then_inc(stores, 16)
        act.wait_ge(fin_v, 3 + 2)
        act.dma_start(y_prompt[0, P - N_META:2 * P - N_META], acc[:, 1]).then_inc(stores, 16)
        act.wait_ge(fin_v, 3 + 3)
        act.dma_start(y_prompt[0, 2 * P - N_META:SEQ], acc[0:QT, 2]).then_inc(stores, 16)
        act.dma_start(y_sample.rearrange("b t d -> (b t) d"), acc[QT:TAIL, 2]).then_inc(stores, 16)
        act.wait_ge(stores, STORES * 16)

    @block.vector
    def _(v):
        V = nc.vector
        n_own = [0]

        def mark(ins):
            n_own[0] += 1
            ins.then_inc(dve, 1)

        def settle():
            v.wait_ge(dve, n_own[0])

        def chain(ins):
            mark(ins)
            settle()

        def split(u, it=None):
            if u >= U_MOE:
                return
            v.wait_ge(hi_done, (u + 1) if it is None else it * 6 + (u + 1))
            his = [o for o, _ in split_copies(u, w_hi[:, u % SPLIT], raw[:, u % RAW])]
            los = split_copies(u, w_lo[:, u % SPLIT], raw[:, u % RAW])
            for hi, (lo, src) in zip(his, los):
                last = V.tensor_tensor(lo, src, hi.bitcast(F32), ALU.subtract)
            last.then_inc(lo_done, 1)

        for c in range(DC):
            v.wait_ge(xin_raw, c + 1)
            V.tensor_tensor(x_lo[:, c], ps[:, 6 + c % 2, 0:T], x_hi[:, c].bitcast(F32), ALU.subtract)
            V.tensor_copy(xres[:, c], ps[:, 6 + c % 2, 0:T]).then_inc(xpose_free, 1)
        for u in range(AHEAD):
            split(u)
        v.wait_ge(taps_turned, 1)
        V.tensor_copy(w_dw[:].rearrange("p t c -> p c t"), ps[:, 0, 0:DC * TAPS].rearrange("p (c t) -> p c t", c=DC)
                      ).then_inc(taps_ready, 1)
        for c in range(DC):
            v.wait_ge(xpose, DC + c + 1)
            last = V.tensor_copy(u_s[:, c, :, 0:HIST], ps[:, 6 + c % 2, 0:DEC_B * HIST].rearrange("p (s t) -> p s t", s=DEC_B))
            last.then_inc(xpose_free, 1)
        v.wait_ge(const_ld, CONST_LOADS * 16)
        v.wait_ge(taps_ready, 1)
        v.wait_ge(consts_made, 8)
        def add_taps(m):
            v.wait_ge(diag_used, PE_TAPS * (m + 1))
            V.tensor_tensor(work[:, m], work[:, m], ps[:, 6 + m % 2, 0:T], ALU.add).then_inc(ln_in, 1)

        for m in range(8):
            split(U_CIN + m + AHEAD)
            v.wait_ge(gate_ready, m + 1)
            a = ps[:, 2 * ((G_CIN + m) % 3)]
            V.scalar_tensor_tensor(out=u_p[:, m, HIST:], in0=a[:, 0:T_P], scalar=b_in[:, m:m + 1],
                                   in1=gate[:, m % 2, 0:T_P], op0=ALU.add, op1=ALU.mult)
            last = V.scalar_tensor_tensor(out=u_s[:, m, :, HIST:], in0=a[:, T_P:T].rearrange("p (s t) -> p s t", s=DEC_B),
                                          scalar=b_in[:, m:m + 1],
                                          in1=gate[:, m % 2, T_P:T].rearrange("p (s t) -> p s t", s=DEC_B),
                                          op0=ALU.add, op1=ALU.mult)
            last.then_inc(group_free, 1)
            v.wait_ge(group_free, m + 1)
            wp = work[:, m, 0:T_P]
            wsm = work[:, m, T_P:T].rearrange("p (s t) -> p s t", s=DEC_B)
            for t in range(PE_TAPS, TAPS):
                if t == PE_TAPS:
                    mark(V.tensor_scalar(wp, u_p[:, m, t:t + T_P], w_dw[:, t, m:m + 1], b_dw[:, m:m + 1], ALU.mult, ALU.add))
                    mark(V.tensor_scalar(wsm, u_s[:, m, :, t:t + DEC_T], w_dw[:, t, m:m + 1], b_dw[:, m:m + 1], ALU.mult, ALU.add))
                else:
                    v.wait_ge(dve, n_own[0] - 1)
                    mark(V.scalar_tensor_tensor(out=wp, in0=u_p[:, m, t:t + T_P], scalar=w_dw[:, t, m:m + 1], in1=wp,
                                                op0=ALU.mult, op1=ALU.add))
                    v.wait_ge(dve, n_own[0] - 1)
                    mark(V.scalar_tensor_tensor(out=wsm, in0=u_s[:, m, :, t:t + DEC_T], scalar=w_dw[:, t, m:m + 1],
                                                in1=wsm, op0=ALU.mult, op1=ALU.add))
            if m >= 1:
                add_taps(m - 1)
        settle()
        add_taps(7)
        V.tensor_copy(u_new[:].rearrange("p c (s t) -> p c s t", s=DEC_B), u_s[:, :, :, HIST:]).then_inc(ln_in, 1)
        v.wait_ge(edge_ready, 1)
        V.tensor_copy(edge[0:HIST, 0].rearrange("p (b n) -> p b n", b=2), ps[0:HIST, 4:6, :])
        V.tensor_copy(edge[0:T_S, 1].rearrange("p (b n) -> p b n", b=2), ps[0:T_S, 0:2, :]).then_inc(edge_copied, 1)

        def layer_norm(n, out, split_x=True):
            v.wait_ge(ln_mean, n + 1)
            chain(V.tensor_scalar(rstd[:], ps[:, 6, 0:T], 1.0 / D, None, ALU.mult))
            for c in range(DC):
                V.tensor_tensor(work[:, c], work[:, c], rstd[:], ALU.subtract).then_inc(ln_cent, 1)
            v.wait_ge(ln_std, n + 1)
            chain(V.reciprocal(rstd[:], rstd[:]))
            for c in range(DC + 2):
                if c < DC:
                    V.tensor_tensor(work[:, c], work[:, c], rstd[:], ALU.mult).then_inc(ln_scaled, 1)
                if c >= 2 and split_x:
                    v.wait_ge(ln_hi, DC * n + c - 1)
                    V.tensor_tensor(x_lo[:, c - 2], out[:, c - 2], x_hi[:, c - 2].bitcast(F32), ALU.subtract).then_inc(x_split, 1)

        def residual(u, g, c0):
            v.wait_ge(unit_used, u + 1)
            for o in range(2):
                last = V.scalar_tensor_tensor(out=work[:, c0 + o], in0=xres[:, c0 + o], scalar=ALPHA,
                                              in1=ps[:, 2 * (g % 3) + o, 0:T], op0=ALU.mult, op1=ALU.add)
            last.then_inc(group_free, 1)

        layer_norm(0, sq)
        for i in range(4):
            split(U_COUT + i + AHEAD)
            residual(U_COUT + i, G_COUT + i, 2 * i)
        layer_norm(1, xres)

        own_gu = n_own[0]
        v.wait_ge(edge_out, 16 * (1 + DEC_B))

        def ffn_h(r, it=0):
            if isinstance(it, int):
                split(U_GU + 6 * it + r + AHEAD)
            else:
                split(U_GU + r + AHEAD, it)
            v.wait_ge(gate_ready, it * 6 + (8 + r + 1))
            idx = it * 6 + r
            hs, ls = (h_hi[:, idx], h_lo[:, idx]) if isinstance(it, int) else (
                h_hi[:, bass.ds(idx, 1)].rearrange("p a t -> p (a t)"), h_lo[:, bass.ds(idx, 1)].rearrange("p a t -> p (a t)"))
            V.tensor_tensor(htmp[:, r % 2], gate[:, r % 2], ps[:, 2 * ((G_GU + r) % 3) + 1, 0:T], ALU.mult).then_inc(group_free, 1)
            v.wait_ge(group_free, it * 6 + (G_GU + r + 1))
            V.tensor_scalar(hs, htmp[:, r % 2], 1.0, None, ALU.mult).then_inc(dve, 1)
            v.wait_ge(dve, it * 6 + (own_gu + r + 1))
            V.tensor_tensor(ls, htmp[:, r % 2], hs.bitcast(F32), ALU.subtract).then_inc(h_split, 1)

        with v.Fori(0, 3) as it:
            for r in range(6):
                ffn_h(r, it)
        for r in range(FC - 18):
            ffn_h(r, 3)
        n_own[0] += FC
        for i in range(4):
            for k in range(3):
                split(U_DOWN + 3 * i + k + AHEAD)
            residual(U_DOWN + 3 * i + 2, G_DOWN + i, 2 * i)
        layer_norm(2, xres)

        for i in range(3):
            split(U_MIN + i + AHEAD)
            g = G_MIN + i
            v.wait_ge(unit_used, U_MIN + i + 1)
            for o in range(2):
                dst = cq_f[:, 2 * i + o] if i < 2 else ckvT[:, o]
                last = V.tensor_copy(dst, ps[:, 2 * (g % 3) + o, 0:T])
            last.then_inc(group_free, 1)
        split(U_MIN + 3 + AHEAD)
        v.wait_ge(att_ld, 32)
        g = G_MIN + 3

        def rotate(dst, x_ps, sw_ps):
            mark(V.tensor_tensor(htmp_a, sw_ps, sinT[:], ALU.mult))
            chain(V.tensor_tensor(dst, x_ps, cosT[:], ALU.mult))
            return V.tensor_tensor(dst, dst, htmp_a, ALU.add)

        htmp_a = work[:, 0]
        v.wait_ge(unit_used, U_MIN + 4)
        rotate(krT[:], ps[:, 2 * (g % 3), 0:T], ps[:, 2 * (g % 3) + 1, 0:T]).then_inc(group_free, 1)
        v.wait_ge(group_free, G_MIN + 4)
        v.wait_ge(rms_rt, 1)
        chain(V.reciprocal(rstd[:], rstd[:]))
        for c in range(4):
            V.tensor_tensor(cq_f[:, c], cq_f[:, c], rstd[:], ALU.mult).then_inc(mla_dve, 1)
        chain(V.reciprocal(rms_kv, rms_kv))
        V.tensor_tensor(ckvT[:], ckvT[:], rms_kv.unsqueeze(1).broadcast_to([P, RC, T]), ALU.mult).then_inc(mla_dve, 1)
        for c in range(4):
            v.wait_ge(cq_hi_done, c + 1)
            V.tensor_tensor(cq_lo[:, c], cq_f[:, c], cq_hi[:, c].bitcast(F32), ALU.subtract).then_inc(cq_lo_done, 1)
        for i in range(4):
            split(U_UQ + i + AHEAD)
            v.wait_ge(unit_used, U_UQ + i + 1)
            pb = 4 * (i % 2)
            V.tensor_copy(qnT[:, 2 * i], ps[:, pb, 0:T])
            V.tensor_copy(qnT[:, 2 * i + 1], ps[:, pb + 1, 0:T])
            if i:
                v.wait_ge(uq_free, i)
            rotate(qrT[:, i], ps[:, pb + 2, 0:T], ps[:, pb + 3, 0:T]).then_inc(uq_free, 1)
        v.wait_ge(attc, 8)
        chain(V.tensor_scalar(row_i[:], row_i[:], QT - 1, None, ALU.bitwise_and))
        chain(V.tensor_copy(row_f[:], row_i[:]))
        chain(V.tensor_scalar(causal_t[:], key_f[:], row_f[:, 0:1], NEG, ALU.is_gt, ALU.mult))

        def shift(i, groups, mask_at, mask):
            b = i % 2
            v.wait_ge(p_sc, i + 1)
            bank = 2 + i % 2
            n = groups[-1][2]
            if i >= 2:
                v.wait_ge(p_tr, i - 1)
            if mask_at:
                V.tensor_copy(sc[:, b, 0:mask_at], ps[:, bank, 0:mask_at])
            chain(V.tensor_tensor(sc[:, b, mask_at:n], ps[:, bank, mask_at:n], mask, ALU.add))
            for o, a, e in groups:
                mark(V.reduce_max(pst[:, b, 4 + o:5 + o], sc[:, b, a:e], AX))
            settle()
            V.tensor_scalar(pst[:, b, 0:2], pst[:, b, 4:6], -SM_SCALE, None, ALU.mult).then_inc(p_sm, 1)

        def norm(i, groups):
            b = i % 2
            v.wait_ge(p_ex, i + 1)
            chain(V.reciprocal(pst[:, b, 6:8], pst[:, b, 2:4]))
            for o, a, e in groups:
                last = V.tensor_scalar(sc[:, b, a:e], sc[:, b, a:e], pst[:, b, 6 + o:7 + o], None, ALU.mult)
            last.then_inc(p_nm, 1)

        G2 = [(0, 0, P), (1, P, 3 * P)]
        v.wait_ge(p_ql, 1)
        chain(V.memset(pst[:], 1.0))
        def ot_copy(k):
            v.wait_ge(p_pv, k + 1)
            if k >= 2:
                v.wait_ge(p_v, k - 1)
            V.tensor_copy(oT[:, k % 2], ps[:, 6, :].rearrange("p (c q) -> p c q", c=RC)).then_inc(p_ot, 1)

        def v_copy(k):
            v.wait_ge(p_v, k + 1)
            r0 = VH * (k % 2)
            V.tensor_copy(qnT[r0:r0 + VH, k // 2, 0:2 * P], ps[r0:r0 + VH, 7, 0:2 * P]).then_inc(p_vc, 1)

        for h in range(HEADS + 4):
            if h < HEADS:
                shift(h, G2, 0, causal[:])
            if h >= 4:
                v_copy(h - 4)
            if h < HEADS:
                norm(h, G2)
            if 2 <= h < HEADS + 2:
                ot_copy(h - 2)
        v.wait_ge(p_qc, HEADS)
        v.wait_ge(qrt_ld, 16 * 16)
        for i in range(2):
            for c in range(RC):
                V.tensor_copy(tailq[i][:, c].rearrange("p (h q) -> p h q", h=8), qlt[:, c, 8 * i:8 * i + 8, 0:QT])
            V.tensor_copy(tailq[i][:, RC].rearrange("p (h q) -> p h q", h=8), qrt[:, 8 * i:8 * i + 8, 0:QT]).then_inc(tail_ready, 1)
        for i in range(2):
            k = HEADS + i
            shift(k, [(0, 0, T_P)], 2 * P, causal_t[:])
            norm(k, [(0, 0, T_P)])
            v.wait_ge(p_pv, k + 1)
            V.tensor_copy(qlt[:, :, 8 * i:8 * i + 8, 0:QT], ps[:, 6, 0:RC * P].rearrange("p (c h q) -> p c h q", c=RC, h=8)).then_inc(p_vc, 1)

        v.wait_ge(p_ql, HEADS)
        for b in range(2):
            mark(V.memset(qsr[b][:], 0.0))
            mark(V.memset(mx[b][:, NQ:2 * NQ], 0.0))
        settle()
        cnt = [0]

        def heads(ap):
            return ap.rearrange("p (h t) -> p h t", h=HEADS)

        def done(ins, off):
            cnt[0] += 1
            ins.then_inc(s_st, 1)
            v.wait_ge(s_st, off + cnt[0])

        def queries(s, b):
            for c in range(RC):
                V.tensor_scalar(heads(qs[b][:, c]), qlt[:, c, :, bass.ds(s * DEC_T + QT, DEC_T)], 1.0, None, ALU.mult)
                V.tensor_scalar(kn[b][:, c], ckvT[:, c, bass.ds(s * DEC_T + T_P, DEC_T)], 1.0, None, ALU.mult)
            V.tensor_scalar(kn[b][:, RC], krT[:, bass.ds(s * DEC_T + T_P, DEC_T)], 1.0, None, ALU.mult)
            for p in range(4):
                rs = slice(32 * p, 32 * p + 32)
                last = V.tensor_scalar(heads(qsr[b][rs, p]), qrt[rs, :, bass.ds(s * DEC_T + QT, DEC_T)], 1.0, None, ALU.mult)
            last.then_inc(s_q, 1)

        def kr_copy(s, g):
            v.wait_ge(s_t, s * 4 + (g + 1))
            if not isinstance(s, int) or s * 4 + g >= 2:
                v.wait_ge(s_sc, s * 4 + (g - 1))
            V.tensor_copy(kr4[:, g % 2], ps[:, 2, 0:P]).then_inc(s_kn, 1)

        def pages_of(b):
            return ps[:, 3:5, :] if b == 0 else ps[:, 6:8, :]

        def new_keys(s, b):
            v.wait_ge(s_t, s * 4 + 1)
            V.tensor_copy(knN[b][0:DEC_T], ps[0:DEC_T, 2, P:P + LORA])
            V.tensor_tensor(sn[b][0:DEC_T], ps[0:DEC_T, 2, 384:384 + NQ],
                            causal_s[0:DEC_T].rearrange("p h t -> p (h t)"), ALU.add)

        def maxima(s, b, off):
            v.wait_ge(s_sc, s * 4 + 4)
            done(V.reduce_max(mx[b][:, 0:NQ], pages_of(b).rearrange("p b (g q) -> p q (b g)", q=NQ), AX), off)
            V.tensor_tensor(mx[b][0:DEC_T, 0:NQ], mx[b][0:DEC_T, 0:NQ], sn[b][0:DEC_T], ALU.max).then_inc(s_mt, 1)

        def diagonal(s, b, off):
            v.wait_ge(s_dg, s * 2 + 1)
            done(V.reduce_max(m1[b][0:NQ], ps[0:NQ, 5, P:2 * P], AX), off)
            V.tensor_scalar(dg[b][0:NQ], ident[0:NQ, 0:NQ], m1[b][0:NQ, 0:1], None, ALU.mult).then_inc(s_mb, 1)

        def subtract(s, b, off):
            v.wait_ge(s_dg, s * 2 + 2)
            done(V.tensor_copy(dg[b][:], ps[:, 5, 256:256 + NQ]), off)
            V.tensor_tensor(ss[b][:].rearrange("p (b g) q -> p b g q", b=2), pages_of(b).rearrange("p b (g q) -> p b g q", q=NQ),
                            dg[b][:].unsqueeze(1).unsqueeze(1).broadcast_to([P, 2, 8, NQ]), ALU.subtract)
            V.tensor_tensor(sn[b][0:DEC_T], sn[b][0:DEC_T], dg[b][0:DEC_T], ALU.subtract).then_inc(s_sh, 1)

        def sums(s, b, off):
            v.wait_ge(s_ex, s + 1)
            done(V.reduce_sum(mx[b][:, 0:NQ], ss[b][:].rearrange("p g q -> p q g"), AX), off)
            V.tensor_tensor(mx[b][0:DEC_T, 0:NQ], mx[b][0:DEC_T, 0:NQ], sn[b][0:DEC_T], ALU.add).then_inc(s_sum, 1)

        def finish(s, b, off):
            v.wait_ge(s_pv, s + 1)
            done(V.reciprocal(dg[b][:], ps[:, 5, 320:320 + NQ]), off)
            for c in range(RC):
                last = V.tensor_tensor(qlt[:, c, :, bass.ds(s * DEC_T + QT, DEC_T)], heads(ps[:, 5, NQ * c:NQ * c + NQ]),
                                       heads(dg[b][:]), ALU.mult)
            last.then_inc(s_free, 1)

        def sample(s, b, off, following=True):
            maxima(s - 1, 1 - b, off)
            new_keys(s, b)
            kr_copy(s, 0)
            diagonal(s - 1, 1 - b, off)
            kr_copy(s, 1)
            subtract(s - 1, 1 - b, off)
            kr_copy(s, 2)
            if following:
                queries(s + 1, 1 - b)
            sums(s - 1, 1 - b, off)
            kr_copy(s, 3)
            finish(s - 1, 1 - b, off)

        queries(0, 0)
        new_keys(0, 0)
        for g in range(4):
            kr_copy(0, g)
        queries(1, 1)
        ROUND = 10
        with v.Fori(0, (DEC_B - 2) // 2) as it:
            sample(it * 2 + 1, 1, it * ROUND)
            sample(it * 2 + 2, 0, it * ROUND)
        assert cnt[0] == ROUND, cnt[0]
        cnt[0] = ROUND * (DEC_B - 2) // 2
        sample(DEC_B - 1, 1, 0, following=False)
        maxima(DEC_B - 1, 1, 0)
        diagonal(DEC_B - 1, 1, 0)
        subtract(DEC_B - 1, 1, 0)
        sums(DEC_B - 1, 1, 0)
        finish(DEC_B - 1, 1, 0)
        v.wait_ge(p_v, HEADS + 1)
        for h in range(HEADS):
            r0 = VH * (h % 2)
            last = V.tensor_copy(qnT[r0:r0 + VH, h // 2, TAIL0:T], ps[r0:r0 + VH, (h % 4) // 2 + 4 * (h % 2), TAIL * (h // 4):TAIL * (h // 4) + TAIL])
        last.then_inc(v_ready, 1)
        for c in range(DC):
            v.wait_ge(ln_hi, DC * 3 + c + 1)
            V.tensor_tensor(x_lo[:, c], qnT[:, c], x_hi[:, c].bitcast(F32), ALU.subtract).then_inc(x_split, 1)
        for i in range(4):
            split(U_MOUT + i + AHEAD)
            residual(U_MOUT + i, G_MOUT + i, 2 * i)
        layer_norm(3, xres, split_x=False)
        def acc_start(i):
            b, hf = divmod(i, 2)
            n = TB[b][1]
            v.wait_ge(rt_act, i + 1)
            V.tensor_scalar(acc[0:n, b, 512 * hf:512 * hf + 512], ps[0:n, ROW_BANKS[i], :], ALPHA, None, ALU.mult).then_inc(xpose_free, 1)

        v.wait_ge(rt_const, 8)
        v.wait_ge(rt_pe, 1)
        for b, (t0, n) in enumerate(TB):
            last = V.tensor_copy(lg[0:n, b], ps[0:n, LOGIT_BANKS[b], 0:NEXP])
        last.then_inc(rt_logits, 1)
        v.wait_ge(rt_logits, 1)
        every = [P, 3, NEXP, NEXP]
        one = lg[:].unsqueeze(3).broadcast_to(every)
        other = lg[:].unsqueeze(2).broadcast_to(every)
        mark(V.tensor_tensor(gt8[:], other, one, ALU.is_gt))
        chain(V.tensor_tensor(eq8[:], other, one, ALU.is_equal))
        chain(V.tensor_tensor(eq8[:], eq8[:], lt8[:].unsqueeze(1).broadcast_to(every), ALU.mult))
        chain(V.tensor_tensor(eq8[:], eq8[:], gt8[:], ALU.add))
        chain(V.reduce_sum(rank[:], eq8[:], AX))
        mark(V.tensor_scalar(oneA[:], rank[:], 0.0, None, ALU.is_equal))
        chain(V.tensor_scalar(oneB[:], rank[:], 1.0, None, ALU.is_equal))
        mark(V.tensor_tensor(oneA[:], oneA[:], valid[:], ALU.mult))
        chain(V.tensor_tensor(oneB[:], oneB[:], valid[:], ALU.mult))
        mark(V.tensor_tensor(selt[:], oneA[:], oneB[:], ALU.add))
        chain(V.tensor_tensor(keyt[:], oneA[:], lg[:], ALU.mult))
        chain(V.reduce_sum(tk[:, 0], keyt[:], AX))
        chain(V.tensor_tensor(keyt[:], oneB[:], lg[:], ALU.mult))
        chain(V.reduce_sum(tk[:, 1], keyt[:], AX))
        V.tensor_tensor(tk[:, 2], tk[:, 1], tk[:, 0], ALU.subtract).then_inc(rt_dve, 1)
        for i in range(3):
            acc_start(i)
        v.wait_ge(rt_act, 7)
        chain(V.tensor_scalar(tk[:, 4], tk[:, 3], 1.0, None, ALU.add))
        chain(V.reciprocal(tk[:, 4], tk[:, 4]))
        chain(V.tensor_tensor(tk[:, 5], tk[:, 4], tk[:, 3], ALU.mult))
        v.wait_ge(rt_pe, 8)
        counts = ps[:, 4, 32:32 + NEXP]
        mark(V.tensor_scalar(jobs[:, 0], counts, float(SLOTS), None, ALU.is_gt))
        chain(V.tensor_scalar(jobs[:, 1], counts, float(2 * SLOTS), None, ALU.is_gt))
        chain(V.tensor_tensor(jobs[:, 0], jobs[:, 0], jobs[:, 1], ALU.add))
        chain(V.tensor_scalar(jobs[:, 0], jobs[:, 0], 1.0, None, ALU.add))
        chain(V.tensor_tensor(cmp2[:], jobs[:, 0].unsqueeze(1).broadcast_to([P, NEXP, NEXP]), lt8[:], ALU.mult))
        chain(V.reduce_sum(starts[:], cmp2[:], AX))
        for b in range(3):
            chain(V.scalar_tensor_tensor(out=keyt[:, b], in0=starts[:], scalar=float(SLOTS), in1=ps[:, 4, NEXP * b:NEXP * b + NEXP],
                                         op0=ALU.mult, op1=ALU.add))
        chain(V.tensor_scalar(keyt[:], keyt[:], 1.0, None, ALU.add))
        for o, one in enumerate((oneA, oneB)):
            chain(V.tensor_tensor(rank[:], keyt[:], one[:], ALU.mult))
            chain(V.reduce_sum(tk[:, 6 + o], rank[:], AX))
            chain(V.tensor_scalar(tk[:, 6 + o], tk[:, 6 + o], -1.0, None, ALU.add))
        chain(V.tensor_tensor(cmp_[:], jobf[:, 0:MAX_JOBS].unsqueeze(2).broadcast_to([P, MAX_JOBS, NEXP]),
                              starts[:].unsqueeze(1).broadcast_to([P, MAX_JOBS, NEXP]), ALU.is_ge))
        chain(V.reduce_sum(jobf[:, 0:MAX_JOBS], cmp_[:], AX))
        chain(V.tensor_scalar(jobf[:, 0:MAX_JOBS], jobf[:, 0:MAX_JOBS], -1.0, None, ALU.add))
        chain(V.reduce_sum(jobf[:, MAX_JOBS:MAX_JOBS + 1], jobs[:, 0], AX))
        V.tensor_copy(jobi[:], jobf[:]).then_inc(table_ready, 1)
        v.wait_ge(table_ready, 1)

        n_jobs = v.value_load(jobi[0:1, MAX_JOBS:MAX_JOBS + 1], min_val=NEXP, max_val=MAX_JOBS)

        def make_pick(settled):
            for b in range(3):
                settled(V.tensor_scalar(pick[:, b], iota[:], tk[:, 6, b:b + 1], None, ALU.is_equal), b == 2)
            for b in range(3):
                last = V.scalar_tensor_tensor(out=pick[:, b], in0=iota[:], scalar=tk[:, 7, b:b + 1], in1=pick[:, b],
                                              op0=ALU.is_equal, op1=ALU.add)
            last.then_inc(m_pick, 1)

        def next_lower(job):
            v.wait_ge(m_gh, job + 1)
            V.tensor_tensor(g_lo[:], g_next[:], g_hi[:].bitcast(F32), ALU.subtract).then_inc(m_gl, 1)

        def y_lower(j):
            v.wait_ge(m_yhi, j + 1)
            V.tensor_tensor(y_lo[:].rearrange("p (q n) -> p q n", q=2), ps[:, 4:6, :],
                            y_hi[:].bitcast(F32).rearrange("p (q n) -> p q n", q=2), ALU.subtract).then_inc(m_ylo, 1)

        def add_rows(i, j):
            b, q = divmod(i, 2)
            n = TB[b][1]
            cs = slice(512 * q, 512 * q + 512)
            v.wait_ge(m_sct, j * 6 + (i + 1))
            V.scalar_tensor_tensor(out=acc[0:n, b, cs], in0=ps[0:n, 6 + i % 2, :], scalar=tk[0:n, 8, b:b + 1],
                                   in1=acc[0:n, b, cs], op0=ALU.mult, op1=ALU.add).then_inc(m_acc, 1)

        make_pick(lambda ins, end: chain(ins) if end else mark(ins))
        for i in range(3, 6):
            acc_start(i)
        v.wait_ge(xpose_free, 2 * DC + 6)
        V.memset(ps[:, 4:6, :], 0.0)
        V.memset(pickT[:].bitcast(F32), 0.0)
        V.memset(tk[:, 8], 0.0).then_inc(m_zero, 1)
        next_lower(0)
        with v.Fori(0, n_jobs) as j:
            OWN = 11
            cnt = [0]

            def mo_mark(ins):
                cnt[0] += 1
                ins.then_inc(m_own, 1)

            def mo_settle():
                v.wait_ge(m_own, j * OWN + cnt[0])

            def split_moe(k):
                u = U_MOE + k
                v.wait_ge(hi_done, j * JOB_UNITS + (u + 1))
                V.tensor_tensor(w_lo[:, u % SPLIT], raw[:, u % RAW], w_hi[:, u % SPLIT].bitcast(F32), ALU.subtract).then_inc(lo_done, 1)

            split_moe(0)
            split_moe(1)
            y_lower(j)
            k = 0
            for s in range(STEPS + 1):
                if s < STEPS:
                    split_moe(k + 2)
                    split_moe(k + 3)
                    k += 2
                if s == 0:
                    add_rows(0, j)
                    add_rows(1, j)
                if s >= 1:
                    v.wait_ge(m_hTc, j * STEPS + s)
                    V.tensor_tensor(hT_lo[:], ps[:, 6, :].rearrange("p (c s) -> p c s", c=4), hT_hi[:].bitcast(F32),
                                    ALU.subtract).then_inc(m_hTl, 1)
                if s < STEPS:
                    split_moe(k + 2)
                    split_moe(k + 3)
                    k += 2
                    v.wait_ge(m_sg, j * STEPS + (s + 1))
                    v.wait_ge(unit_used, j * JOB_UNITS + (U_MOE + first_unit(s) + 4))
                    V.tensor_tensor(hh[:, s % 2], sg[:, s % 2], ps[:, 2 * (s % 2) + 1, :], ALU.mult).then_inc(m_h, 1)
                if s <= 1:
                    add_rows(2 * s + 2, j)
                    add_rows(2 * s + 3, j)
                if s == TURN_STEP:
                    for o in range(2):
                        mo_mark(V.tensor_scalar(tk[:, 8 + o], tk[:, 6 + o], 0.0, None, ALU.is_ge))
                    for o in range(2):
                        mo_mark(V.tensor_scalar(tk[:, 10 + o], tk[:, 6 + o], float(SLOTS), None, ALU.is_lt))
                    mo_settle()
                    mo_mark(V.tensor_tensor(tk[:, 8:10], tk[:, 8:10], tk[:, 10:12], ALU.mult))
                    mo_settle()
                    mo_mark(V.tensor_tensor(tk[:, 8:10], tk[:, 8:10], tk[:, 4:6], ALU.mult))
                    mo_settle()
                    mo_mark(V.tensor_tensor(tk[:, 8], tk[:, 8], tk[:, 9], ALU.add))
                    mo_mark(V.tensor_scalar(tk[:, 6:8], tk[:, 6:8], -float(SLOTS), None, ALU.add))
                    mo_settle()
                if s == TURN_STEP + 1:
                    v.wait_ge(m_pickT, j + 1)
                    make_pick(lambda ins, end: (mo_mark(ins), mo_settle() if end else None))
                if 1 <= s < STEPS:
                    split_moe(k + 2)
                    split_moe(k + 3)
                    k += 2
            next_lower(j + 1)
            assert cnt[0] == OWN, cnt[0]
        y_lower(n_jobs)
        for b, (t0, n) in enumerate(TB):
            a = acc[0:n, b]
            add_rows(2 * b, n_jobs)
            add_rows(2 * b + 1, n_jobs)
            v.wait_ge(m_acc, n_jobs * 6 + (2 * b + 2))
            chain(V.reduce_sum(stat[0:n, b, 0:1], a, AX))
            chain(V.tensor_scalar(stat[0:n, b, 1:2], stat[0:n, b, 0:1], -1.0 / D, None, ALU.mult))
            V.tensor_scalar(a, a, stat[0:n, b, 1:2], None, ALU.add).then_inc(fin_v, 1)
        v.wait_ge(fin_ld, 32)
        for b, (t0, n) in enumerate(TB):
            a = acc[0:n, b]
            v.wait_ge(fin_a, b + 1)
            chain(V.reciprocal(stat[0:n, b, 3:4], stat[0:n, b, 3:4]))
            chain(V.scalar_tensor_tensor(out=a, in0=a, scalar=stat[0:n, b, 3:4], in1=gbc[0:n], op0=ALU.mult, op1=ALU.mult))
            V.tensor_tensor(a, a, bbc[0:n], ALU.add).then_inc(fin_v, 1)

    @block.tensor
    def _(pe):
        def mm3(out, hi, lo, xh, xl, start, stop):
            nc.tensor.matmul(out, hi, xh, start=start, stop=False, skip_group_check=True)
            nc.tensor.matmul(out, lo, xh, start=False, stop=False, skip_group_check=True)
            return nc.tensor.matmul(out, hi, xl, start=False, stop=stop, skip_group_check=True)

        def linear(u, g, nk, layout, xh, xl, it=None, first=True, last=True, free=True, chunks=None):
            off = 0 if it is None else it * 6
            pe.wait_ge(lo_done, off + (u + 1))
            if first and g >= 3 and free:
                pe.wait_ge(group_free, off + (g - 2))
            hi, lo = layout(w_hi[:, u % SPLIT]), layout(w_lo[:, u % SPLIT])
            order = [(k, o) for k in range(nk) for o in range(2)] if chunks is not None else [
                (k, o) for o in range(2) for k in range(nk)]
            for k, o in order:
                if chunks is not None and o == 0:
                    pe.wait_ge(x_split, chunks + k + 1)
                m = mm3(ps[:, 2 * (g % 3) + o, 0:T], hi(k, o), lo(k, o), xh(k), xl(k),
                        first and k == 0, last and k == nk - 1)
            m.then_inc(unit_used, 1)

        def pairs(w):
            v = w.rearrange("p (c a n) -> p c a n", c=8, a=2)
            return lambda k, o: v[:, k, o, :]

        X = (lambda k: x_hi[:, k], lambda k: x_lo[:, k])
        pe.wait_ge(x_ld, 5 * 16)
        pe.wait_ge(consts_made, 8)
        for c in range(DC):
            if c >= 2:
                pe.wait_ge(xpose_free, c - 1)
            for t0, n in TB:
                m = nc.tensor.transpose(ps[:, 6 + c % 2, t0:t0 + n], xtok[0:n, t0 // P, P * c:P * c + P], ident[0:n, 0:n])
            m.then_inc(xpose, 1)
        pe.wait_ge(tap_ld, 16)
        for c in range(DC):
            m = nc.tensor.transpose(ps[:, 0, TAPS * c:TAPS * c + TAPS], tap_rows[:, P * c:P * c + P], ident[0:TAPS, 0:TAPS])
        m.then_inc(taps_turned, 1)
        pe.wait_ge(hist_ld, 32)
        hb = 4 * HIST
        for c in range(DC):
            pe.wait_ge(xpose_free, DC + c - 1)
            for b in range(2):
                m = nc.tensor.transpose(ps[:, 6 + c % 2, hb * b:hb * b + hb], hist[0:hb, b, P * c:P * c + P], ident[0:hb, 0:hb])
            m.then_inc(xpose, 1)
        pe.wait_ge(xpose_free, 2 * DC)
        pe.wait_ge(taps_ready, 1)
        def taps(m):
            pe.wait_ge(group_free, m + 1)
            if m >= 2:
                pe.wait_ge(ln_in, m - 1)
            for t in range(PE_TAPS):
                q = PE_TAPS * m + t
                pe.wait_ge(diag_ready, q + 1)
                d = diag[:, q % DIAGS]
                nc.tensor.matmul(ps[:, 6 + m % 2, 0:T_P], d, u_p[:, m, t:t + T_P], start=t == 0, stop=t == PE_TAPS - 1,
                                 skip_group_check=True)
                last = nc.tensor.matmul(ps[:, 6 + m % 2, T_P:T].rearrange("p (s t) -> p s t", s=DEC_B), d, u_s[:, m, :, t:t + DEC_T],
                                        start=False, stop=t == PE_TAPS - 1, skip_group_check=True)
                last.then_inc(diag_used, 1)

        for m_ in range(8):
            linear(U_CIN + m_, G_CIN + m_, 8, pairs, *X)
            if m_ >= 1:
                taps(m_ - 1)
        taps(7)
        pe.wait_ge(group_free, 8)
        pe.wait_ge(ln_in, DC + 1)
        for c in range(DC):
            cs = slice(P * (c % 4), P * (c % 4) + P)
            nc.tensor.transpose(ps[0:HIST, 4 + c // 4, cs], u_p[:, c, T_P:T_P + HIST], ident[:])
            m = nc.tensor.transpose(ps[0:T_S, c // 4, cs], u_new[:, c], ident[:])
        m.then_inc(edge_ready, 1)

        def stats(n, chunks, bank, src, signal):
            for c in range(chunks):
                m = nc.tensor.matmul(ps[:, bank, 0:T], ones[:], src(c), start=c == 0, stop=c == chunks - 1)
            if signal is not None:
                m.then_inc(signal, 1)

        def mean_terms(c0, n_chunks, signal=False):
            for c in range(c0, c0 + n_chunks):
                m = nc.tensor.matmul(ps[:, 6, 0:T], ones[:], work[:, c], start=c == 0, stop=c == DC - 1, skip_group_check=True)
            if signal:
                m.then_inc(ln_mean, 1)

        def spread(n):
            for c in range(DC):
                pe.wait_ge(ln_sq, DC * n + c + 1)
                m = nc.tensor.matmul(ps[:, 7, 0:T], ones[:], sq[:, c], start=c == 0, stop=c == DC - 1, skip_group_check=True)
            m.then_inc(ln_var, 1)

        def product_and_norm(n, g0, product):
            for i in range(4):
                product(i)
                if i >= 1:
                    pe.wait_ge(group_free, g0 + i)
                    mean_terms(2 * i - 2, 2)
            pe.wait_ge(group_free, g0 + 4)
            mean_terms(DC - 2, 2, signal=True)
            spread(n)

        mean_terms(0, DC, signal=True)
        spread(0)
        pe.wait_ge(edge_copied, 1)

        def blocks(w):
            v = w.rearrange("p (c a n) -> p c a n", c=8, a=2)
            return lambda k, o: v[:, k, o, :]

        product_and_norm(1, G_COUT, lambda i: linear(U_COUT + i, G_COUT + i, 8, blocks, *X, chunks=0 if i == 0 else None))
        with pe.Fori(0, 3) as it:
            for r in range(6):
                linear(U_GU + r, G_GU + r, 8, pairs, *X, it=it, chunks=DC if r == 0 else None)
        for j in range(18, FC):
            linear(U_GU + j, G_GU + j, 8, pairs, *X)
        pe.wait_ge(h_split, FC)

        def down(i):
            for k, (k0, nk) in enumerate(DOWN_KC):
                linear(U_DOWN + 3 * i + k, G_DOWN + i, nk, blocks, lambda q: h_hi[:, k0 + q], lambda q: h_lo[:, k0 + q],
                       first=k == 0, last=k == 2)

        product_and_norm(2, G_DOWN, down)
        for i in range(4):
            linear(U_MIN + i, G_MIN + i, 8, blocks, *X, chunks=2 * DC if i == 0 else None)
        pe.wait_ge(mla_act, 1)
        stats(0, 4, 6, lambda c: sq[:, c], None)
        stats(0, RC, 7, lambda c: sq[:, 4 + c], mla_pe)
        pe.wait_ge(wuk_ld, 16)
        for j in range(HEADS // 2):
            for c in range(RC):
                a = 256 * (j % 2) + P * c
                m = nc.tensor.transpose(ps[:, WUK_BANKS[j // 2], a:a + P], wuk[:, c, P * j:P * j + P], ident[:])
        m.then_inc(mla_pe, 1)

        def kv_rows():
            pe.wait_ge(mla_act, 3)
            for b, (t0, n) in enumerate(TB):
                for c in range(RC):
                    o = 256 * b + P * c
                    nc.tensor.transpose(ps[0:n, 6 + o // 512, o % 512:o % 512 + P], ckvT[:, c, t0:t0 + n], ident[:])
                m = nc.tensor.transpose(ps[0:n, 7, 256 + 32 * b:288 + 32 * b], krT[0:ROPE, t0:t0 + n], ident[0:ROPE, 0:ROPE])
            m.then_inc(mla_pe, 1)

        pe.wait_ge(mla_act, 2)
        pe.wait_ge(group_free, G_MIN + 4)
        for i in range(4):
            u = U_UQ + i
            pe.wait_ge(lo_done, u + 1)
            if i == 1:
                kv_rows()
                pe.wait_ge(kvN_copied, 1)
            if i >= 2:
                pe.wait_ge(uq_free, i - 1)
            for k in range(4):
                if i == 0:
                    pe.wait_ge(cq_lo_done, k + 1)
                for o in range(4):
                    cs = slice(512 * k + P * o, 512 * k + P * o + P)
                    m = mm3(ps[:, 4 * (i % 2) + o, 0:T], w_hi[:, u % SPLIT, cs], w_lo[:, u % SPLIT, cs],
                            cq_hi[:, k], cq_lo[:, k], k == 0, k == 3)
            m.then_inc(unit_used, 1)
        pe.wait_ge(uq_free, 4)

        def qlat(h):
            r0 = NOPE * (h % 2)
            if h >= 1:
                pe.wait_ge(p_qc, h)
            for c in range(RC):
                m = nc.tensor.matmul(ps[:, c, 0:T], wukT[r0:r0 + NOPE, h // 2, P * c:P * c + P], qnT[r0:r0 + NOPE, h // 2],
                                     start=True, stop=True)
            m.then_inc(p_ql, 1)

        def scores(h):
            pe.wait_ge(p_qc, h + 1)
            if h >= 2:
                pe.wait_ge(p_sm, h - 1)
            bank, r0 = 2 + h % 2, 32 * (h % 4)
            for q0, n, c0 in ((0, P, 0), (P, 2 * P, P)):
                for c in range(RC):
                    nc.tensor.matmul(ps[:, bank, c0:c0 + n], ql[:, h % 2, c, q0:q0 + P], ckvT[:, c, 0:n], start=c == 0,
                                     stop=False, skip_group_check=True)
                m = nc.tensor.matmul(ps[:, bank, c0:c0 + n], qrT[r0:r0 + 32, h // 4, q0:q0 + P], krT[r0:r0 + 32, 0:n],
                                     start=False, stop=True, skip_group_check=True)
            m.then_inc(p_sc, 1)

        def turn(i, widths):
            pe.wait_ge(p_nm, i + 1)
            if i >= 1:
                pe.wait_ge(p_pt, i)
            for b, n in enumerate(widths):
                m = nc.tensor.transpose(ps[0:n, 5, P * b:P * b + P], sc[:, i % 2, P * b:P * b + n], ident[:])
            m.then_inc(p_tr, 1)

        def pv(i, parts, n_out):
            pe.wait_ge(p_pt, i + 1)
            if i >= 1:
                pe.wait_ge(p_ot, min(i, HEADS))
            if i > HEADS:
                pe.wait_ge(p_vc, i)
            for c in range(RC):
                for o0, terms in parts:
                    for t, (kb, nk, s0) in enumerate(terms):
                        m = nc.tensor.matmul(ps[:, 6, n_out * c + o0:n_out * c + o0 + P], ckvN[0:nk, kb, P * c:P * c + P],
                                             pT[0:nk, i % 2, s0:s0 + P], start=t == 0, stop=t == len(terms) - 1,
                                             skip_group_check=True)
            m.then_inc(p_pv, 1)

        def values(h):
            pe.wait_ge(p_ot, h + 1)
            if h == 0:
                pe.wait_ge(att_w, 16)
            if h >= 1:
                pe.wait_ge(p_vc, h)
            r0 = VH * (h % 2)
            for c in range(RC):
                m = nc.tensor.matmul(ps[r0:r0 + VH, 7, 0:2 * P], wuv[:, c, VH * h:VH * h + VH], oT[:, h % 2, c], start=c == 0, stop=c == RC - 1)
            m.then_inc(p_v, 1)

        PARTS = [(0, [(0, P, 0)]), (P, [(0, P, P), (1, P, 2 * P)])]
        qlat(0)
        for h in range(HEADS + 3):
            if h < HEADS:
                scores(h)
            if h + 1 < HEADS:
                qlat(h + 1)
            if 1 <= h < HEADS + 1:
                turn(h - 1, (P, P, P))
            if 2 <= h < HEADS + 2:
                pv(h - 2, PARTS, 2 * P)
            if h >= 3:
                values(h - 3)
        for i in range(2):
            n = HEADS + i
            pe.wait_ge(p_sm, n - 1)
            bank = 2 + n % 2
            pe.wait_ge(tail_ready, i + 1)
            for c in range(RC):
                nc.tensor.matmul(ps[:, bank, 0:T_P], tailq[i][:, c], ckvT[:, c, 0:T_P], start=c == 0, stop=False)
            nc.tensor.matmul(ps[:, bank, 0:T_P], tailq[i][0:32, RC], krT[0:32, 0:T_P], start=False, stop=True).then_inc(p_sc, 1)
            turn(n, (P, P, QT))
            pv(n, [(0, [(0, P, 0), (1, P, P), (2, QT, 2 * P)])], P)
        pe.wait_ge(p_vc, HEADS + 2)

        def turn_keys(s, half, b, g):
            if not isinstance(s, int) or s * 4 + g >= 1:
                pe.wait_ge(s_kt, s * 4 + g)
            pe.wait_ge(kv_ready[b][g], half * (16 * 4) + 16 * 4)
            for p in range(4):
                for c in range(RC):
                    nc.tensor.transpose(ps[:, p // 2, 256 * (p % 2) + P * c:256 * (p % 2) + P * c + P],
                                        kvn[b][:, 4 * g + p, P * c:P * c + P], ident[:])
            if g == 0:
                pe.wait_ge(s_q, s + 1)
            if not isinstance(s, int) or s * 4 + g >= 1:
                pe.wait_ge(s_kn, s * 4 + g)
            if g == 0:
                new_scores(b)
            pe.wait_ge(kr_ready[b][g], half * (16 * 4) + 16 * 4)
            nc.tensor.transpose(ps[:, 2, 0:P], krn[b][:, 4 * g:4 * g + 4].rearrange("p a r -> p (a r)"), ident[:]
                                ).then_inc(s_t, 1)

        def new_scores(b):
            out = ps[0:DEC_T, 2, 384:384 + NQ]
            for c in range(RC):
                nc.tensor.matmul(out, kn[b][:, c], qs[b][:, c], start=c == 0, stop=False, skip_group_check=True)
            nc.tensor.matmul(out, kn[b][:, RC], qsr[b][:, 0], start=False, stop=True, skip_group_check=True)
            for c in range(RC):
                nc.tensor.transpose(ps[0:DEC_T, 2, P + P * c:2 * P + P * c], kn[b][:, c], ident[:])

        def page_scores(s, b, g):
            pe.wait_ge(s_kt, s * 4 + (g + 1))
            pe.wait_ge(s_kn, s * 4 + (g + 1))
            bank = (3, 6)[b] + g // 2
            for p in range(4):
                q0 = NQ * (4 * (g % 2) + p)
                out = ps[:, bank, q0:q0 + NQ]
                for c in range(RC):
                    nc.tensor.matmul(out, kt[:, g % 2, p, P * c:P * c + P], qs[b][:, c], start=c == 0, stop=False, skip_group_check=True)
                m = nc.tensor.matmul(out, kr4[:, g % 2], qsr[b][:, p], start=False, stop=True, skip_group_check=True)
            m.then_inc(s_sc, 1)

        def latent_out(s, b, c):
            for p in range(PAGES):
                nc.tensor.matmul(ps[:, 5, NQ * c:NQ * c + NQ], kvn[b][:, p, P * c:P * c + P], ss[b][:, p], start=p == 0, stop=False,
                                 skip_group_check=True)
            nc.tensor.matmul(ps[:, 5, NQ * c:NQ * c + NQ], knN[b][0:DEC_T, P * c:P * c + P], sn[b][0:DEC_T], start=False, stop=True,
                             skip_group_check=True)

        def turn_maxima(s, b):
            if not isinstance(s, int) or s >= 1:
                pe.wait_ge(s_free, s)
            pe.wait_ge(s_mt, s + 1)
            nc.tensor.transpose(ps[:, 5, P:2 * P], mx[b][:], ident[:]).then_inc(s_dg, 1)

        def spread_maxima(s, b):
            pe.wait_ge(s_mb, s + 1)
            nc.tensor.matmul(ps[:, 5, 256:256 + NQ], ones[0:NQ], dg[b][0:NQ], start=True, stop=True, skip_group_check=True).then_inc(s_dg, 1)

        def spread_sums(s, b):
            pe.wait_ge(s_sum, s + 1)
            nc.tensor.matmul(ps[:, 5, 320:320 + NQ], ones[:], mx[b][:, 0:NQ], start=True, stop=True, skip_group_check=True).then_inc(s_pv, 1)

        def outputs(s, b):
            pe.wait_ge(s_ex, s + 1)
            for c in range(RC):
                latent_out(s, b, c)
            spread_sums(s, b)

        def sample(s, half, b):
            turn_keys(s, half, b, 0)
            turn_maxima(s - 1, 1 - b)
            turn_keys(s, half, b, 1)
            spread_maxima(s - 1, 1 - b)
            page_scores(s, b, 0)
            turn_keys(s, half, b, 2)
            page_scores(s, b, 1)
            outputs(s - 1, 1 - b)
            turn_keys(s, half, b, 3)
            page_scores(s, b, 2)
            page_scores(s, b, 3)

        turn_keys(0, 0, 0, 0)
        for g in range(4):
            if g < 3:
                turn_keys(0, 0, 0, g + 1)
            page_scores(0, 0, g)
        sample(1, 0, 1)
        sample(2, 1, 0)
        with pe.Fori(1, (DEC_B - 2) // 2) as it:
            sample(it * 2 + 1, it, 1)
            sample(it * 2 + 2, it + 1, 0)
        sample(DEC_B - 1, (DEC_B - 1) // 2, 1)
        turn_maxima(DEC_B - 1, 1)
        spread_maxima(DEC_B - 1, 1)
        outputs(DEC_B - 1, 1)
        pe.wait_ge(s_free, DEC_B)
        for h in range(HEADS):
            r0 = VH * (h % 2)
            bank, c0 = (h % 4) // 2 + 4 * (h % 2), TAIL * (h // 4)
            for c in range(RC):
                m = nc.tensor.matmul(ps[r0:r0 + VH, bank, c0:c0 + TAIL], wuv[:, c, VH * h:VH * h + VH], qlt[:, c, h],
                                     start=c == 0, stop=c == RC - 1, skip_group_check=True)
        m.then_inc(p_v, 1)
        product_and_norm(3, G_MOUT, lambda i: linear(U_MOUT + i, G_MOUT + i, 8, blocks, *X, chunks=3 * DC if i == 0 else None))
        pe.wait_ge(rt_w, 16)
        pe.wait_ge(group_free, G_MOUT + 4)
        for c in range(DC):
            pe.wait_ge(ln_hi, DC * 4 + c + 1)
            for b, (t0, n) in enumerate(TB):
                m = nc.tensor.matmul(ps[0:n, LOGIT_BANKS[b], 0:NEXP], xres[:, c, t0:t0 + n], w_rt[:, c],
                                     start=c == 0, stop=c == DC - 1, skip_group_check=True)
        m.then_inc(rt_pe, 1)
        for i in range(6):
            b, hf = divmod(i, 2)
            t0, n = TB[b]
            if ROW_BANKS[i] in LOGIT_BANKS:
                pe.wait_ge(rt_logits, 1)
            for c in range(4):
                m = nc.tensor.transpose(ps[0:n, ROW_BANKS[i], P * c:P * c + P], xres[:, 4 * hf + c, t0:t0 + n], ident[:])
            m.then_inc(rt_pe, 1)
        pe.wait_ge(rt_dve, 1)
        for b in range(4):
            o = ps[:, 4, NEXP * b:NEXP * b + NEXP] if b < 3 else ps[:, 4, 32:32 + NEXP]
            for a in range(min(b, 2) + 1 if b < 3 else 3):
                m = nc.tensor.matmul(o, before[:] if a == b else ones[:], selt[:, a], start=a == 0,
                                     stop=a == (b if b < 3 else 2), skip_group_check=True)
        m.then_inc(rt_pe, 1)

        pe.wait_ge(table_ready, 1)
        pe.wait_ge(xpose_free, 2 * DC + 1)
        pe.wait_ge(rt_act, 6)
        n_jobs = pe.value_load(jobi[0:1, MAX_JOBS:MAX_JOBS + 1], min_val=NEXP, max_val=MAX_JOBS)

        def gather(part, job):
            if part == 0:
                pe.wait_ge(m_pick, job + 1)
            for c in range(4 * part, 4 * part + 4):
                for b, (t0, n) in enumerate(TB):
                    m = nc.tensor.matmul(ps[:, 7, P * (c % 4):P * (c % 4) + SLOTS], xt[0:n, b, P * c:P * c + P],
                                         pick[0:n, b], start=b == 0, stop=b == 2, skip_group_check=True)
            m.then_inc(m_g, 1)

        def scatter(i, j):
            b, q = divmod(i, 2)
            n = TB[b][1]
            if i >= 2:
                pe.wait_ge(m_acc, j * 6 + (i - 1))
            nc.tensor.matmul(ps[0:n, 6 + i % 2, :], pickT[:, b, 0:n], y_hi[:, 512 * q:512 * q + 512], start=True, stop=False)
            nc.tensor.matmul(ps[0:n, 6 + i % 2, :], pickT[:, b, 0:n], y_lo[:, 512 * q:512 * q + 512], start=False, stop=True
                             ).then_inc(m_sct, 1)

        gather(0, 0)
        pe.wait_ge(m_gc, 1)
        gather(1, 0)
        pe.wait_ge(m_gc, 2)
        pe.wait_ge(m_zero, 1)
        with pe.Fori(0, n_jobs) as j:
            pe.wait_ge(m_gl, j + 1)
            k = 0

            def unit(tok_hi, tok_lo, outs, first, last):
                nonlocal k
                u = U_MOE + k
                pe.wait_ge(lo_done, j * JOB_UNITS + (u + 1))
                for i in range(4):
                    bank, c = outs(i)
                    wh, wl = w_hi[:, u % SPLIT, 512 * i:512 * i + 512], w_lo[:, u % SPLIT, 512 * i:512 * i + 512]
                    nc.tensor.matmul(ps[:, bank, :], tok_hi[:, c], wh, start=first(i), stop=False, skip_group_check=True)
                    nc.tensor.matmul(ps[:, bank, :], tok_hi[:, c], wl, start=False, stop=False, skip_group_check=True)
                    m = nc.tensor.matmul(ps[:, bank, :], tok_lo[:, c], wh, start=False, stop=last(i), skip_group_check=True)
                m.then_inc(unit_used, 1)
                k += 1

            for s in range(STEPS + 1):
                if s < STEPS:
                    if s >= 2:
                        pe.wait_ge(m_h, j * STEPS + (s - 1))
                    for part in range(2):
                        unit(g_hi, g_lo, lambda i: (2 * (s % 2), 4 * part + i), lambda i: part == 0 and i == 0,
                             lambda i: part == 1 and i == 3)
                if s == 0:
                    pe.wait_ge(m_ylo, j + 1)
                    scatter(0, j)
                    scatter(1, j)
                if s >= 1:
                    pe.wait_ge(m_acc, j * 6 + (4 if s == 1 else 6))
                    pe.wait_ge(m_h, j * STEPS + s)
                    for c in range(4):
                        m = nc.tensor.transpose(ps[:, 6, P * c:P * c + P], hh[:, (s - 1) % 2, P * c:P * c + P], ident[:])
                    m.then_inc(m_hT, 1)
                if s < STEPS:
                    for part in range(2):
                        unit(g_hi, g_lo, lambda i: (2 * (s % 2) + 1, 4 * part + i), lambda i: part == 0 and i == 0,
                             lambda i: part == 1 and i == 3)
                if s == 0:
                    scatter(2, j)
                    scatter(3, j)
                if s == TURN_STEP:
                    for b in range(3):
                        m = nc.tensor.transpose(ps[:, 7, P * b:P * b + P], pick[:, b], ident[:])
                    m.then_inc(m_pickT, 1)
                if s == GATHER_STEPS[0]:
                    pe.wait_ge(m_pickTc, j + 1)
                    gather(0, j + 1)
                if s == GATHER_STEPS[1]:
                    pe.wait_ge(m_gc, j * 2 + 3)
                    gather(1, j + 1)
                if s >= 1:
                    pe.wait_ge(m_hTl, j * STEPS + s)
                if s == 1:
                    scatter(4, j)
                    scatter(5, j)
                if s >= 1:
                    for part in range(2):
                        unit(hT_hi, hT_lo, lambda i: (4 + i % 2, 2 * part + i // 2), lambda i: s == 1 and part == 0 and i < 2,
                             lambda i: s == STEPS and part == 1 and i >= 2)
        pe.wait_ge(m_ylo, n_jobs + 1)
        pe.wait_ge(m_pickTc, n_jobs)
        for i in range(6):
            scatter(i, n_jobs)

    ctx.close()


CONST_LOADS = 9
STORES = 1 + 8 + 4
_INS = ['x_prompt', 'x_sample', 'state_conv', 'cache_ckv', 'cache_krope', 'page_table', 'meta_tokens',
        'conv_w_in', 'conv_b_in', 'conv_w_dw', 'conv_b_dw', 'conv_ln_g', 'conv_ln_b', 'conv_w_out',
        'mla_w_in', 'mla_g_q', 'mla_g_kv', 'mla_w_uq', 'mla_w_uk', 'mla_w_uv', 'mla_w_out',
        'ffn_w_gu', 'ffn_w_down', 'moe_w_router', 'moe_w_gu', 'moe_w_down', 'ln_g', 'ln_b']
_OUTS = [(1, SEQ, D), (DEC_B, DEC_T, D), (1, 1, HIST, D), (1, DEC_B, HIST, D), (1, 1, T_P, LORA), (1, 1, T_P, ROPE),
         (1, DEC_B, DEC_T, LORA), (1, DEC_B, DEC_T, ROPE)]


def kernel(**inputs):
    import concourse.bacc as bacc
    from concourse.bass_utils import run_bass_kernel_spmd

    nc = bacc.Bacc("TRN2", target_bir_lowering=False, num_devices=1)
    arrays, args = {}, []
    cos_t, sin_t = rope_tables()
    for name, a in [(n, np.ascontiguousarray(inputs[n])) for n in _INS] + [("cos_t", cos_t), ("sin_t", sin_t)]:
        arrays["in_" + name] = a
        args.append(nc.dram_tensor("in_" + name, a.shape, mybir.dt.from_np(a.dtype), kind="ExternalInput").ap())
    for i, shape in enumerate(_OUTS):
        args.append(nc.dram_tensor(f"out_{i}", shape, F32, kind="ExternalOutput").ap())
    build(nc, *args)
    r = run_bass_kernel_spmd(nc, [arrays], core_ids=[0])
    return tuple(r.results[0][f"out_{i}"] for i in range(len(_OUTS)))
```
